# Optimizing a Trainium2 kernel written in Bass

```python
import jax, jax.numpy as jnp
from jax import lax
import numpy as np

D_MODEL = 1024
BATCH = 1
SEQ = 512
DEPTH = 1
DEC_BATCH = 8
DEC_SEQ = 8
PAST_LEN = 2048
PAGE_SIZE = 128

N_HEADS = 8
HEAD_DIM = 64
ATT_WIDTH = N_HEADS * HEAD_DIM
IDX_HEADS = 4
IDX_DIM = 64
TOP_K_MAX = 256
Q_BLOCK = 128
ROPE_THETA = 10000.0
POOL_WINDOWS = (2, 4, 8, 16)
POOL_GROUPS = 4
POOL_WIDTH = 512
POOL_GW = POOL_WIDTH // POOL_GROUPS
POOL_STATE = 15
N_EXPERTS = 64
TOP_K_EXPERTS = 8
N_GROUPS = 8
TOPK_GROUPS = 4
EXPERT_DIM = 256
SHARED_DIM = 256
ROUTED_SCALE = 2.5
PLE_DIM = 256
LN_EPS = 1e-5
DN_ALPHA = (2 * DEPTH) ** 0.25
DN_BETA = (8 * DEPTH) ** -0.25
IN_SIZES = (ATT_WIDTH, HEAD_DIM, HEAD_DIM, IDX_HEADS * IDX_DIM, IDX_DIM, IDX_HEADS, POOL_WIDTH, D_MODEL, D_MODEL)
IN_WIDTH = sum(IN_SIZES)

kernel_name = 'dsa_pool_hybrid_moe_step'

def layer_norm(x, g, b):
    xf = x.astype(jnp.float32)
    mu = jnp.mean(xf, axis=-1, keepdims=True)
    var = jnp.mean(jnp.square(xf - mu), axis=-1, keepdims=True)
    return ((xf - mu) * lax.rsqrt(var + LN_EPS) * g + b).astype(x.dtype)

def rope(x, pos):
    d = x.shape[-1]
    inv = ROPE_THETA ** (-jnp.arange(0, d, 2, dtype=jnp.float32) / d)
    ang = pos.astype(jnp.float32)[:, None] * inv[None, :]
    cos = jnp.cos(ang)[:, None, :]
    sin = jnp.sin(ang)[:, None, :]
    xf = x.astype(jnp.float32)
    x1, x2 = xf[..., : d // 2], xf[..., d // 2:]
    return jnp.concatenate([x1 * cos - x2 * sin, x2 * cos + x1 * sin], axis=-1).astype(x.dtype)

def project_in(x, pos, w_in):
    B, T, _ = x.shape
    offs = np.cumsum(IN_SIZES)[:-1].tolist()
    q, k, v, qi, ki, wi, u, ga, gb = jnp.split(x @ w_in, offs, axis=-1)
    q = rope(q.reshape(B, T, N_HEADS, HEAD_DIM), pos)
    k = rope(k[:, :, None, :], pos)[:, :, 0]
    qi = rope(qi.reshape(B, T, IDX_HEADS, IDX_DIM), pos)
    ki = rope(ki[:, :, None, :], pos)[:, :, 0]
    wi = wi * IDX_HEADS ** -0.5
    return q, k, v, qi, ki, wi, u, ga, gb

def sparse_attention(q, qi, wi, q_pos, k, v, ki, top_k):
    B, T = q.shape[:2]
    L = k.shape[1]
    k_pos = jnp.arange(L, dtype=jnp.int32)
    dots = jnp.einsum('bthd,bsd->bths', qi.astype(jnp.float32), ki.astype(jnp.float32)) * IDX_DIM ** -0.5
    score = jnp.einsum('bth,bths->bts', wi.astype(jnp.float32), jax.nn.relu(dots))
    admissible = k_pos[None, :] <= q_pos[:, None]
    score = jnp.where(admissible[None], score, -jnp.inf)
    _, idx = lax.top_k(score, top_k)
    valid = idx <= q_pos[None, :, None]
    gather = jax.vmap(lambda rows, ids: rows[ids])
    k_sel = gather(k, idx).astype(jnp.float32)
    v_sel = gather(v, idx).astype(jnp.float32)
    logits = jnp.einsum('bthd,btkd->bthk', q.astype(jnp.float32), k_sel) * HEAD_DIM ** -0.5
    logits = jnp.where(valid[:, :, None, :], logits, -jnp.inf)
    p = jax.nn.softmax(logits, axis=-1)
    o = jnp.einsum('bthk,btkd->bthd', p, v_sel)
    return o.reshape(B, T, ATT_WIDTH).astype(q.dtype)

def prompt_attention(q, qi, wi, k, v, ki):
    B, T = q.shape[:2]
    nb = T // Q_BLOCK
    top_k = min(TOP_K_MAX, T // 4)

    def to_blocks(a):
        return jnp.moveaxis(a.reshape((B, nb, Q_BLOCK) + a.shape[2:]), 1, 0)

    def block(args):
        qb, qib, wib, pb = args
        return sparse_attention(qb, qib, wib, pb, k, v, ki, top_k)

    pos = jnp.arange(T, dtype=jnp.int32).reshape(nb, Q_BLOCK)
    out = lax.map(block, (to_blocks(q), to_blocks(qi), to_blocks(wi), pos))
    return jnp.moveaxis(out, 0, 1).reshape(B, T, ATT_WIDTH)

def pool_mix(u_ext, pos, w_grp, scale):
    B = u_ext.shape[0]
    P = POOL_STATE
    T = u_ext.shape[1] - P
    cs = jnp.cumsum(u_ext.astype(jnp.float32), axis=1)
    cs = jnp.concatenate([jnp.zeros_like(cs[:, :1]), cs], axis=1)
    u_new = u_ext[:, P:].astype(jnp.float32)
    outs = []
    for g, w in enumerate(POOL_WINDOWS):
        sl = slice(g * POOL_GW, (g + 1) * POOL_GW)
        win_sum = cs[:, P + 1:P + T + 1, sl] - cs[:, P + 1 - w:P + T + 1 - w, sl]
        count = jnp.minimum(pos + 1, w).astype(jnp.float32)[None, :, None]
        outs.append(win_sum / count - u_new[:, :, sl])
    r = jnp.stack(outs, axis=2)
    r = jnp.einsum('btgc,gcd->btgd', r, w_grp.astype(jnp.float32)).reshape(B, T, POOL_WIDTH)
    return (r * scale).astype(u_ext.dtype)

def merge_out(attn, pool, ga, gb, w_att_out, w_pool_out, w_out):
    return (jax.nn.sigmoid(ga) * (attn @ w_att_out) + jax.nn.sigmoid(gb) * (pool @ w_pool_out)) @ w_out

def swiglu(x, w13, w2):
    a, b = jnp.split(x @ w13, 2, axis=-1)
    return (jax.nn.silu(a) * b) @ w2

def moe(h, w_router, router_bias, w_exp13, w_exp2, w_sh13, w_sh2):
    N = h.shape[0]
    s = jax.nn.sigmoid((h @ w_router).astype(jnp.float32))
    sb = s + router_bias.astype(jnp.float32)
    grp = sb.reshape(N, N_GROUPS, N_EXPERTS // N_GROUPS)
    grp_score = jnp.sum(lax.top_k(grp, 2)[0], axis=-1)
    _, gidx = lax.top_k(grp_score, TOPK_GROUPS)
    gmask = jnp.sum(jax.nn.one_hot(gidx, N_GROUPS, dtype=jnp.float32), axis=1) > 0
    emask = jnp.repeat(gmask, N_EXPERTS // N_GROUPS, axis=1)
    _, eidx = lax.top_k(jnp.where(emask, sb, -jnp.inf), TOP_K_EXPERTS)
    gate = jnp.take_along_axis(s, eidx, axis=1)
    gate = gate / jnp.sum(gate, axis=-1, keepdims=True) * ROUTED_SCALE
    combine = jnp.einsum('nk,nke->ne', gate, jax.nn.one_hot(eidx, N_EXPERTS, dtype=jnp.float32)).astype(h.dtype)
    y = swiglu(h, w_sh13, w_sh2)
    for e in range(N_EXPERTS):
        y = y + combine[:, e:e + 1] * swiglu(h, w_exp13[e], w_exp2[e])
    return y

def setup_inputs(seed: int = 0) -> dict:
    key = jax.random.key(seed)
    keys = jax.random.split(key, 32)

    def nrm(i, shape, scale=1.0):
        return jax.random.normal(keys[i], shape, jnp.float32) * scale

    n_pages = PAST_LEN // PAGE_SIZE
    n_used = DEC_BATCH * n_pages
    n_phys = n_used + max(1, n_used // 4)
    page_table = jax.random.permutation(keys[0], n_phys)[:n_used].reshape(DEC_BATCH, n_pages).astype(jnp.int32)
    return {
        'x_prompt': nrm(1, (BATCH, SEQ, D_MODEL)),
        'x_sample': nrm(2, (DEC_BATCH, DEC_SEQ, D_MODEL)),
        'cache_k': nrm(3, (DEPTH, n_phys, PAGE_SIZE, HEAD_DIM)),
        'cache_v': nrm(4, (DEPTH, n_phys, PAGE_SIZE, HEAD_DIM)),
        'cache_kidx': nrm(5, (DEPTH, n_phys, PAGE_SIZE, IDX_DIM)),
        'state_pool': nrm(6, (DEPTH, DEC_BATCH, POOL_STATE, POOL_WIDTH)),
        'page_table': page_table,
        'p_prompt': nrm(7, (DEPTH, BATCH, SEQ, PLE_DIM)),
        'p_sample': nrm(8, (DEPTH, DEC_BATCH, DEC_SEQ, PLE_DIM)),
        'w_in': nrm(9, (DEPTH, D_MODEL, IN_WIDTH), D_MODEL ** -0.5),
        'w_att_out': nrm(10, (DEPTH, ATT_WIDTH, D_MODEL), ATT_WIDTH ** -0.5),
        'w_pool_grp': nrm(11, (DEPTH, POOL_GROUPS, POOL_GW, POOL_GW), POOL_GW ** -0.5),
        'pool_scale': 1.0 + nrm(12, (DEPTH, POOL_WIDTH), 0.05),
        'w_pool_out': nrm(13, (DEPTH, POOL_WIDTH, D_MODEL), POOL_WIDTH ** -0.5),
        'w_out': nrm(14, (DEPTH, D_MODEL, D_MODEL), D_MODEL ** -0.5 * DN_BETA),
        'ln1_g': 1.0 + nrm(15, (DEPTH, D_MODEL), 0.05),
        'ln1_b': nrm(16, (DEPTH, D_MODEL), 0.02),
        'w_router': nrm(17, (DEPTH, D_MODEL, N_EXPERTS), D_MODEL ** -0.5),
        'router_bias': nrm(18, (DEPTH, N_EXPERTS), 0.01),
        'w_exp13': nrm(19, (DEPTH, N_EXPERTS, D_MODEL, 2 * EXPERT_DIM), D_MODEL ** -0.5),
        'w_exp2': nrm(20, (DEPTH, N_EXPERTS, EXPERT_DIM, D_MODEL), EXPERT_DIM ** -0.5 * DN_BETA),
        'w_sh13': nrm(21, (DEPTH, D_MODEL, 2 * SHARED_DIM), D_MODEL ** -0.5),
        'w_sh2': nrm(22, (DEPTH, SHARED_DIM, D_MODEL), SHARED_DIM ** -0.5 * DN_BETA),
        'ln2_g': 1.0 + nrm(23, (DEPTH, D_MODEL), 0.05),
        'ln2_b': nrm(24, (DEPTH, D_MODEL), 0.02),
        'w_ple_in': nrm(25, (DEPTH, PLE_DIM, D_MODEL), PLE_DIM ** -0.5),
        'w_ple_gate': nrm(26, (DEPTH, D_MODEL, D_MODEL), D_MODEL ** -0.5),
    }

def reference(x_prompt, x_sample, cache_k, cache_v, cache_kidx, state_pool, page_table, p_prompt, p_sample,
              w_in, w_att_out, w_pool_grp, pool_scale, w_pool_out, w_out, ln1_g, ln1_b,
              w_router, router_bias, w_exp13, w_exp2, w_sh13, w_sh2, ln2_g, ln2_b, w_ple_in, w_ple_gate):
    B, S, D = x_prompt.shape
    DB, T, _ = x_sample.shape
    past = page_table.shape[1] * cache_k.shape[2]
    pos_p = jnp.arange(S, dtype=jnp.int32)
    pos_s = past + jnp.arange(T, dtype=jnp.int32)
    top_k_s = min(TOP_K_MAX, (past + T) // 4)
    xp, xs = x_prompt, x_sample
    kp_l, vp_l, kip_l, pp_l, ks_l, vs_l, kis_l, ps_l = [], [], [], [], [], [], [], []
    for i in range(DEPTH):
        q, k, v, qi, ki, wi, u, ga, gb = project_in(xp, pos_p, w_in[i])
        attn_p = prompt_attention(q, qi, wi, k, v, ki)
        u_ext = jnp.concatenate([jnp.zeros((B, POOL_STATE, POOL_WIDTH), u.dtype), u], axis=1)
        pool_p = pool_mix(u_ext, pos_p, w_pool_grp[i], pool_scale[i])
        mix_p = merge_out(attn_p, pool_p, ga, gb, w_att_out[i], w_pool_out[i], w_out[i])
        kp_l.append(k); vp_l.append(v); kip_l.append(ki); pp_l.append(u_ext[:, -POOL_STATE:])
        qs, ks, vs, qis, kis, wis, us, gas, gbs = project_in(xs, pos_s, w_in[i])
        k_all = jnp.concatenate([cache_k[i][page_table].reshape(DB, past, HEAD_DIM), ks], axis=1)
        v_all = jnp.concatenate([cache_v[i][page_table].reshape(DB, past, HEAD_DIM), vs], axis=1)
        ki_all = jnp.concatenate([cache_kidx[i][page_table].reshape(DB, past, IDX_DIM), kis], axis=1)
        attn_s = sparse_attention(qs, qis, wis, pos_s, k_all, v_all, ki_all, top_k_s)
        us_ext = jnp.concatenate([state_pool[i].astype(us.dtype), us], axis=1)
        pool_s = pool_mix(us_ext, pos_s, w_pool_grp[i], pool_scale[i])
        mix_s = merge_out(attn_s, pool_s, gas, gbs, w_att_out[i], w_pool_out[i], w_out[i])
        ks_l.append(ks); vs_l.append(vs); kis_l.append(kis); ps_l.append(us_ext[:, -POOL_STATE:])
        h = jnp.concatenate([(DN_ALPHA * xp + mix_p).reshape(B * S, D), (DN_ALPHA * xs + mix_s).reshape(DB * T, D)], axis=0)
        h = layer_norm(h, ln1_g[i], ln1_b[i])
        h = layer_norm(DN_ALPHA * h + moe(h, w_router[i], router_bias[i], w_exp13[i], w_exp2[i], w_sh13[i], w_sh2[i]), ln2_g[i], ln2_b[i])
        pe = jnp.concatenate([p_prompt[i].reshape(B * S, PLE_DIM), p_sample[i].reshape(DB * T, PLE_DIM)], axis=0).astype(h.dtype)
        h = h + jax.nn.sigmoid(h @ w_ple_gate[i]) * (pe @ w_ple_in[i])
        xp = h[:B * S].reshape(B, S, D)
        xs = h[B * S:].reshape(DB, T, D)
    return (xp, xs, jnp.stack(kp_l), jnp.stack(vp_l), jnp.stack(kip_l), jnp.stack(pp_l),
            jnp.stack(ks_l), jnp.stack(vs_l), jnp.stack(kis_l), jnp.stack(ps_l))


_drawn_inputs = setup_inputs


def setup_inputs(seed=0):
    import zlib

    import numpy as np

    out = dict(_drawn_inputs(seed))
    spreads = {}
    factors = {'ln2_b': 3.171}
    for name, (base, spread) in spreads.items():
        noise = np.random.default_rng([zlib.crc32(name.encode()), seed]).standard_normal(out[name].shape)
        drawn = base * np.exp(spread * noise) if base else spread * noise
        out[name] = __import__('jax').numpy.asarray(drawn.astype(out[name].dtype))
    for name, factor in factors.items():
        out[name] = (out[name] * factor).astype(out[name].dtype)
    return out
```

```python
from contextlib import ExitStack

import concourse.bass as bass
from concourse import mybir

P = 128
D = 1024
KT = D // P
SEQ = 512
DB = 8
DT = 8
NS = DB * DT
NTOK = SEQ + NS
PAST = 2048
PAGE = 128
NPG = PAST // PAGE
SK = PAST + DT
H = 8
HD = 64
IH = 4
IDX = 64
PW = 512
PG = 4
PST = 15
NE = 64
TOPE = 8
ED = 256
PLE = 256
TOP_P = 128
TOP_S = 256
ALPHA = 2 ** 0.25
EPS = 1e-5
SCALE_ROUTED = 2.5
CAP = 128
BIG = 8192.0
STRUCK = -3.4e38
BARRED = -3.0e38
STRUCK_TEST = -3.3e38
MASKED = -1e30

F32 = mybir.dt.float32
BF16 = mybir.dt.bfloat16
I32 = mybir.dt.int32
U32 = mybir.dt.uint32
ALU = mybir.AluOpType
ACT = mybir.ActivationFunctionType
AX = mybir.AxisListType.X

ROWS = [128, 128, 128, 128, 64]
NT = len(ROWS)
KEYS = [128 * (t + 1) for t in range(4)]
SP_OFF = [0, 128, 384, 768]

QC, KVC, UC, GAC, GBC = 0, 512, 964, 1476, 2500
KVW = UC - KVC

CONSTS = {}
_at = 0
for _name, _w in (("ident", 128), ("upper", 128), ("ones", 128), ("iota", 128), ("hmask", 4), ("selT", 32),
                  ("icount", 64), ("newmask", 8), ("tokid", 5), ("gid", 32), ("sel", 256), ("rep", 512), ("mhalf", 1), ("blocks", 4)):
    CONSTS[_name] = (_at, _w)
    _at += _w
NCONST = _at


def constants():
    import numpy as np
    c = np.zeros((P, NCONST), np.float32)

    def put(name, a):
        o, w = CONSTS[name]
        c[:a.shape[0], o:o + w] = a.reshape(a.shape[0], w)

    p = np.arange(P)
    put("ident", np.eye(P))
    put("upper", (p[:, None] < p[None, :]).astype(np.float32))
    put("ones", np.ones((P, P)))
    put("iota", np.tile(np.where(p < CAP, p, -5)[None, :], (P, 1)))
    h_of = (p // 8) % 4
    put("hmask", (h_of[:, None] == np.arange(4)[None, :]))
    bt = (p // 32) * 8 + p % 8
    put("selT", (bt[:, None] == np.arange(32)[None, :]))
    ic = np.stack([1.0 / np.minimum(np.arange(16) + 1, w) for w in (2, 4, 8, 16)]).astype(np.float32)
    put("icount", np.tile(ic.reshape(1, 64), (P, 1)))
    r = np.arange(64)
    put("newmask", (np.arange(8)[None, :] <= (r % 8)[:, None]))
    put("tokid", (np.arange(5)[None, :] * 128 + p[:, None]).astype(np.float32))
    put("gid", np.tile(np.repeat(np.arange(8), 4)[None, :], (P, 1)))
    sel = np.zeros((64, 2, 128))
    for g in range(2):
        for q in range(128):
            sel[(4 * g + q // 32) * 8 + q % 8, g, q] = 1
    put("sel", sel)
    rep = np.zeros((64, 4, 128))
    for k in range(4):
        for q in range(128):
            rep[(2 * k + q // 64) * 8 + q % 8, k, q] = 1
    put("rep", rep)
    put("blocks", np.tile(CAP * np.arange(1, 5)[None, :], (P, 1)))
    put("mhalf", np.full((P, 1), -0.5))
    pos = np.concatenate([np.arange(SEQ), np.tile(PAST + np.arange(DT), DB)]).astype(np.float32)
    inv = (10000.0 ** (-np.arange(0, HD, 2) / HD)).astype(np.float32)
    ang = (pos[:, None] * inv[None, :]).astype(np.float32)
    cs, sn = np.cos(ang.astype(np.float64)).astype(np.float32), np.sin(ang.astype(np.float64)).astype(np.float32)
    rot = np.zeros((NT * P, 2, HD), np.float32)
    rot[:NTOK, 0] = np.concatenate([cs, cs], 1)
    rot[:NTOK, 1] = np.concatenate([-sn, sn], 1)
    return c, rot


def plan_banks():
    jobs = []
    add = lambda key, who: jobs.append((key, who))
    for t in range(NT):
        add(("xT", t, 0), "act")
        add(("xT", t, 1), "dve")

    def qkv(t):
        add(("q", t), "dve")
        add(("kv", t), "dve")

    def rt(t):
        for i in range(3):
            add(("rt", t, i), "act")

    qkv(0)
    for t in range(1, NT):
        qkv(t)
        rt(t - 1)
    rt(NT - 1)
    add(("wsel",), "dve")
    for t in range(1, 4):
        for h in range(IH):
            add(("dot", t, h), "act")
    def kT(b):
        for i in range(4):
            add(("kT", b, i), "act" if i % 2 else "dve")
    kT(0)
    for b in range(DB):
        if b + 1 < DB:
            kT(b + 1)
        for c in range(5):
            add(("sd", b, c), "act")
            add(("sl", b, c), "dve")
        if b % 4 == 3:
            for c in range(5):
                add(("sc", b // 4, c), "dve")
    add(("st",), "act")
    for g in range(PG):
        add(("u", g, 0), "act")
        add(("u", g, 1), "act")
    add(("uo", 0), "act")
    add(("uo", 1), "act")
    for c in range(2):
        for t in range(NT):
            add(("gb", c, t), "act")
    for g in range(PG):
        add(("pp", g, 0), "act")
        add(("pp", g, 1), "act")
    for t in range(NT):
        for c in range(2):
            add(("pm", t, c), "act")
    for c in range(2):
        for t in range(NT):
            add(("ga", c, t), "act")
    heads = [(t, h) for t in range(4) for h in range(H)]
    add(("l",) + heads[0], "dve")
    add(("l",) + heads[1], "dve")
    for n, (t, h) in enumerate(heads):
        if n + 2 < len(heads):
            add(("l",) + heads[n + 2], "dve")
        add(("pt", t, h), "act" if h % 2 else "dve")
        if h == H - 1:
            add(("at", t), "act")
    for c in range(5):
        add(("bs", 0, c), "dve")
    for p in range(4):
        if p < 3:
            for c in range(5):
                add(("bs", p + 1, c), "dve")
        for i in range(5):
            add(("ps", p, i), "act" if i % 2 else "dve")
        add(("ost", p), "dve")
    for t in range(NT):
        for c in range(2):
            add(("m1", t, c), "dve")
    for t in range(NT):
        add(("mT", t, 0), "act")
        add(("mT", t, 1), "dve")
    for c in range(2):
        for t in range(NT):
            add(("wo", c, t), "dve")
    for t in range(NT):
        add(("hT", t, 0), "act")
        add(("hT", t, 1), "act")
    for t in range(NT):
        add(("r", t), "act")
    for t in range(NT):
        add(("rank", t), "dve")
    add(("count",), "dve")
    for t in range(NT):
        add(("s13", t), "dve")
    for t in range(NT):
        add(("s13T", t), "act")
    for t in range(NT):
        for c in range(2):
            add(("s2", t, c), "dve")
    return jobs


def build(nc, a, o):
    jobs = plan_banks()
    NB = 6
    number, bank_of, prev = {}, {}, {}
    count = {"act": 0, "dve": 0}
    last_in = [None] * NB
    for n, (key, who) in enumerate(jobs):
        count[who] += 1
        number[key] = (who, count[who])
        bank_of[key] = n % NB
        prev[key] = last_in[n % NB]
        last_in[n % NB] = key

    ctx = ExitStack()
    with ctx:
        def sem(name):
            return ctx.enter_context(nc.semaphore(name))

        KB = 1024
        ARENA = 212800
        arena = ctx.enter_context(nc.sbuf_tensor("arena", [P, ARENA // 4], F32))

        def at(byte, width, rows=P):
            assert byte % 4 == 0 and byte + 4 * width <= ARENA, (byte, width)
            return arena[0:rows, byte // 4:byte // 4 + width]

        C0, SMALL, RING, GATE = 0, 7 * KB, 14 * KB, 46 * KB
        assert NCONST * 4 <= SMALL
        LG = GATE + 40 * KB
        SS = LG + 4 * SK * 4
        REL = SS + SK * 4
        SPR = REL + SK * 4
        XT = SPR + sum(KEYS) * 4
        QT = XT + 18 * KB
        PV = QT + 18 * KB

        def const(name, rows=P):
            of, w = CONSTS[name]
            return at(C0 + 4 * of, w, rows)

        cst = at(C0, NCONST)
        ident = const("ident")
        small = [SMALL]

        def little(width, rows=P):
            v = at(small[0], width, rows)
            small[0] += 4 * width
            assert small[0] <= RING
            return v

        v_prompt = little(4 * HD).rearrange("p (t d) -> p t d", t=4)
        kk_prompt = little(SEQ)
        kk_new = little(NS)
        v_new = little(DB * HD, 8).rearrange("p (b d) -> p b d", b=DB)
        v_samp = little(HD, NS)
        wi = little(NT * IH).rearrange("p (t h) -> p t h", t=NT)
        wcol8 = little(8).rearrange("p (g h) -> p g h", g=2)
        wcol = little(2)
        w_comb = little(64).rearrange("p (g q) -> p g q", g=2)
        top8 = little(4 * 8).rearrange("p (t k) -> p t k", t=4)
        mx = little(5)
        nmax = little(16)
        esum = little(16)
        erec = little(16)
        pscale = little(PG)
        pages = little(P, 1).bitcast(I32)
        mask_new = little(4, NS).bitcast(BF16)

        ring = [at(RING + 16 * KB * s, 4096) for s in range(2)]
        xs = at(GATE, NT * D).rearrange("p (t n) -> p t n", t=NT)
        xT = at(XT, KT * NTOK).rearrange("p (k n) -> p k n", k=KT)
        qT = at(QT, H * SEQ).rearrange("p (h n) -> p h n", h=H)
        qTs = at(QT + 4 * H * SEQ, H * NS).rearrange("p (b h t) -> p b h t", b=DB, h=H)
        rowsR = at(PV, 2 * 9 * P).rearrange("p (s h d) -> p s h d", s=2, h=9)
        ropeA = at(PV + 10 * KB, 512)
        ropeB = at(PV + 12 * KB, 512)
        rotary = at(REL, NT * 2 * HD).rearrange("p (t c d) -> p t c d", t=NT, c=2)
        knat = [at(GATE + (20 + 8 * s) * KB, NPG * P).rearrange("p (g d) -> p g d", g=NPG) for s in range(2)]
        kkT = [at(GATE + 8 * KB * s, PAST) for s in range(2)]
        relP = [at(REL + 2 * KB * s, 512) for s in range(4)]
        relS = at(REL, SK)
        scoreS = at(SS, SK, NS)
        scoreP = [at(SPR + 4 * SP_OFF[t], KEYS[t]) for t in range(4)]
        logit = at(LG, 4 * SK).rearrange("p (c s) -> p c s", c=4)
        uext = at(PV, PG * 528).rearrange("p (g n) -> p g n", g=PG)
        uexs = at(PV + 8448, PG * DB * 23).rearrange("p (g b n) -> p g b n", g=PG, b=DB)
        win = [at(PV + 11392 + 2112 * s, 528) for s in range(2)]
        wins = [at(PV + 15616 + 736 * s, DB * 23).rearrange("p (b n) -> p b n", b=DB) for s in range(2)]
        wgrp = at(PV + 17152, PG * P).rearrange("p (g d) -> p g d", g=PG)
        poolT = at(PV + 19200, PG * NTOK).rearrange("p (g n) -> p g n", g=PG)
        pmt = [at(PV + 28416 + 2048 * s, 512) for s in range(2)]
        ust = at(REL, 1024).rearrange("p (s n) -> p s n", s=2)
        stnat = at(REL + 4096, 512, DB * PST)
        uflat = at(REL + 6144, PG * NS).rearrange("p (g n) -> p g n", g=PG)
        sga = at(GATE, NT * D).rearrange("p (t n) -> p t n", t=NT)
        m = at(GATE + 20 * KB, NT * D).rearrange("p (t n) -> p t n", t=NT)
        values = at(PV, DB * NPG * HD).rearrange("p (g d) -> p g d", d=HD)
        probs = [at(REL + 2 * KB * s, 512) for s in range(3)]
        attnT = at(XT, 4 * NTOK).rearrange("p (k n) -> p k n", k=4)
        att = at(XT + 9216, 512)
        probsT = [at(XT + 11264 + 2 * KB * s, 512) for s in range(2)]
        maskS = [at(REL + 6 * KB, 256, NS).bitcast(BF16), at(REL + 7 * KB, 256, NS).bitcast(BF16),
                 at(XT + 15360, 256, NS).bitcast(BF16), at(XT + 16384, 256, NS).bitcast(BF16),
                 mask_new]
        rep_b = at(XT + 17408, 256, NS).bitcast(BF16).rearrange("p (k q) -> p k q", k=4)
        attS = at(REL, HD)
        probsTS = [at(QT + 9 * KB * s, 17 * P).rearrange("p (k q) -> p k q", k=17) for s in range(2)]
        mtmp = [at(XT + 9216 + 2 * KB * s, 512) for s in range(2)]
        mT = at(GATE, KT * NTOK).rearrange("p (k n) -> p k n", k=KT)
        hT = mT
        xr = at(PV, NT * D).rearrange("p (t n) -> p t n", t=NT)
        lng, lnb = at(PV + 20 * KB, D), at(PV + 24 * KB, D)
        wrout = at(PV + 28 * KB, KT * NE).rearrange("p (k e) -> p k e", k=KT)
        rbias = at(PV + 30 * KB, NE)
        stat6 = at(PV + 30 * KB + 256, 12).rearrange("p (c k) -> p c k", c=2)
        mv = at(PV + 30 * KB + 320, 2)
        rstd = at(PV + 30 * KB + 336, 2)
        R0 = PV + 8 * KB
        sS = at(R0, NT * NE).rearrange("p (t e) -> p t e", t=NT)
        selM = at(R0 + 1280, NT * NE).rearrange("p (t e) -> p t e", t=NT)
        sbt = at(R0 + 2560, NE)
        g88 = at(R0 + 2816, NE).rearrange("p (g k) -> p g k", g=8)
        gsum = at(R0 + 3072, 8)
        gtop = at(R0 + 3104, 8)
        gidx = at(R0 + 3136, 8).bitcast(U32)
        gidf = at(R0 + 3168, 8)
        geq = at(R0 + 3200, 32).rearrange("p (g k) -> p g k", g=8)
        gmask = at(R0 + 3328, 8)
        gadd = at(R0 + 3360, 8)
        msk = at(R0 + 3392, NE)
        e8 = at(R0 + 3648, 8)
        repl = at(R0 + 3680, NE)
        ggate = at(R0 + 3936, NE)
        gden = at(R0 + 4192, 4)
        incl = at(R0 + 4208, NE)
        tok8 = at(R0 + 4464, 8)
        shsig = [at(R0 + 5 * KB + KB * s, ED) for s in range(2)]
        shact = [at(R0 + 7 * KB + KB * s, ED) for s in range(2)]
        shaT = at(R0 + 10 * KB, 2 * NTOK).rearrange("p (k n) -> p k n", k=2)
        V4 = at(SMALL, NT * NE * 4).rearrange("p (t e k) -> p t e k", t=NT, e=NE)
        posm = at(SMALL + 5120, NT * NE).rearrange("p (t e) -> p t e", t=NT)
        meta = at(SMALL + 6400, 4 * 4).rearrange("p (s k) -> p s k", s=4)
        metai = meta.bitcast(U32)
        WSLOT = 24 * KB
        w13 = [at(LG + WSLOT * s, KT * 512).rearrange("p (k n) -> p k n", k=KT) for s in range(4)]
        w2 = [at(LG + WSLOT * s + 16 * KB, 2 * D).rearrange("p (k n) -> p k n", k=2) for s in range(4)]
        xg = [at(PV + (8 + 4 * s) * KB, D) for s in range(2)]
        xgT = [at(PV + (16 + 4 * s) * KB, D).rearrange("p (k n) -> p k n", k=KT) for s in range(2)]
        ye = [at(PV + 24 * KB, D), at(GATE + 12 * KB, D)]
        onehot = [at(GATE + 2560 * s, NT * P).rearrange("p (t n) -> p t n", t=NT) for s in range(2)]
        esig = [at(GATE + (5 + s) * KB, ED) for s in range(2)]
        eact = [at(GATE + (7 + s) * KB, ED) for s in range(2)]
        eactT = [at(GATE + (9 + s) * KB, 2 * P).rearrange("p (k n) -> p k n", k=2) for s in range(2)]
        longest = at(SMALL + 6528, 8, 1)
        blocks_f = at(SMALL + 6560, 8, 1)
        blocks_i = at(SMALL + 6592, 1, 1).bitcast(I32)
        yt = [at(LG + 32 * KB * s, TOPE * D).rearrange("p (j n) -> p j n", j=TOPE) for s in range(2)]
        g2, b2 = at(LG + 64 * KB, D), at(LG + 68 * KB, D)
        wpin = at(LG + 72 * KB, 2 * D).rearrange("p (k n) -> p k n", k=2)
        h2T = [at(PV + (8 + 4 * s) * KB, D).rearrange("p (k n) -> p k n", k=KT) for s in range(2)]
        pnat = at(LG + 85 * KB, NT * PLE).rearrange("p (t n) -> p t n", t=NT)
        peT = at(LG + 80 * KB, 2 * NTOK).rearrange("p (k n) -> p k n", k=2)
        sg = [at(GATE + 2 * KB * s, 512) for s in range(2)]
        pez = [at(GATE + (4 + 2 * s) * KB, 512) for s in range(2)]
        wpg = at(RING, KT * D).rearrange("p (k n) -> p k n", k=KT)
        stat6b = at(GATE + 9 * KB, 12).rearrange("p (c k) -> p c k", c=2)
        mvb = at(GATE + 9 * KB + 64, 2)
        rstdb = at(GATE + 9 * KB + 80, 2)

        ps = [ctx.enter_context(nc.psum_tensor(f"ps{i}", [P, 512], F32)) for i in range(8)]

        h_dram = nc.dram_tensor("h_rows", [NTOK, D], F32, kind="Internal").ap()
        y_dram = nc.dram_tensor("y_rows", [NTOK * TOPE, D], F32, kind="Internal").ap()

        xp = a["x_prompt"].rearrange("a (t p) n -> p (a t) n", p=P)
        xsm = a["x_sample"].rearrange("b t n -> (b t) n")
        w_in = a["w_in"][0].rearrange("(k p) n -> p k n", p=P)
        out_k_p = o["k_prompt"].rearrange("a b (t p) d -> p (a b t) d", p=P)
        out_v_p = o["v_prompt"].rearrange("a b (t p) d -> p (a b t) d", p=P)
        out_i_p = o["kidx_prompt"].rearrange("a b (t p) d -> p (a b t) d", p=P)
        out_k_s = o["k_sample"].rearrange("a b t d -> (a b t) d")
        out_v_s = o["v_sample"].rearrange("a b t d -> (a b t) d")
        out_i_s = o["kidx_sample"].rearrange("a b t d -> (a b t) d")

        def wide(w, rows, c0, c1):
            return a[w][0].rearrange("(k p) n -> p k n", p=P)[:, :, c0:c1]

        RING_ITEMS = [("wq", w_in[:, :, QC:QC + 512], ("q", NT - 1)), ("wkv", w_in[:, :, KVC:UC], ("kv", NT - 1)),
                      ("wu", w_in[:, :, UC:GAC], ("u", PG - 1, 1)),
                      ("wgb0", w_in[:, :, GBC:GBC + 512], ("gb", 0, NT - 1)),
                      ("wgb1", w_in[:, :, GBC + 512:GBC + 1024], ("gb", 1, NT - 1)),
                      ("wpo", wide("w_pool_out", 4, 0, D), ("pm", NT - 1, 1)),
                      ("wga0", w_in[:, :, GAC:GAC + 512], ("ga", 0, NT - 1)),
                      ("wga1", w_in[:, :, GAC + 512:GAC + 1024], ("ga", 1, NT - 1)),
                      ("wao", wide("w_att_out", 4, 0, D), ("m1", NT - 1, 1)),
                      ("wo0", wide("w_out", 8, 0, 512), ("wo", 0, NT - 1)),
                      ("wo1", wide("w_out", 8, 512, D), ("wo", 1, NT - 1)),
                      ("sh13", wide("w_sh13", 8, 0, 512), ("s13", NT - 1)),
                      ("sh2", wide("w_sh2", 2, 0, D), ("s2", NT - 1, 1))]
        ring_no = {name: n for n, (name, _, _) in enumerate(RING_ITEMS)}

        def ring_view(name):
            n = ring_no[name]
            k, w = RING_ITEMS[n][1].shape[1:]
            return ring[n % 2][:, 0:k * w].rearrange("p (k n) -> p k n", k=k)

        bank_filled = {"act": sem("banks_filled_for_scalar"), "dve": sem("banks_filled_for_vector")}
        bank_read = {"act": sem("banks_read_by_scalar"), "dve": sem("banks_read_by_vector")}
        consts_in = sem("consts_in")
        rotary_in = sem("rotary_in")
        x_in = [sem(f"x_in{t}") for t in range(NT)]
        ring_in = [sem("ring_in0"), sem("ring_in1")]
        pages_in = sem("page_table_in")
        knat_in = [sem("cached_keys_in0"), sem("cached_keys_in1")]
        v_in = sem("cached_values_in")
        rows_cleared = sem("rows_cleared")
        roped = sem("roped")
        rows_stored = [sem("rows_stored0"), sem("rows_stored1")]
        vnew_in = sem("new_values_in")
        step = sem("vector_step")
        pstep = sem("pool_step")
        comb_ready = sem("index_weights_ready")
        rel_used = sem("relu_rows_used")
        summed = sem("prompt_scores_summed")
        barred = sem("later_keys_barred")
        struck = sem("struck")
        mask_s = sem("sample_mask_ready")
        aux_in = sem("pool_inputs_in")
        cleared = sem("pool_edges_cleared")
        ust_out = sem("pool_rows_stored")
        pooled = sem("pooled")
        mixed = sem("pool_branch_mixed")
        maxed = sem("row_max_ready")
        expd = sem("exp_done")
        pv_done = sem("pv_done")
        att_ready = sem("att_ready")
        xr_in = sem("residual_in")
        ln_in = sem("layer_norm_weights_in")
        m_ready = sem("gated_sum_ready")
        var_ready = sem("variance_ready")
        rstd_ready = sem("rstd_ready")
        h_ready = sem("h_ready")
        h_stored = sem("h_stored")
        s_ready = sem("router_scores_ready")
        routed = sem("routed")
        shsig_ready = sem("shared_sigmoid_ready")
        sh_done = sem("shared_done")
        sha_ready = sem("shared_act_ready")

        ew_in = [sem(f"expert_weights_in{s}") for s in range(4)]
        oh_ready = sem("onehot_ready")
        list_ready = sem("list_ready")
        meta_ready = sem("meta_ready")
        xg_clear = sem("gather_buffers_cleared")
        gathered = [sem("gathered0"), sem("gathered1")]
        turned = sem("gathered_turned")
        xta = sem("turned_read_by_scalar")
        xtb = sem("turned_read_by_vector")
        up = sem("up_done")
        sig_ready = sem("sigmoid_ready")
        silu_done = sem("silu_done")
        act_ready = sem("act_ready")
        act_turned = sem("act_turned")
        actT_ready = sem("actT_ready")
        down = sem("down_done")
        ya = sem("y_half_by_scalar")
        yb = sem("y_half_by_vector")
        scattered = [sem("scattered0"), sem("scattered1")]

        passed_dve = sem("vector_passed_a_wait")
        passed_pool = sem("pool_passed_a_wait")

        ov_w = sem("further_weights_in")
        ov_v = sem("further_vector_steps")
        ov_p = sem("further_tensor_steps")
        ov_a = sem("further_scalar_steps")
        ov_g = sem("further_gathered")
        ov_s = sem("further_scattered")
        shifted = sem("further_block_shifted")
        ov_done = sem("further_rounds_done")

        y_in = [sem("choices_in0"), sem("choices_in1")]
        fin_in = sem("finish_inputs_in")
        pe_turned = sem("embeddings_turned")
        pe_read = sem("embeddings_read")
        y_summed = sem("choices_summed")
        var2 = sem("variance2_ready")
        rstd2 = sem("rstd2_ready")
        h2_ready = sem("h2_ready")
        h2_turned = sem("h2_turned")
        h2_read = sem("h2T_ready")
        gate_up = sem("ple_gate_up")
        pin_up = sem("ple_in_up")
        sg_ready = sem("ple_sigmoid_ready")
        mul_done = sem("ple_product_done")
        out_ready = sem("out_ready")
        stored = sem("outputs_stored")

        order = {"pe": [], "act": [], "dve": []}

        def filled(eng, key):
            who, n = number[key]
            eng.wait_ge(bank_filled[who], n)

        def read(eng, key):
            who, n = number[key]
            eng.wait_ge(bank_read[who], n)

        def claim(pe, key):
            order["pe"].append(key)
            if prev[key]:
                read(pe, prev[key])
            return ps[bank_of[key]]

        def take(eng, key):
            order[number[key][0]].append(key)
            filled(eng, key)
            return ps[bank_of[key]]

        def fills(ins, key):
            ins.then_inc(bank_filled[number[key][0]], 1)

        def frees(ins, key):
            ins.then_inc(bank_read[number[key][0]], 1)

        def weights(pe, name):
            n = ring_no[name]
            pe.wait_ge(ring_in[n % 2], 16 * (n // 2 + 1))
            return ring_view(name)

        def all_rows_stored(eng):
            eng.wait_ge(rows_stored[0], 16 * 3 * 3)
            eng.wait_ge(rows_stored[1], 16 * 3 * 2)

        def span(t):
            return slice(P * t, P * t + ROWS[t])

        V_STEPS, P_STEPS = 6, 5

        def further(eng, body, before=None):
            eng.wait_ge(ov_v, 1)
            extra = eng.value_load(blocks_i[0:1, 0:1], min_val=0, max_val=(NTOK - 1) // CAP)
            with eng.If(extra > 0):
                with eng.Fori(0, extra) as blk:
                    if before:
                        before(blk)
                    with eng.Fori(0, NE) as e:
                        body(blk * NE + e, e)
            return extra * NE

        block = ctx.enter_context(nc.Block())


        @block.sync
        def _(sp):
            sp.dma_start(cst, a["consts"]).then_inc(consts_in, 16)
            for t in range(4):
                sp.dma_start(xs[:, t, :], xp[:, t, :]).then_inc(x_in[t], 16)
            sp.dma_start(xs[0:NS, 4, :], xsm).then_inc(x_in[4], 16)

            def load_ring(name):
                n = ring_no[name]
                if n >= 2:
                    filled(sp, RING_ITEMS[n - 2][2])
                sp.dma_start(ring_view(name), RING_ITEMS[n][1]).then_inc(ring_in[n % 2], 16)

            load_ring("wq")
            load_ring("wkv")

            def load_keys(b, s):
                with sp.Fori(0, NPG) as g:
                    page = sp.value_load(pages[0:1, bass.ds(b * NPG + g, 1)], min_val=0, max_val=a["n_phys"] - 1)
                    dst = knat[s][:, bass.ds(g, 1), :]
                    sp.dma_start(dst[:, 0, 0:IDX], a["cache_kidx"][0][bass.ds(page, 1)].rearrange("a p d -> p (a d)")).then_inc(knat_in[s], 16)
                    sp.dma_start(dst[:, 0, IDX:], a["cache_k"][0][bass.ds(page, 1)].rearrange("a p d -> p (a d)")).then_inc(knat_in[s], 16)

            sp.wait_ge(pages_in, 16)
            for b in range(DB):
                if b >= 2:
                    filled(sp, ("kT", b - 2, 3))
                load_keys(b, b % 2)
                if b == 2:
                    load_ring("wu")
                if b == 3:
                    load_ring("wgb0")
            for name in ("wgb1", "wpo", "wga0", "wga1"):
                load_ring(name)
            for t in range(NT):
                filled(sp, ("pm", t, 1))
            sp.wait_ge(mixed, 2 * NT)
            with sp.Fori(0, DB * NPG) as g:
                page = sp.value_load(pages[0:1, bass.ds(g, 1)], min_val=0, max_val=a["n_phys"] - 1)
                sp.dma_start(values[:, bass.ds(g, 1), :][:, 0, :], a["cache_v"][0][bass.ds(page, 1)].rearrange("a p d -> p (a d)")).then_inc(v_in, 16)
            load_ring("wao")
            load_ring("wo0")
            sp.wait_ge(pv_done, 4 + 4)
            for t in range(4):
                sp.dma_start(xr[:, t, :], xp[:, t, :]).then_inc(xr_in, 16)
            sp.dma_start(xr[0:NS, 4, :], xsm).then_inc(xr_in, 16)
            sp.dma_start(lng, a["ln1_g"].partition_broadcast(P)).then_inc(ln_in, 16)
            sp.dma_start(lnb, a["ln1_b"].partition_broadcast(P)).then_inc(ln_in, 16)
            sp.dma_start(wrout, a["w_router"][0].rearrange("(k p) e -> p k e", p=P)).then_inc(ln_in, 16)
            sp.dma_start(rbias, a["router_bias"].partition_broadcast(P)).then_inc(ln_in, 16)

            def load_expert(e, s, static):
                if not static:
                    sp.wait_ge(down, 2 * e - 6)
                sp.dma_start(w13[s], a["w_exp13"][0][bass.ds(e, 1)].rearrange("a (k p) n -> p (a k) n", p=P)).then_inc(ew_in[s], 16)
                sp.dma_start(w2[s], a["w_exp2"][0][bass.ds(e, 1)].rearrange("a (k p) n -> p (a k) n", p=P)).then_inc(ew_in[s], 16)

            read(sp, ("ost", 3))
            load_expert(0, 0, True)
            load_expert(1, 1, True)
            load_ring("wo1")
            sp.wait_ge(m_ready, NT)
            load_expert(2, 2, True)
            load_ring("sh13")
            load_ring("sh2")
            read(sp, ("wo", 1, NT - 1))
            load_expert(3, 3, True)
            with sp.Fori(1, NE // 4) as q4:
                for s in range(4):
                    load_expert(4 * q4 + s, s, False)
            sp.wait_ge(sh_done, 1)
            sp.dma_start(wpg, a["w_ple_gate"][0].rearrange("(k p) n -> p k n", p=P)).then_inc(fin_in, 16)
            sp.wait_ge(down, 2 * NE)
            sp.dma_start(g2, a["ln2_g"].partition_broadcast(P)).then_inc(fin_in, 16)
            sp.dma_start(b2, a["ln2_b"].partition_broadcast(P)).then_inc(fin_in, 16)
            sp.dma_start(wpin, a["w_ple_in"][0].rearrange("(k p) n -> p k n", p=P)).then_inc(fin_in, 16)
            sp.dma_start(pnat[:, 0:4, :], a["p_prompt"].rearrange("a b (t p) n -> p (a b t) n", p=P)).then_inc(fin_in, 16)
            sp.dma_start(pnat[0:NS, 4, :], a["p_sample"].rearrange("a b t n -> (a b t) n")).then_inc(fin_in, 16)

            def further_weights(n, e):
                sp.wait_ge(ov_done, n + 1)
                sp.dma_start(w13[0], a["w_exp13"][0][bass.ds(e, 1)].rearrange("a (k p) n -> p (a k) n", p=P)).then_inc(ov_w, 16)
                sp.dma_start(w2[0], a["w_exp2"][0][bass.ds(e, 1)].rearrange("a (k p) n -> p (a k) n", p=P)).then_inc(ov_w, 16)

            rounds = further(sp, further_weights)
            sp.wait_ge(ov_done, rounds + 1)
            for t in range(NT):
                if t >= 2:
                    sp.wait_ge(y_summed, t - 1)
                sp.dma_start(yt[t % 2][0:ROWS[t]], y_dram[TOPE * P * t:TOPE * (P * t + ROWS[t]), :].rearrange("(p j) n -> p j n", j=TOPE)).then_inc(y_in[t % 2], 16)
            yp = o["y_prompt"].rearrange("a (t p) n -> p (a t) n", p=P)
            ysm = o["y_sample"].rearrange("b t n -> (b t) n")
            for t in range(NT):
                sp.wait_ge(out_ready, 2 * t + 2)
                sp.dma_start(yp[:, t, :] if t < 4 else ysm, m[0:ROWS[t], t, :]).then_inc(stored, 16)
            sp.wait_ge(stored, 16 * NT)
            all_rows_stored(sp)
            sp.wait_ge(ust_out, 48)

        @block.gpsimd
        def _(pool):
            count = [0]

            def link(ins):
                count[0] += 1
                ins.then_inc(pstep, 1)
                pool.wait_ge(pstep, count[0])

            pool.dma_start(rotary, a["rotary"].rearrange("(t p) c d -> p t c d", p=P)).then_inc(rotary_in, 16)
            pool.dma_start(pages, a["page_table"].rearrange("b g -> (b g)").unsqueeze(0)).then_inc(pages_in, 16)
            pool.dma_start(pscale, a["pool_scale"][0].rearrange("(g p) -> p g", p=P), allow_slow_non_contiguous=True).then_inc(aux_in, 16)
            for s in range(2):
                ins = nc.gpsimd.memset(rowsR[:, s, 4:8, 0:HD], 0.0)
            ins.then_inc(rows_cleared, 1)

            for t in range(NT):
                pool.wait_ge(roped, t + 1)
                n, s = ROWS[t], t % 2
                pool.dma_start(out_k_p[:, t, :] if t < 4 else out_k_s, rowsR[0:n, s, 8, IDX:]).then_inc(rows_stored[s], 16)
                pool.dma_start(out_i_p[:, t, :] if t < 4 else out_i_s, rowsR[0:n, s, 8, 0:IDX]).then_inc(rows_stored[s], 16)
                pool.dma_start(out_v_p[:, t, :] if t < 4 else out_v_s, v_prompt[:, t, :] if t < 4 else v_samp).then_inc(rows_stored[s], 16)
            all_rows_stored(pool)
            pool.dma_start(v_new, o["v_sample"][0].rearrange("b t d -> t b d")).then_inc(vnew_in, 16)

            link(nc.gpsimd.memset(scoreP[0], 0.0))
            nc.gpsimd.affine_select(out=scoreP[0], in_=scoreP[0], compare_op=ALU.is_ge, fill=MASKED, base=0,
                                    pattern=[[-1, P]], channel_multiplier=1).then_inc(barred, 1)
            for t in range(1, 4):
                pool.wait_ge(summed, t)
                diag = scoreP[t][:, P * t:P * t + P]
                nc.gpsimd.affine_select(out=diag, in_=diag, compare_op=ALU.is_ge, fill=BARRED, base=0,
                                        pattern=[[-1, P]], channel_multiplier=1).then_inc(barred, 1)

            pool.dma_start(wgrp, a["w_pool_grp"][0].rearrange("g c d -> c g d")).then_inc(aux_in, 16)
            link(nc.gpsimd.memset(uext[:, :, 0:PST], 0.0))
            nc.gpsimd.memset(uext[:, :, PST + SEQ:528], 0.0).then_inc(cleared, 1)
            filled(pool, ("sc", 1, 4))
            pool.dma_start(stnat, a["state_pool"][0].rearrange("b s n -> (b s) n")).then_inc(aux_in, 16)
            pool.dma_start(o["pool_sample"][0, :, 0:PST - DT, :], a["state_pool"][0, :, DT:PST, :]).then_inc(ust_out, 16)
            read(pool, ("uo", 1))
            pool.dma_start(o["pool_prompt"][0, 0], ust[0:PST, 0, :]).then_inc(ust_out, 16)
            pool.dma_start(o["pool_sample"][0, :, PST - DT:PST, :].rearrange("b t n -> b t n"), ust[0:NS, 1, :]).then_inc(ust_out, 16)
            read(pool, ("uo", 1))

            pool.wait_ge(consts_in, 16)
            icount = const("icount").rearrange("p (g n) -> p g n", g=PG)
            for g in range(PG):
                if g >= 1:
                    pool.wait_ge(pooled, g)
                w = 2 ** (g + 1)
                src, srcs = uext[:, g, :], uexs[:, g, :, :]
                for lv in range(g + 1):
                    d = 2 ** lv
                    j0 = 2 ** (lv + 1) - 1
                    nc.gpsimd.tensor_tensor(win[lv % 2][:, j0:527], src[:, j0:527], src[:, j0 - d:527 - d], ALU.add)
                    link(nc.gpsimd.tensor_tensor(wins[lv % 2][:, :, j0:23], srcs[:, :, j0:23], srcs[:, :, j0 - d:23 - d], ALU.add))
                    src, srcs = win[lv % 2], wins[lv % 2]
                u = uext[:, g, :]
                nc.gpsimd.tensor_scalar(src[:, 31:527], src[:, 31:527], 1.0 / w, None, ALU.mult)
                nc.gpsimd.tensor_scalar(srcs[:, :, 15:23], srcs[:, :, 15:23], 1.0 / w, None, ALU.mult)
                link(nc.gpsimd.tensor_tensor(src[:, 15:31], src[:, 15:31], icount[:, g, :], ALU.mult))
                link(nc.gpsimd.tensor_tensor(u[:, 15:527], src[:, 15:527], u[:, 15:527], ALU.subtract))
                us = uexs[:, g, :, 15:23]
                nc.gpsimd.tensor_tensor(us, srcs[:, :, 15:23], us, ALU.subtract).then_inc(pooled, 1)
            for n, (t, c) in enumerate([(t, c) for t in range(NT) for c in range(2)]):
                read(pool, ("pm", t, c))
                r = ROWS[t]
                nc.gpsimd.tensor_tensor(m[0:r, t, 512 * c:512 * c + 512], m[0:r, t, 512 * c:512 * c + 512], pmt[n % 2][0:r, :], ALU.mult).then_inc(mixed, 1)

            for t in range(NT):
                r = ROWS[t]
                pool.wait_ge(var_ready, t + 1)
                nc.gpsimd.tensor_tensor(rstd[0:r, 0:1], mv[0:r, 1:2], const("mhalf", r), ALU.pow).then_inc(rstd_ready, 1)
                pool.wait_ge(h_ready, t + 1)
                pool.dma_start(h_dram[P * t:P * t + r, :], m[0:r, t, :]).then_inc(h_stored, 16)

            pool.wait_ge(h_stored, 16 * NT)
            pool.wait_ge(sh_done, 1)
            for s in range(2):
                ins = nc.gpsimd.memset(xg[s], 0.0)
            ins.then_inc(xg_clear, 1)
            pool.wait_ge(xg_clear, 1)

            last_row, last_choice = pool.to_reg(NTOK - 1), pool.to_reg(NTOK * TOPE - 1)

            def gather(e, k, q):
                pool.wait_ge(meta_ready, e + 1)
                if not (isinstance(e, int) and e < 2):
                    pool.wait_ge(turned, 2 * e - 2)
                pool.sem_inc(passed_pool, 1)
                pool.indirect_dma_start(out=xg[k % 2], out_offset=None, in_=h_dram,
                                        in_offset=bass.IndirectOffsetOnAxis(ap=metai[:, k, 0:1], axis=0),
                                        bounds_check=last_row, oob_is_err=False).then_inc(gathered[k % 2], 16)

            def scatter(e, k, q):
                pool.wait_ge(ya, e + 1)
                pool.wait_ge(yb, e + 1)
                pool.sem_inc(passed_pool, 1)
                pool.indirect_dma_start(out=y_dram, out_offset=bass.IndirectOffsetOnAxis(ap=metai[:, k, 1:2], axis=0),
                                        in_=ye[k % 2], in_offset=None,
                                        bounds_check=last_choice, oob_is_err=False).then_inc(scattered[k % 2], 16)

            def expert(i, k, first=False, last=False):
                if not (last and k >= 2):
                    gather(i + 2, (k + 2) % 4, None)
                if not (first and k == 0):
                    scatter(i - 1, (k - 1) % 4, None)

            gather(0, 0, 0)
            gather(1, 1, 0)
            for k in range(4):
                expert(k, k, first=True)
            with pool.Fori(1, NE // 4 - 1) as q4:
                for k in range(4):
                    expert(4 * q4 + k, k)
            for k in range(4):
                expert(NE - 4 + k, k, last=True)
            scatter(NE - 1, 3, None)
            for s in range(2):
                pool.wait_ge(scattered[s], 16 * NE // 2)
            pool.sem_inc(ov_done, 1)

            def further_rows(n, e):
                pool.wait_ge(ov_v, V_STEPS * n + 3)
                pool.sem_inc(passed_pool, 1)
                pool.indirect_dma_start(out=xg[0], out_offset=None, in_=h_dram,
                                        in_offset=bass.IndirectOffsetOnAxis(ap=metai[:, 0, 0:1], axis=0),
                                        bounds_check=last_row, oob_is_err=False).then_inc(ov_g, 16)
                pool.wait_ge(ov_v, V_STEPS * n + 7)
                pool.sem_inc(passed_pool, 1)
                pool.indirect_dma_start(out=y_dram, out_offset=bass.IndirectOffsetOnAxis(ap=metai[:, 0, 1:2], axis=0),
                                        in_=ye[0], in_offset=None,
                                        bounds_check=last_choice, oob_is_err=False).then_inc(ov_s, 16)
                pool.wait_ge(ov_s, 16 * n + 16)
                pool.sem_inc(ov_done, 1)

            further(pool, further_rows)

            for t in range(NT):
                r = ROWS[t]
                pool.wait_ge(var2, t + 1)
                nc.gpsimd.tensor_tensor(rstdb[0:r, 0:1], mvb[0:r, 1:2], const("mhalf", r), ALU.pow).then_inc(rstd2, 1)

        @block.scalar
        def _(act):
            def copy(out, in_, scale=1.0):
                return nc.scalar.activation(out, in_, ACT.Copy, scale=scale)

            for t in range(NT):
                b = take(act, ("xT", t, 0))
                frees(copy(xT[:, 0:4, span(t)], b[:, :].rearrange("p (k n) -> p k n", k=4)[:, :, 0:ROWS[t]]), ("xT", t, 0))
            for t in range(NT):
                n = ROWS[t]
                for i in range(2):
                    b = take(act, ("rt", t, i))
                    heads4 = b[:, :].rearrange("p (k n) -> p k n", k=4)[:, :, 0:n]
                    if t < 4:
                        ins = copy(qT[:, 4 * i:4 * i + 4, span(t)], heads4)
                    else:
                        ins = copy(qTs[:, :, 4 * i:4 * i + 4, :].rearrange("p b h t -> p h b t"),
                                   heads4.rearrange("p h (b t) -> p h b t", b=DB))
                    frees(ins, ("rt", t, i))
                b = take(act, ("rt", t, 2))
                frees(copy(kk_prompt[:, span(t)] if t < 4 else kk_new, b[:, 0:n]), ("rt", t, 2))
            c_idx = IDX ** -0.5 * IH ** -0.5
            for n, (t, h) in enumerate([(t, h) for t in range(1, 4) for h in range(IH)]):
                b = take(act, ("dot", t, h))
                if n == 0:
                    act.wait_ge(roped, NT)
                if n >= 4:
                    act.wait_ge(rel_used, n - 3)
                frees(nc.scalar.activation(relP[n % 4][:, 0:KEYS[t]], b[:, 0:KEYS[t]], ACT.Relu, scale=c_idx), ("dot", t, h))

            def keysT(b):
                for i in (1, 3):
                    bk = take(act, ("kT", b, i))
                    frees(copy(kkT[b % 2][:, 512 * i:512 * i + 512], bk[:, :]), ("kT", b, i))

            act.wait_ge(rel_used, 12)
            keysT(0)
            for b in range(DB):
                if b + 1 < DB:
                    keysT(b + 1)
                if b == 4:
                    filled(act, ("sc", 0, 4))
                q = 32 * (b % 4)
                for c in range(5):
                    bk = take(act, ("sd", b, c))
                    w = 512 if c < 4 else DT
                    frees(nc.scalar.activation(relS[q:q + 32, 512 * c:512 * c + w], bk[q:q + 32, 0:w], ACT.Relu, scale=c_idx), ("sd", b, c))

            all_rows_stored(act)
            act.wait_ge(cleared, 1)
            bk = take(act, ("st",))
            frees(copy(uexs[:, :, :, 0:PST], bk[:, 0:480].rearrange("p (g b n) -> p g b n", g=PG, b=DB)), ("st",))
            for g in range(PG):
                bk = take(act, ("u", g, 0))
                frees(copy(uext[:, g, PST:PST + SEQ], bk[:, :]), ("u", g, 0))
                bk = take(act, ("u", g, 1))
                copy(uflat[:, g, :], bk[:, 0:NS])
                frees(copy(uexs[:, g, :, PST:], bk[:, 0:NS].rearrange("p (b n) -> p b n", b=DB)), ("u", g, 1))
            bk = take(act, ("uo", 0))
            ins = copy(ust[0:PST, 0, :], bk[0:PST, :])
            frees(ins, ("uo", 0))
            bk = take(act, ("uo", 1))
            frees(copy(ust[0:NS, 1, :], bk[0:NS, :]), ("uo", 1))
            for c in range(2):
                for t in range(NT):
                    r = ROWS[t]
                    bk = take(act, ("gb", c, t))
                    frees(nc.scalar.activation(m[0:r, t, 512 * c:512 * c + 512], bk[0:r, :], ACT.Sigmoid), ("gb", c, t))
            act.wait_ge(aux_in, 48)
            for g in range(PG):
                bk = take(act, ("pp", g, 0))
                frees(copy(poolT[:, g, 0:SEQ], bk[:, :], scale=pscale[:, g:g + 1]), ("pp", g, 0))
                bk = take(act, ("pp", g, 1))
                frees(copy(poolT[:, g, SEQ:], bk[:, 0:NS], scale=pscale[:, g:g + 1]), ("pp", g, 1))
            for n, (t, c) in enumerate([(t, c) for t in range(NT) for c in range(2)]):
                bk = take(act, ("pm", t, c))
                if n >= 2:
                    act.wait_ge(mixed, n - 1)
                frees(copy(pmt[n % 2][0:ROWS[t], :], bk[0:ROWS[t], :]), ("pm", t, c))
            for c in range(2):
                for t in range(NT):
                    r = ROWS[t]
                    bk = take(act, ("ga", c, t))
                    frees(nc.scalar.activation(sga[0:r, t, 512 * c:512 * c + 512], bk[0:r, :], ACT.Sigmoid), ("ga", c, t))

            heads = [(t, h) for t in range(4) for h in range(H)]

            def exp_p(n):
                t, h = heads[n]
                act.wait_ge(maxed, n + 1)
                col = 8 * (t % 2) + h
                nc.scalar.activation(probs[n % 3][:, 0:KEYS[t]], probs[n % 3][:, 0:KEYS[t]], ACT.Exp,
                                     bias=nmax[:, col:col + 1], accum_out=esum[:, col:col + 1]).then_inc(expd, 1)

            exp_p(0)
            for n, (t, h) in enumerate(heads):
                if n + 1 < len(heads):
                    exp_p(n + 1)
                if h % 2:
                    bk = take(act, ("pt", t, h))
                    frees(copy(probsT[n % 2][:, 0:KEYS[t]], bk[:, 0:KEYS[t]]), ("pt", t, h))
                if h == H - 1:
                    bk = take(act, ("at", t))
                    frees(copy(attnT[:, :, span(t)], bk[:, :].rearrange("p (k n) -> p k n", k=4)), ("at", t))
            for p in range(4):
                act.wait_ge(maxed, 32 + p + 1)
                nc.scalar.activation(logit[:, p, :], logit[:, p, :], ACT.Exp, bias=nmax[:, p:p + 1],
                                     accum_out=esum[:, p:p + 1]).then_inc(expd, 1)
                for i in (1, 3):
                    bk = take(act, ("ps", p, i))
                    frees(copy(probsTS[p % 2][:, 4 * i:4 * i + 4, :], bk[:, :].rearrange("p (k n) -> p k n", k=4)), ("ps", p, i))
            for t in range(NT):
                r = ROWS[t]
                bk = take(act, ("mT", t, 0))
                frees(copy(mT[:, 0:4, span(t)], bk[:, :].rearrange("p (k n) -> p k n", k=4)[:, :, 0:r]), ("mT", t, 0))
            for t in range(NT):
                r = ROWS[t]
                for i in range(2):
                    bk = take(act, ("hT", t, i))
                    frees(copy(hT[:, 4 * i:4 * i + 4, span(t)], bk[:, :].rearrange("p (k n) -> p k n", k=4)[:, :, 0:r]), ("hT", t, i))
            for t in range(NT):
                r = ROWS[t]
                bk = take(act, ("r", t))
                if t == 0:
                    read(act, ("wo", 1, NT - 1))
                frees(nc.scalar.activation(sS[0:r, t, :], bk[0:r, 0:NE], ACT.Sigmoid), ("r", t))
            for t in range(NT):
                r = ROWS[t]
                filled(act, ("s13", t))
                if t >= 2:
                    act.wait_ge(sha_ready, t - 1)
                nc.scalar.activation(shsig[t % 2][0:r, :], ps[bank_of[("s13", t)]][0:r, 0:ED], ACT.Sigmoid).then_inc(shsig_ready, 1)
            for t in range(NT):
                r = ROWS[t]
                bk = take(act, ("s13T", t))
                frees(copy(shaT[:, :, span(t)], bk[:, 0:256].rearrange("p (k n) -> p k n", k=2)[:, :, 0:r]), ("s13T", t))

            def x_turned(e):
                act.wait_ge(turned, e + 1)
            def xgT_half(e, k):
                act.wait_ge(turned, 2 * e + 1)
                copy(xgT[k % 2][:, 0:4, :], ps[4][:, :].rearrange("p (k n) -> p k n", k=4)).then_inc(xta, 1)

            def y_half(e, k):
                act.wait_ge(down, 2 * e + 1)
                if not (isinstance(e, int) and e < 2):
                    act.wait_ge(scattered[k % 2], 8 * e - 8 * (k % 2))
                copy(ye[k % 2][:, 0:512], ps[2][:, :], scale=meta[:, k, 2:3]).then_inc(ya, 1)

            def expert(i, k, first=False, last=False):
                act.wait_ge(up, i + 1)
                if not (first and k < 2):
                    act.wait_ge(act_ready, i - 1)
                nc.scalar.activation(esig[k % 2], ps[k % 2][:, 0:ED], ACT.Sigmoid).then_inc(sig_ready, 1)
                if not (first and k == 0):
                    y_half(i - 1, (k - 1) % 4)
                if not (last and k == 3):
                    xgT_half(i + 1, (k + 1) % 4)
                act.wait_ge(act_turned, i + 1)
                copy(eactT[k % 2], ps[7][:, 0:256].rearrange("p (k n) -> p k n", k=2)).then_inc(actT_ready, 1)

            act.wait_ge(sh_done, 1)
            xgT_half(0, 0)
            for k in range(4):
                expert(k, k, first=True)
            with act.Fori(1, NE // 4 - 1) as q4:
                for k in range(4):
                    expert(4 * q4 + k, k)
            for k in range(4):
                expert(NE - 4 + k, k, last=True)
            y_half(NE - 1, 3)

            def further_sigmoid(n, e):
                act.wait_ge(ov_p, P_STEPS * n + 3)
                nc.scalar.activation(esig[0], ps[0][:, 0:ED], ACT.Sigmoid).then_inc(ov_a, 1)

            further(act, further_sigmoid)

            for t in range(NT):
                r = ROWS[t]
                act.wait_ge(pe_turned, t + 1)
                copy(peT[:, :, span(t)], ps[6][:, 0:256].rearrange("p (k n) -> p k n", k=2)[:, :, 0:r]).then_inc(pe_read, 1)
            for t in range(NT):
                r = ROWS[t]
                for i in range(2):
                    act.wait_ge(h2_turned, 2 * t + i + 1)
                    copy(h2T[t % 2][:, 4 * i:4 * i + 4, 0:r], ps[4 + i][:, :].rearrange("p (k n) -> p k n", k=4)[:, :, 0:r]).then_inc(h2_read, 1)
                for c in range(2):
                    n = 2 * t + c
                    act.wait_ge(gate_up, n + 1)
                    if n >= 2:
                        act.wait_ge(mul_done, n - 1)
                    nc.scalar.activation(sg[c][0:r, :], ps[c][0:r, :], ACT.Sigmoid).then_inc(sg_ready, 1)

        @block.tensor
        def _(pe):
            mm = nc.tensor.matmul

            def turn4(key, srcs, rows, cols=P):
                b = claim(pe, key)
                for j, src in enumerate(srcs):
                    ins = nc.tensor.transpose(b[0:cols, P * j:P * j + rows], src, ident[0:rows, 0:rows])
                fills(ins, key)

            pe.wait_ge(consts_in, 16)
            for t in range(NT):
                pe.wait_ge(x_in[t], 16)
                for i in range(2):
                    turn4(("xT", t, i), [xs[0:ROWS[t], t, P * k:P * k + P] for k in range(4 * i, 4 * i + 4)], ROWS[t])

            def project(key, t, w, width, last=None):
                b = claim(pe, key)
                for k in range(KT):
                    ins = mm(b[0:ROWS[t], 0:width], xT[:, k, span(t)], w[:, k, 0:width], start=(k == 0), stop=(k == KT - 1))
                fills(ins, key)
                return ins

            def qkv(t):
                read(pe, ("xT", t, 0))
                read(pe, ("xT", t, 1))
                project(("q", t), t, weights(pe, "wq"), 512)
                project(("kv", t), t, weights(pe, "wkv"), KVW)

            def rt(t):
                pe.wait_ge(roped, t + 1)
                s, n = t % 2, ROWS[t]
                turn4(("rt", t, 0), [rowsR[0:n, s, j, :] for j in range(4)], n)
                turn4(("rt", t, 1), [rowsR[0:n, s, j, :] for j in range(4, 8)], n)
                turn4(("rt", t, 2), [rowsR[0:n, s, 8, :]], n)

            qkv(0)
            for t in range(1, NT):
                qkv(t)
                rt(t - 1)
            rt(NT - 1)
            sel = const("sel", NS).rearrange("p (g q) -> p g q", g=2)
            b = claim(pe, ("wsel",))
            for g in range(2):
                ins = mm(b[:, 4 * g:4 * g + 4], sel[:, g, :], wi[0:NS, 4, :], start=True, stop=True)
            fills(ins, ("wsel",))
            for t in range(1, 4):
                for h in range(IH):
                    if h == 0 and t == 1:
                        read(pe, ("rt", NT - 1, 2))
                    b = claim(pe, ("dot", t, h))
                    fills(mm(b[:, 0:KEYS[t]], qT[0:IDX, h, span(t)], kk_prompt[0:IDX, 0:KEYS[t]], start=True, stop=True), ("dot", t, h))

            def keysT(b):
                pe.wait_ge(knat_in[b % 2], 512 * (b // 2 + 1))
                for i in range(4):
                    turn4(("kT", b, i), [knat[b % 2][:, 4 * i + j, :] for j in range(4)], P)

            keysT(0)
            for b in range(DB):
                if b + 1 < DB:
                    keysT(b + 1)
                q, o2 = 32 * (b % 4), 64 * (b % 2)
                for c in range(5):
                    key = ("sd", b, c)
                    bk = claim(pe, key)
                    if c < 4:
                        read(pe, ("kT", b, c))
                        keys, w = kkT[b % 2][:, 512 * c:512 * c + 512], 512
                    else:
                        keys, w = kk_new[:, DT * b:DT * b + DT], DT
                    fills(mm(bk[q:q + 32, 0:w], qTs[0:IDX, b, 0:IH, :].rearrange("p h t -> p (h t)"), keys[0:IDX, :], start=True, stop=True), key)
                    key = ("sl", b, c)
                    bk = claim(pe, key)
                    fills(mm(bk[o2:o2 + 64, 0:w], qTs[IDX:, b, :, :].rearrange("p h t -> p (h t)"), keys[IDX:, :], start=True, stop=True), key)
                if b % 4 == 3:
                    g = b // 4
                    pe.wait_ge(comb_ready, 1)
                    for c in range(5):
                        key = ("sc", g, c)
                        w = 512 if c < 4 else DT
                        bk = claim(pe, key)
                        read(pe, ("sd", b, c))
                        fills(mm(bk[32 * g:32 * g + 32, 0:w], w_comb[:, g, :], relS[:, 512 * c:512 * c + w], start=True, stop=True), key)

            pe.wait_ge(aux_in, 48)
            key = ("st",)
            b = claim(pe, key)
            for g in range(PG):
                ins = nc.tensor.transpose(b[:, 120 * g:120 * g + 120], stnat[:, P * g:P * g + P], ident[0:120, 0:120])
            fills(ins, key)
            w = weights(pe, "wu")
            for g in range(PG):
                for i, (c0, c1) in enumerate(((0, SEQ), (SEQ, NTOK))):
                    key = ("u", g, i)
                    b = claim(pe, key)
                    for k in range(KT):
                        ins = mm(b[:, 0:c1 - c0], w[:, k, P * g:P * g + P], xT[:, k, c0:c1], start=(k == 0), stop=(k == KT - 1))
                    fills(ins, key)
            key = ("uo", 0)
            read(pe, ("u", PG - 1, 1))
            b = claim(pe, key)
            for g in range(PG):
                ins = nc.tensor.transpose(b[0:PST, P * g:P * g + P], uext[:, g, SEQ:SEQ + PST], ident)
            fills(ins, key)
            key = ("uo", 1)
            b = claim(pe, key)
            for g in range(PG):
                ins = nc.tensor.transpose(b[0:NS, P * g:P * g + P], uflat[:, g, :], ident)
            fills(ins, key)
            for c in range(2):
                w = weights(pe, f"wgb{c}")
                for t in range(NT):
                    project(("gb", c, t), t, w, 512)
            for g in range(PG):
                pe.wait_ge(pooled, g + 1)
                key = ("pp", g, 0)
                b = claim(pe, key)
                fills(mm(b[:, :], wgrp[:, g, :], uext[:, g, PST:PST + SEQ], start=True, stop=True), key)
                key = ("pp", g, 1)
                b = claim(pe, key)
                fills(mm(b[:, 0:NS], wgrp[:, g, :], uexs[:, g, :, PST:], start=True, stop=True), key)
            w = weights(pe, "wpo")
            read(pe, ("pp", PG - 1, 1))
            for t in range(NT):
                for c in range(2):
                    key = ("pm", t, c)
                    b = claim(pe, key)
                    for g in range(PG):
                        ins = mm(b[0:ROWS[t], :], poolT[:, g, span(t)], w[:, g, 512 * c:512 * c + 512], start=(g == 0), stop=(g == PG - 1))
                    fills(ins, key)
            for c in range(2):
                w = weights(pe, f"wga{c}")
                for t in range(NT):
                    project(("ga", c, t), t, w, 512)

            heads = [(t, h) for t in range(4) for h in range(H)]

            def logits(n):
                t, h = heads[n]
                key = ("l", t, h)
                b = claim(pe, key)
                fills(mm(b[:, 0:KEYS[t]], qT[IDX:, h, span(t)], kk_prompt[IDX:, 0:KEYS[t]], start=True, stop=True), key)

            logits(0)
            logits(1)
            for n, (t, h) in enumerate(heads):
                if n + 2 < len(heads):
                    logits(n + 2)
                pe.wait_ge(expd, n + 1)
                turn4(("pt", t, h), [probs[n % 3][:, P * j:P * j + P] for j in range(t + 1)], P)
                read(pe, ("pt", t, h))
                if h == 0 and t >= 2:
                    pe.wait_ge(att_ready, t - 1)
                for j in range(t + 1):
                    ins = mm(ps[6 + t % 2][:, HD * h:HD * h + HD], probsT[n % 2][:, P * j:P * j + P], v_prompt[:, j, :],
                             start=(j == 0), stop=(j == t))
                if h == H - 1:
                    ins.then_inc(pv_done, 1)
                    pe.wait_ge(att_ready, t + 1)
                    turn4(("at", t), [att[:, P * k:P * k + P] for k in range(4)], P)

            def bias(p):
                for c in range(5):
                    key = ("bs", p, c)
                    w = 512 if c < 4 else DT
                    b = claim(pe, key)
                    fills(mm(b[:, 0:w], rep_b[:, p, :], maskS[c][:, 0:w], start=True, stop=True), key)

            pe.wait_ge(mask_s, 1)
            bias(0)
            pe.wait_ge(v_in, 16 * DB * NPG)
            pe.wait_ge(vnew_in, 16)
            for p in range(4):
                if p < 3:
                    bias(p + 1)
                pe.wait_ge(expd, 32 + p + 1)
                for i in range(4):
                    turn4(("ps", p, i), [logit[:, p, P * (4 * i + j):P * (4 * i + j) + P] for j in range(4)], P)
                turn4(("ps", p, 4), [logit[:, p, PAST:SK]], P, DT)
                for i in range(5):
                    read(pe, ("ps", p, i))
                pv = ps[6 + p % 2]
                if p >= 2:
                    pe.wait_ge(att_ready, 4 + p - 1)
                for b2 in range(2):
                    o2 = 64 * b2
                    for g in range(NPG):
                        mm(pv[o2:o2 + 64, 0:HD], probsTS[p % 2][:, g, o2:o2 + 64], values[:, (2 * p + b2) * NPG + g, :], start=(g == 0), stop=False)
                    ins = mm(pv[o2:o2 + 64, 0:HD], probsTS[p % 2][0:DT, NPG, o2:o2 + 64], v_new[:, 2 * p + b2, :], start=False, stop=True)
                ins.then_inc(pv_done, 1)
                pe.wait_ge(att_ready, 4 + p + 1)
                turn4(("ost", p), [attS], P, HD)

            w = weights(pe, "wao")
            read(pe, ("at", 3))
            read(pe, ("ost", 3))
            for t in range(NT):
                for c in range(2):
                    key = ("m1", t, c)
                    b = claim(pe, key)
                    for k in range(4):
                        ins = mm(b[0:ROWS[t], :], attnT[:, k, span(t)], w[:, k, 512 * c:512 * c + 512], start=(k == 0), stop=(k == 3))
                    fills(ins, key)
            for t in range(NT):
                pe.wait_ge(m_ready, NT)
                for i in range(2):
                    turn4(("mT", t, i), [m[0:ROWS[t], t, P * k:P * k + P] for k in range(4 * i, 4 * i + 4)], ROWS[t])

            def by_tiles(tag, name, src, width):
                w = weights(pe, name)
                for t in range(NT):
                    b = claim(pe, tag + (t,))
                    for k in range(KT):
                        ins = mm(b[0:ROWS[t], 0:width], src[:, k, span(t)], w[:, k, 0:width], start=(k == 0), stop=(k == KT - 1))
                    fills(ins, tag + (t,))

            read(pe, ("mT", NT - 1, 0))
            read(pe, ("mT", NT - 1, 1))
            by_tiles(("wo", 0), "wo0", mT, 512)
            by_tiles(("wo", 1), "wo1", mT, 512)
            for t in range(NT):
                pe.wait_ge(h_ready, t + 1)
                for i in range(2):
                    turn4(("hT", t, i), [m[0:ROWS[t], t, P * k:P * k + P] for k in range(4 * i, 4 * i + 4)], ROWS[t])
            pe.wait_ge(ln_in, 64)
            for t in range(NT):
                read(pe, ("hT", t, 1))
                key = ("r", t)
                b = claim(pe, key)
                for k in range(KT):
                    ins = mm(b[0:ROWS[t], 0:NE], hT[:, k, span(t)], wrout[:, k, :], start=(k == 0), stop=(k == KT - 1))
                fills(ins, key)
            for t in range(NT):
                key = ("rank", t)
                pe.wait_ge(routed, t + 1)
                b = claim(pe, key)
                r = ROWS[t]
                for u in range(t):
                    mm(b[0:r, 0:NE], const("ones")[:, 0:r], selM[:, u, :], start=(u == 0), stop=False)
                fills(mm(b[0:r, 0:NE], const("upper", r)[:, 0:r], selM[0:r, t, :], start=(t == 0), stop=True), key)
            b = claim(pe, ("count",))
            for t in range(NT):
                ins = mm(b[0:1, 0:NE], const("ones", ROWS[t])[:, 0:1], selM[0:ROWS[t], t, :], start=(t == 0), stop=(t == NT - 1))
            fills(ins, ("count",))
            by_tiles(("s13",), "sh13", hT, 512)
            for t in range(NT):
                pe.wait_ge(sha_ready, t + 1)
                turn4(("s13T", t), [shact[t % 2][0:ROWS[t], P * k:P * k + P] for k in range(2)], ROWS[t])
            w = weights(pe, "sh2")
            for t in range(NT):
                read(pe, ("s13T", t))
                for c in range(2):
                    key = ("s2", t, c)
                    b = claim(pe, key)
                    for k in range(2):
                        ins = mm(b[0:ROWS[t], :], shaT[:, k, span(t)], w[:, k, 512 * c:512 * c + 512], start=(k == 0), stop=(k == 1))
                    fills(ins, key)

            def make_list(e, k):
                pe.wait_ge(oh_ready, e + 1)
                if not (isinstance(e, int) and e < 1):
                    pe.wait_ge(meta_ready, e)
                for t in range(NT):
                    r = ROWS[t]
                    ins = mm(ps[6][:, 0:4], onehot[k % 2][0:r, t, :], V4[0:r, t, bass.ds(e, 1), :][:, 0, :], start=(t == 0), stop=(t == NT - 1))
                ins.then_inc(list_ready, 1)

            def turn_x(e, k):
                pe.wait_ge(gathered[k % 2], 8 * e + 16 - 8 * (k % 2))
                if not (isinstance(e, int) and e < 1):
                    pe.wait_ge(xta, e)
                    pe.wait_ge(xtb, e)
                for i in range(2):
                    for j in range(4):
                        kk = 4 * i + j
                        ins = nc.tensor.transpose(ps[4 + i][:, P * j:P * j + P], xg[k % 2][:, P * kk:P * kk + P], ident)
                    ins.then_inc(turned, 1)

            def up_x(e, k):
                q16 = 8 * (e - k) + 32
                pe.wait_ge(ew_in[k], q16)
                pe.wait_ge(xta, e + 1)
                pe.wait_ge(xtb, e + 1)
                if not (isinstance(e, int) and e < 2):
                    pe.wait_ge(act_ready, e - 1)
                for kk in range(KT):
                    ins = mm(ps[k % 2][:, :], xgT[k % 2][:, kk, :], w13[k][:, kk, :], start=(kk == 0), stop=(kk == KT - 1))
                ins.then_inc(up, 1)

            def down_x(e, k):
                pe.wait_ge(actT_ready, e + 1)
                if not (isinstance(e, int) and e < 1):
                    pe.wait_ge(ya, e)
                    pe.wait_ge(yb, e)
                for c in range(2):
                    for kk in range(2):
                        ins = mm(ps[2 + c][:, :], eactT[k % 2][:, kk, :], w2[k][:, kk, 512 * c:512 * c + 512], start=(kk == 0), stop=(kk == 1))
                    ins.then_inc(down, 1)

            def turn_act(e, k):
                pe.wait_ge(act_ready, e + 1)
                if not (isinstance(e, int) and e < 1):
                    pe.wait_ge(actT_ready, e)
                for kk in range(2):
                    ins = nc.tensor.transpose(ps[7][:, P * kk:P * kk + P], eact[k % 2][:, P * kk:P * kk + P], ident)
                ins.then_inc(act_turned, 1)

            def expert(i, k, first=False, last=False):
                up_x(i, k)
                if not (first and k == 0):
                    down_x(i - 1, (k - 1) % 4)
                if not (last and k >= 2):
                    make_list(i + 2, (k + 2) % 4)
                if not (last and k == 3):
                    turn_x(i + 1, (k + 1) % 4)
                turn_act(i, k)

            pe.wait_ge(sh_done, 1)
            make_list(0, 0)
            make_list(1, 1)
            turn_x(0, 0)
            for k in range(4):
                expert(k, k, first=True)
            with pe.Fori(1, NE // 4 - 1) as q4:
                for k in range(4):
                    expert(4 * q4 + k, k)
            for k in range(4):
                expert(NE - 4 + k, k, last=True)
            down_x(NE - 1, 3)

            pe.wait_ge(ya, NE)
            pe.wait_ge(yb, NE)

            def further_products(n, e):
                pe.wait_ge(ov_v, V_STEPS * n + 2)
                for t in range(NT):
                    r = ROWS[t]
                    ins = mm(ps[6][:, 0:4], onehot[0][0:r, t, :], V4[0:r, t, bass.ds(e, 1), :][:, 0, :], start=(t == 0), stop=(t == NT - 1))
                ins.then_inc(ov_p, 1)
                pe.wait_ge(ov_g, 16 * n + 16)
                for kk in range(KT):
                    ins = nc.tensor.transpose(ps[4 + kk // 4][:, P * (kk % 4):P * (kk % 4) + P], xg[0][:, P * kk:P * kk + P], ident)
                ins.then_inc(ov_p, 1)
                pe.wait_ge(ov_w, 32 * n + 32)
                pe.wait_ge(ov_v, V_STEPS * n + 4)
                for kk in range(KT):
                    ins = mm(ps[0][:, :], xgT[0][:, kk, :], w13[0][:, kk, :], start=(kk == 0), stop=(kk == KT - 1))
                ins.then_inc(ov_p, 1)
                pe.wait_ge(ov_v, V_STEPS * n + 5)
                for kk in range(2):
                    ins = nc.tensor.transpose(ps[7][:, P * kk:P * kk + P], eact[0][:, P * kk:P * kk + P], ident)
                ins.then_inc(ov_p, 1)
                pe.wait_ge(ov_v, V_STEPS * n + 6)
                for c in range(2):
                    for kk in range(2):
                        ins = mm(ps[2 + c][:, :], eactT[0][:, kk, :], w2[0][:, kk, 512 * c:512 * c + 512], start=(kk == 0), stop=(kk == 1))
                ins.then_inc(ov_p, 1)

            rounds = further(pe, further_products)
            pe.wait_ge(ov_v, rounds * V_STEPS + 1)

            pe.wait_ge(fin_in, 96)
            for t in range(NT):
                r = ROWS[t]
                if t >= 1:
                    pe.wait_ge(pe_read, t)
                for k in range(2):
                    ins = nc.tensor.transpose(ps[6][:, P * k:P * k + r], pnat[0:r, t, P * k:P * k + P], ident[0:r, 0:r])
                ins.then_inc(pe_turned, 1)
            pe.wait_ge(pe_read, NT)
            for t in range(NT):
                r = ROWS[t]
                for c in range(2):
                    n = 2 * t + c
                    if n >= 2:
                        pe.wait_ge(mul_done, n - 1)
                    for k in range(2):
                        ins = mm(ps[2 + c][0:r, :], peT[:, k, span(t)], wpin[:, k, 512 * c:512 * c + 512], start=(k == 0), stop=(k == 1))
                    ins.then_inc(pin_up, 1)
                pe.wait_ge(h2_ready, t + 1)
                for i in range(2):
                    if t >= 1:
                        pe.wait_ge(h2_read, 2 * t)
                    for j in range(4):
                        k = 4 * i + j
                        ins = nc.tensor.transpose(ps[4 + i][:, P * j:P * j + r], m[0:r, t, P * k:P * k + P], ident[0:r, 0:r])
                    ins.then_inc(h2_turned, 1)
                pe.wait_ge(h2_read, 2 * t + 2)
                for c in range(2):
                    n = 2 * t + c
                    if n >= 2:
                        pe.wait_ge(sg_ready, n - 1)
                    for k in range(KT):
                        ins = mm(ps[c][0:r, :], h2T[t % 2][:, k, 0:r], wpg[:, k, 512 * c:512 * c + 512], start=(k == 0), stop=(k == KT - 1))
                    ins.then_inc(gate_up, 1)

        @block.vector
        def _(dve):
            v = nc.vector
            steps = [0]

            def link(ins):
                steps[0] += 1
                ins.then_inc(step, 1)
                dve.wait_ge(step, steps[0])

            def mine(key):
                read(dve, key)

            for t in range(NT):
                b = take(dve, ("xT", t, 1))
                frees(v.tensor_copy(xT[:, 4:8, span(t)], b[:, :].rearrange("p (k n) -> p k n", k=4)[:, :, 0:ROWS[t]]), ("xT", t, 1))
            dve.wait_ge(consts_in, 16)
            dve.wait_ge(rotary_in, 16)
            dve.wait_ge(rows_cleared, 1)

            def rotate(r, t, src, nh, a_, b_, out, last=None):
                s = src.rearrange("p (h d) -> p h d", h=nh)
                ca = a_.rearrange("p (h d) -> p h d", h=nh)
                cb = b_.rearrange("p (h d) -> p h d", h=nh)
                cos = rotary[0:r, t, 0, :].unsqueeze(1).broadcast_to([r, nh, HD])
                sin = rotary[0:r, t, 1, :].unsqueeze(1).broadcast_to([r, nh, HD])
                v.tensor_tensor(ca, s, cos, ALU.mult)
                v.tensor_tensor(cb[:, :, 0:32], s[:, :, 32:64], sin[:, :, 0:32], ALU.mult)
                return v.tensor_tensor(cb[:, :, 32:64], s[:, :, 0:32], sin[:, :, 32:64], ALU.mult), (ca, cb, out)

            def total(parts):
                ca, cb, out = parts
                return v.tensor_tensor(out, ca, cb, ALU.add)

            for t in range(NT):
                r, s = ROWS[t], t % 2
                if t >= 1:
                    dve.wait_ge(roped, t)
                if t >= 2:
                    filled(dve, ("rt", t - 2, 2))
                    dve.wait_ge(rows_stored[s], 16 * 3 * (t // 2))
                key = ("q", t)
                b = take(dve, key)
                ins, parts = rotate(r, t, b[0:r, 0:512], H, ropeA[0:r, :], ropeB[0:r, :], rowsR[0:r, s, 0:8, HD:])
                frees(ins, key)
                mine(key)
                link(total(parts))
                key = ("kv", t)
                b = take(dve, key)
                _, p1 = rotate(r, t, b[0:r, 0:64], 1, ropeA[0:r, 0:64], ropeB[0:r, 0:64], rowsR[0:r, s, 8:9, HD:])
                _, p2 = rotate(r, t, b[0:r, 128:448], 5, ropeA[0:r, 64:384], ropeB[0:r, 64:384], None)
                v.tensor_copy(v_prompt[:, t, :] if t < 4 else v_samp, b[0:r, 64:128])
                frees(v.tensor_copy(wi[0:r, t, :], b[0:r, 448:452]), key)
                mine(key)
                total(p1)
                v.tensor_tensor(rowsR[0:r, s, 0:4, 0:HD], p2[0][:, 0:4, :], p2[1][:, 0:4, :], ALU.add)
                v.tensor_tensor(rowsR[0:r, s, 8:9, 0:IDX], p2[0][:, 4:5, :], p2[1][:, 4:5, :], ALU.add).then_inc(roped, 1)

            key = ("wsel",)
            b = take(dve, key)
            for g in range(2):
                ins = v.tensor_tensor(wcol8[:, g, :], b[:, 4 * g:4 * g + 4], const("hmask"), ALU.mult)
            frees(ins, key)
            mine(key)
            link(v.tensor_reduce(wcol, wcol8, AX, ALU.add))
            for g in range(2):
                ins = v.tensor_scalar(w_comb[:, g, :], const("selT"), wcol[:, g:g + 1], None, ALU.mult)
            ins.then_inc(comb_ready, 1)
            for n, (t, h) in enumerate([(t, h) for t in range(1, 4) for h in range(IH)]):
                read(dve, ("dot", t, h))
                rel = relP[n % 4][:, 0:KEYS[t]]
                if h == 0:
                    v.tensor_scalar(scoreP[t], rel, wi[:, t, 0:1], None, ALU.mult).then_inc(rel_used, 1)
                else:
                    dve.wait_ge(rel_used, n)
                    v.scalar_tensor_tensor(out=scoreP[t], in0=rel, scalar=wi[:, t, h:h + 1], in1=scoreP[t],
                                           op0=ALU.mult, op1=ALU.add).then_inc(rel_used, 1)
                if h == IH - 1:
                    dve.wait_ge(rel_used, n + 1)
                    dve.sem_inc(summed, 1)

            def keysT(b):
                for i in (0, 2):
                    bk = take(dve, ("kT", b, i))
                    frees(v.tensor_copy(kkT[b % 2][:, 512 * i:512 * i + 512], bk[:, :]), ("kT", b, i))

            keysT(0)
            for b in range(DB):
                if b + 1 < DB:
                    keysT(b + 1)
                o2 = 64 * (b % 2)
                for c in range(5):
                    w = 512 if c < 4 else DT
                    bk = take(dve, ("sl", b, c))
                    frees(v.tensor_scalar(logit[o2:o2 + 64, b // 2, 512 * c:512 * c + w], bk[o2:o2 + 64, 0:w], HD ** -0.5, None, ALU.mult), ("sl", b, c))
                if b % 4 == 3:
                    g = b // 4
                    for c in range(5):
                        w = 512 if c < 4 else DT
                        bk = take(dve, ("sc", g, c))
                        frees(v.tensor_copy(scoreS[32 * g:32 * g + 32, 512 * c:512 * c + w], bk[32 * g:32 * g + 32, 0:w]), ("sc", g, c))

            dve.wait_ge(barred, 4)
            base = steps[0]
            per = 6
            with dve.Fori(0, TOP_P // 8) as i:
                for t in range(1, 4):
                    dve.wait_ge(step, base + per * i + t - 1)
                    dve.sem_inc(passed_dve, 1)
                    v.max(top8[:, t, :], scoreP[t]).then_inc(step, 1)
                for t in range(1, 4):
                    dve.wait_ge(step, base + per * i + 2 + t)
                    dve.sem_inc(passed_dve, 1)
                    v.match_replace(scoreP[t], top8[:, t, :], scoreP[t], STRUCK).then_inc(step, 1)
            steps[0] += per * (TOP_P // 8)
            dve.wait_ge(step, steps[0])
            for t in range(1, 4):
                link(v.tensor_scalar(scoreP[t], scoreP[t], STRUCK_TEST, MASKED, ALU.is_ge, ALU.mult))
            new = scoreS[:, PAST:SK]
            mine(("sc", 1, 4))
            link(v.tensor_tensor(new, new, const("newmask", NS), ALU.mult))
            link(v.tensor_scalar(top8[0:NS, 0, :], const("newmask", NS), -BARRED, BARRED, ALU.mult, ALU.add))
            link(v.tensor_tensor(new, new, top8[0:NS, 0, :], ALU.add))
            base_s = steps[0]
            with dve.Fori(0, TOP_S // 8) as i:
                dve.wait_ge(step, base_s + 2 * i)
                dve.sem_inc(passed_dve, 1)
                v.max(top8[0:NS, 0, :], scoreS).then_inc(step, 1)
                dve.wait_ge(step, base_s + 2 * i + 1)
                dve.sem_inc(passed_dve, 1)
                v.match_replace(scoreS, top8[0:NS, 0, :], scoreS, STRUCK).then_inc(step, 1)
            steps[0] += 2 * (TOP_S // 8)
            dve.wait_ge(step, steps[0])
            filled(dve, ("ga", 1, NT - 1))
            v.tensor_copy(rep_b, const("rep", NS).rearrange("p (k q) -> p k q", k=4))
            read(dve, ("uo", 1))
            dve.wait_ge(ust_out, 48)
            for c in range(5):
                w = 512 if c < 4 else DT
                ins = v.tensor_scalar(maskS[c][:, 0:w], scoreS[:, 512 * c:512 * c + w], STRUCK_TEST, MASKED, ALU.is_ge, ALU.mult)
            ins.then_inc(mask_s, 1)

            heads = [(t, h) for t in range(4) for h in range(H)]

            def row_max(n):
                t, h = heads[n]
                key = ("l", t, h)
                b = take(dve, key)
                if n >= 3:
                    filled(dve, ("pt",) + heads[n - 3])
                if n >= 1:
                    dve.wait_ge(maxed, n)
                col = 8 * (t % 2) + h
                frees(v.tensor_tensor_reduce(probs[n % 3][:, 0:KEYS[t]], b[:, 0:KEYS[t]], scoreP[t], HD ** -0.5, BARRED,
                                             ALU.add, ALU.max, mx[:, 0:1]), key)
                mine(key)
                v.tensor_scalar(nmax[:, col:col + 1], mx[:, 0:1], -1.0, None, ALU.mult).then_inc(maxed, 1)

            row_max(0)
            row_max(1)
            for n, (t, h) in enumerate(heads):
                if n + 2 < len(heads):
                    row_max(n + 2)
                if h % 2 == 0:
                    b = take(dve, ("pt", t, h))
                    frees(v.tensor_copy(probsT[n % 2][:, 0:KEYS[t]], b[:, 0:KEYS[t]]), ("pt", t, h))
                if h == H - 1:
                    c8 = 8 * (t % 2)
                    dve.wait_ge(expd, n + 1)
                    link(v.reciprocal(erec[:, c8:c8 + 8], esum[:, c8:c8 + 8]))
                    dve.wait_ge(pv_done, t + 1)
                    if t >= 1:
                        filled(dve, ("at", t - 1))
                    v.tensor_tensor(att[:, :].rearrange("p (h d) -> p h d", h=H), ps[6 + t % 2][:, :].rearrange("p (h d) -> p h d", h=H),
                                    erec[:, c8:c8 + 8].unsqueeze(2).broadcast_to([P, H, HD]), ALU.mult).then_inc(att_ready, 1)
            def bias_max(p):
                dve.wait_ge(maxed, 32 + p)
                for c in range(5):
                    w = 512 if c < 4 else DT
                    key = ("bs", p, c)
                    b = take(dve, key)
                    lg = logit[:, p, 512 * c:512 * c + w]
                    frees(v.tensor_tensor_reduce(lg, b[:, 0:w], lg, 1.0, BARRED, ALU.add, ALU.max, mx[:, c:c + 1]), key)
                mine(("bs", p, 4))
                link(v.tensor_reduce(mx[:, 0:1], mx[:, 0:5], AX, ALU.max))
                v.tensor_scalar(nmax[:, p:p + 1], mx[:, 0:1], -1.0, None, ALU.mult).then_inc(maxed, 1)

            dve.wait_ge(expd, 32)
            bias_max(0)
            for p in range(4):
                if p < 3:
                    bias_max(p + 1)
                for i in (0, 2):
                    b = take(dve, ("ps", p, i))
                    frees(v.tensor_copy(probsTS[p % 2][:, 4 * i:4 * i + 4, :], b[:, :].rearrange("p (k n) -> p k n", k=4)), ("ps", p, i))
                b = take(dve, ("ps", p, 4))
                frees(v.tensor_copy(probsTS[p % 2][0:DT, NPG, :], b[0:DT, 0:P]), ("ps", p, 4))
                dve.wait_ge(expd, 32 + p + 1)
                link(v.reciprocal(erec[:, p:p + 1], esum[:, p:p + 1]))
                dve.wait_ge(pv_done, 4 + p + 1)
                v.tensor_scalar(attS, ps[6 + p % 2][:, 0:HD], erec[:, p:p + 1], None, ALU.mult).then_inc(att_ready, 1)
                key = ("ost", p)
                b = take(dve, key)
                for odd in range(2):
                    src = b[0:HD, 0:P].rearrange("d (b k o t) -> d o k b t", b=2, k=4, o=2)[:, odd]
                    c0 = SEQ + 2 * DT * p
                    dst = attnT[64 * odd:64 * odd + 64, :, c0:c0 + 2 * DT].rearrange("d k (b t) -> d k b t", b=2)
                    ins = v.tensor_copy(dst, src)
                frees(ins, key)

            dve.wait_ge(mixed, 2 * NT)
            for n, (t, c) in enumerate([(t, c) for t in range(NT) for c in range(2)]):
                r = ROWS[t]
                key = ("m1", t, c)
                b = take(dve, key)
                cs = slice(512 * c, 512 * c + 512)
                frees(v.tensor_tensor(mtmp[n % 2][0:r, :], b[0:r, :], sga[0:r, t, cs], ALU.mult), key)
                mine(key)
                ins = v.tensor_tensor(m[0:r, t, cs], m[0:r, t, cs], mtmp[n % 2][0:r, :], ALU.add)
                if c == 1:
                    ins.then_inc(m_ready, 1)
            for t in range(NT):
                r = ROWS[t]
                b = take(dve, ("mT", t, 1))
                frees(v.tensor_copy(mT[:, 4:8, span(t)], b[:, :].rearrange("p (k n) -> p k n", k=4)[:, :, 0:r]), ("mT", t, 1))
            dve.wait_ge(xr_in, 16 * NT)
            for c in range(2):
                for t in range(NT):
                    r = ROWS[t]
                    key = ("wo", c, t)
                    b = take(dve, key)
                    cs = slice(512 * c, 512 * c + 512)
                    frees(v.scalar_tensor_tensor(out=m[0:r, t, cs], in0=xr[0:r, t, cs], scalar=ALPHA, in1=b[0:r, :],
                                                 op0=ALU.mult, op1=ALU.add), key)
            dve.wait_ge(ln_in, 64)

            def norm(t, st, mean_var, rs, var_sem, rstd_sem, gamma, beta, done):
                r = ROWS[t]
                row = m[0:r, t, :]
                for c in range(2):
                    link(v.bn_stats(st[0:r, c, :], row[:, 512 * c:512 * c + 512]))
                link(v.bn_aggr(mean_var[0:r, :], st[0:r, :, :]))
                v.tensor_scalar(mean_var[0:r, 1:2], mean_var[0:r, 1:2], EPS, None, ALU.add).then_inc(var_sem, 1)
                dve.wait_ge(rstd_sem, t + 1)
                link(v.tensor_scalar(row, row, mean_var[0:r, 0:1], rs[0:r, 0:1], ALU.subtract, ALU.mult))
                link(v.tensor_tensor(row, row, gamma[0:r, :], ALU.mult))
                v.tensor_tensor(row, row, beta[0:r, :], ALU.add).then_inc(done, 1)

            mine(("wo", 1, NT - 1))
            for t in range(NT):
                norm(t, stat6, mv, rstd, var_ready, rstd_ready, lng, lnb, h_ready)

            link(v.tensor_scalar(tok8[:, 0:5], const("tokid"), float(TOPE), -BIG, ALU.mult, ALU.add))
            for t in range(NT):
                r = ROWS[t]
                read(dve, ("r", t))
                sr = sS[0:r, t, :]
                link(v.tensor_tensor(sbt[0:r, :], sr, rbias[0:r, :], ALU.add))
                for g in range(8):
                    ins = v.max(g88[0:r, g, :], sbt[0:r, 8 * g:8 * g + 8])
                link(ins)
                link(v.tensor_tensor(gsum[0:r, :], g88[0:r, :, 0], g88[0:r, :, 1], ALU.add))
                link(v.max(gtop[0:r, :], gsum[0:r, :]))
                link(v.max_index(gidx[0:r, :], gtop[0:r, :], gsum[0:r, :]))
                link(v.tensor_copy(gidf[0:r, :], gidx[0:r, :]))
                link(v.tensor_tensor(geq[0:r], const("gid", r).rearrange("p (g k) -> p g k", g=8),
                                     gidf[0:r, 0:4].unsqueeze(1).broadcast_to([r, 8, 4]), ALU.is_equal))
                link(v.tensor_reduce(gmask[0:r, :], geq[0:r], AX, ALU.max))
                link(v.tensor_scalar(gadd[0:r, :], gmask[0:r, :], 1e30, -1e30, ALU.mult, ALU.add))
                mk = msk[0:r, :].rearrange("p (g k) -> p g k", g=8)
                link(v.tensor_tensor(mk, sbt[0:r, :].rearrange("p (g k) -> p g k", g=8), gmask[0:r, :].unsqueeze(2).broadcast_to([r, 8, 8]), ALU.mult))
                link(v.tensor_tensor(mk, mk, gadd[0:r, :].unsqueeze(2).broadcast_to([r, 8, 8]), ALU.add))
                link(v.max(e8[0:r, :], msk[0:r, :]))
                link(v.match_replace(repl[0:r, :], e8[0:r, :], msk[0:r, :], -2e30))
                link(v.tensor_scalar(selM[0:r, t, :], repl[0:r, :], -1.5e30, None, ALU.is_le))
                link(v.tensor_tensor(ggate[0:r, :], sr, selM[0:r, t, :], ALU.mult))
                link(v.tensor_reduce(gden[0:r, 0:1], ggate[0:r, :], AX, ALU.add))
                link(v.reciprocal(gden[0:r, 1:2], gden[0:r, 0:1]))
                v.tensor_scalar(V4[0:r, t, :, 2], ggate[0:r, :], gden[0:r, 1:2], SCALE_ROUTED, ALU.mult, ALU.mult)
                link(v.tensor_tensor_scan(incl[0:r, :], const("ones", r)[:, 0:NE], selM[0:r, t, :], 0.0, ALU.mult, ALU.add))
                link(v.tensor_tensor(incl[0:r, :], incl[0:r, :], selM[0:r, t, :], ALU.subtract))
                v.tensor_scalar(V4[0:r, t, :, 1], incl[0:r, :], tok8[0:r, t:t + 1], None, ALU.add)
                v.tensor_scalar(V4[0:r, t, :, 0], const("iota", r)[:, 0:NE], 0.0, const("tokid", r)[:, t:t + 1], ALU.mult, ALU.add)
                link(v.memset(V4[0:r, t, :, 3], 0.0))
                v.tensor_scalar(V4[0:r, t, :, 0], V4[0:r, t, :, 0], -BIG, None, ALU.add).then_inc(routed, 1)
            for t in range(NT):
                r = ROWS[t]
                key = ("rank", t)
                b = take(dve, key)
                frees(v.scalar_tensor_tensor(out=posm[0:r, t, :], in0=b[0:r, 0:NE], scalar=1.0, in1=selM[0:r, t, :],
                                             op0=ALU.add, op1=ALU.mult), key)
                mine(key)
                link(v.tensor_scalar(posm[0:r, t, :], posm[0:r, t, :], -1.0, None, ALU.add))
            b = take(dve, ("count",))
            frees(v.tensor_reduce(longest[:, 0:1], b[0:1, 0:NE], AX, ALU.max), ("count",))
            mine(("count",))
            link(v.tensor_scalar(blocks_f[:, 0:4], const("blocks", 1), longest[:, 0:1], None, ALU.is_lt))
            link(v.tensor_reduce(blocks_f[:, 4:5], blocks_f[:, 0:4], AX, ALU.add))
            v.tensor_copy(blocks_i, blocks_f[:, 4:5]).then_inc(ov_v, 1)
            for t in range(NT):
                r = ROWS[t]
                key = ("s13", t)
                b = take(dve, key)
                dve.wait_ge(shsig_ready, t + 1)
                if t >= 2:
                    filled(dve, ("s13T", t - 2))
                link(v.tensor_tensor(shact[t % 2][0:r, :], b[0:r, 0:ED], shsig[t % 2][0:r, :], ALU.mult))
                frees(v.tensor_tensor(shact[t % 2][0:r, :], b[0:r, ED:512], shact[t % 2][0:r, :], ALU.mult), key)
                mine(key)
                dve.sem_inc(sha_ready, 1)
            for t in range(NT):
                r = ROWS[t]
                for c in range(2):
                    cs = slice(512 * c, 512 * c + 512)
                    key = ("s2", t, c)
                    b = take(dve, key)
                    if (t, c) == (0, 0):
                        dve.wait_ge(h_stored, 16 * NT)
                    frees(v.scalar_tensor_tensor(out=m[0:r, t, cs], in0=m[0:r, t, cs], scalar=ALPHA, in1=b[0:r, :],
                                                 op0=ALU.mult, op1=ALU.add), key)
            mine(("s2", NT - 1, 1))
            dve.sem_inc(sh_done, 1)

            def one_hot(e, k):
                if not (isinstance(e, int) and e < 2):
                    dve.wait_ge(list_ready, e - 1)
                for t in range(NT):
                    r = ROWS[t]
                    ins = v.tensor_scalar(onehot[k % 2][0:r, t, :], const("iota", r), posm[0:r, t, bass.ds(e, 1)], None, ALU.is_equal)
                ins.then_inc(oh_ready, 1)

            def make_meta(e, k):
                dve.wait_ge(list_ready, e + 1)
                if not (isinstance(e, int) and e < 4):
                    dve.wait_ge(scattered[k % 2], 8 * e - 8 * (k % 2) - 16)
                v.tensor_scalar(metai[:, k, 0:2], ps[6][:, 0:2], BIG, None, ALU.add)
                v.tensor_copy(meta[:, k, 2:3], ps[6][:, 2:3]).then_inc(meta_ready, 1)

            def xgT_half(e, k):
                dve.wait_ge(turned, 2 * e + 2)
                v.tensor_copy(xgT[k % 2][:, 4:8, :], ps[5][:, :].rearrange("p (k n) -> p k n", k=4)).then_inc(xtb, 1)

            def y_half(e, k):
                dve.wait_ge(down, 2 * e + 2)
                if not (isinstance(e, int) and e < 2):
                    dve.wait_ge(scattered[k % 2], 8 * e - 8 * (k % 2))
                v.tensor_scalar(ye[k % 2][:, 512:1024], ps[3][:, :], meta[:, k, 2:3], None, ALU.mult).then_inc(yb, 1)

            def expert(i, k, first=False, last=False):
                if not (last and k >= 1):
                    one_hot(i + 3, (k + 3) % 4)
                dve.wait_ge(sig_ready, i + 1)
                if not (first and k < 2):
                    dve.wait_ge(act_turned, i - 1)
                v.tensor_tensor(esig[k % 2], ps[k % 2][:, 0:ED], esig[k % 2], ALU.mult).then_inc(silu_done, 1)
                dve.wait_ge(silu_done, i + 1)
                v.tensor_tensor(eact[k % 2], ps[k % 2][:, ED:512], esig[k % 2], ALU.mult).then_inc(act_ready, 1)
                if not (first and k == 0):
                    y_half(i - 1, (k - 1) % 4)
                if not (last and k >= 2):
                    make_meta(i + 2, (k + 2) % 4)
                if not (last and k == 3):
                    xgT_half(i + 1, (k + 1) % 4)

            one_hot(0, 0)
            one_hot(1, 1)
            one_hot(2, 2)
            make_meta(0, 0)
            make_meta(1, 1)
            xgT_half(0, 0)
            for k in range(4):
                expert(k, k, first=True)
            with dve.Fori(1, NE // 4 - 1) as q4:
                for k in range(4):
                    expert(4 * q4 + k, k)
            for k in range(4):
                expert(NE - 4 + k, k, last=True)
            y_half(NE - 1, 3)

            def next_block(blk):
                dve.wait_ge(ov_done, blk * NE + 1)
                for t in range(NT):
                    r = ROWS[t]
                    ins = v.tensor_scalar(posm[0:r, t, :], posm[0:r, t, :], -float(CAP), None, ALU.add)
                ins.then_inc(shifted, 1)
                dve.wait_ge(shifted, blk + 1)
                dve.sem_inc(passed_dve, 1)

            def further_steps(n, e):
                dve.wait_ge(ov_done, n + 1)
                for t in range(NT):
                    r = ROWS[t]
                    ins = v.tensor_scalar(onehot[0][0:r, t, :], const("iota", r), posm[0:r, t, bass.ds(e, 1)], None, ALU.is_equal)
                ins.then_inc(ov_v, 1)
                dve.wait_ge(ov_p, P_STEPS * n + 1)
                v.tensor_scalar(metai[:, 0, 0:2], ps[6][:, 0:2], BIG, None, ALU.add)
                v.tensor_copy(meta[:, 0, 2:3], ps[6][:, 2:3]).then_inc(ov_v, 1)
                dve.wait_ge(ov_p, P_STEPS * n + 2)
                v.tensor_copy(xgT[0][:, 0:4, :], ps[4][:, :].rearrange("p (k n) -> p k n", k=4))
                v.tensor_copy(xgT[0][:, 4:8, :], ps[5][:, :].rearrange("p (k n) -> p k n", k=4)).then_inc(ov_v, 1)
                dve.wait_ge(ov_a, n + 1)
                v.tensor_tensor(esig[0], ps[0][:, 0:ED], esig[0], ALU.mult).then_inc(silu_done, 1)
                dve.wait_ge(silu_done, n + NE + 1)
                v.tensor_tensor(eact[0], ps[0][:, ED:512], esig[0], ALU.mult).then_inc(ov_v, 1)
                dve.wait_ge(ov_p, P_STEPS * n + 4)
                v.tensor_copy(eactT[0], ps[7][:, 0:256].rearrange("p (k n) -> p k n", k=2)).then_inc(ov_v, 1)
                dve.wait_ge(ov_p, P_STEPS * n + 5)
                for c in range(2):
                    ins = v.tensor_scalar(ye[0][:, 512 * c:512 * c + 512], ps[2 + c][:, :], meta[:, 0, 2:3], None, ALU.mult)
                ins.then_inc(ov_v, 1)

            further(dve, further_steps, next_block)

            dve.wait_ge(fin_in, 96)
            for t in range(NT):
                r = ROWS[t]
                dve.wait_ge(y_in[t % 2], 16 * (t // 2 + 1))
                for j in range(TOPE):
                    ins = v.tensor_tensor(m[0:r, t, :], m[0:r, t, :], yt[t % 2][0:r, j, :], ALU.add)
                    if j < TOPE - 1:
                        link(ins)
                ins.then_inc(y_summed, 1)
                dve.wait_ge(y_summed, t + 1)
                norm(t, stat6b, mvb, rstdb, var2, rstd2, g2, b2, h2_ready)
                for c in range(2):
                    n = 2 * t + c
                    cs = slice(512 * c, 512 * c + 512)
                    dve.wait_ge(sg_ready, n + 1)
                    dve.wait_ge(pin_up, n + 1)
                    v.tensor_tensor(pez[c][0:r, :], ps[2 + c][0:r, :], sg[c][0:r, :], ALU.mult).then_inc(mul_done, 1)
                    dve.wait_ge(mul_done, n + 1)
                    v.tensor_tensor(m[0:r, t, cs], m[0:r, t, cs], pez[c][0:r, :], ALU.add).then_inc(out_ready, 1)

        for who in ("act", "dve"):
            want = [key for key, w_ in jobs if w_ == who]
            got = order[who] + ([("s13", t) for t in range(0)])
            assert got == want, (who, [x for x in zip(got, want) if x[0] != x[1]][:2], len(got), len(want))
        assert order["pe"] == [key for key, _ in jobs]


_INS = ['x_prompt', 'x_sample', 'cache_k', 'cache_v', 'cache_kidx', 'state_pool', 'page_table', 'p_prompt', 'p_sample',
        'w_in', 'w_att_out', 'w_pool_grp', 'pool_scale', 'w_pool_out', 'w_out', 'ln1_g', 'ln1_b', 'w_router',
        'router_bias', 'w_exp13', 'w_exp2', 'w_sh13', 'w_sh2', 'ln2_g', 'ln2_b', 'w_ple_in', 'w_ple_gate']
_OUTS = [('y_prompt', (1, 512, 1024)), ('y_sample', (8, 8, 1024)), ('k_prompt', (1, 1, 512, 64)),
         ('v_prompt', (1, 1, 512, 64)), ('kidx_prompt', (1, 1, 512, 64)), ('pool_prompt', (1, 1, 15, 512)),
         ('k_sample', (1, 8, 8, 64)), ('v_sample', (1, 8, 8, 64)), ('kidx_sample', (1, 8, 8, 64)),
         ('pool_sample', (1, 8, 15, 512))]


def kernel(**inputs):
    import numpy as _np
    import concourse.bacc as _bacc
    from concourse import mybir as _mybir
    from concourse.bass_utils import run_bass_kernel_spmd as _run

    nc = _bacc.Bacc("TRN2", target_bir_lowering=False, num_devices=1)
    arrays, a, o = {}, {}, {}
    data = {name: _np.ascontiguousarray(inputs[name]) for name in _INS}
    data["consts"], data["rotary"] = constants()
    for name, x in data.items():
        arrays[f"in_{name}"] = x
        a[name] = nc.dram_tensor(f"in_{name}", x.shape, _mybir.dt.from_np(x.dtype), kind="ExternalInput").ap()
    a["n_phys"] = data["cache_k"].shape[1]
    for name, shape in _OUTS:
        o[name] = nc.dram_tensor(f"out_{name}", shape, F32, kind="ExternalOutput").ap()
    build(nc, a, o)
    r = _run(nc, [arrays], core_ids=[0])
    return tuple(r.results[0][f"out_{name}"] for name, _ in _OUTS)
```

```python
from contextlib import ExitStack

import concourse.bass as bass
from concourse import mybir

P = 128
D = 1024
KT = D // P
SEQ = 512
DB = 8
DT = 8
NS = DB * DT
NTOK = SEQ + NS
PAST = 2048
PAGE = 128
NPG = PAST // PAGE
SK = PAST + DT
H = 8
HD = 64
IH = 4
IDX = 64
PG = 4
PST = 15
NE = 64
TOPE = 8
ED = 256
PLE = 256
TOP_P = 128
TOP_S = 256
ALPHA = 2 ** 0.25
EPS = 1e-5
SCALE_ROUTED = 2.5
CAP = 128
BIG = 8192.0
STRUCK = -3.4e38
BARRED = -3.0e38
STRUCK_TEST = -3.3e38
MASKED = -1e30

F32 = mybir.dt.float32
BF16 = mybir.dt.bfloat16
I32 = mybir.dt.int32
U32 = mybir.dt.uint32
ALU = mybir.AluOpType
ACT = mybir.ActivationFunctionType
AX = mybir.AxisListType.X

ROWS = [128, 128, 128, 128, 64]
NT = len(ROWS)
LAST_ORDER = [4, 0, 1, 2, 3]
KEYS = [128 * (t + 1) for t in range(4)]
SP_OFF = [0, 128, 384, 768]

QC, KVC, UC, GAC, GBC = 0, 512, 964, 1476, 2500
KVW = UC - KVC

CONSTS = {}
_at = 0
for _name, _w in (("ident", 128), ("upper", 128), ("ones", 128), ("iota", 128), ("hmask", 4), ("selT", 32),
                  ("icount", 64), ("newmask", 8), ("tokid", 5), ("sel", 256), ("rep", 512), ("mhalf", 1), ("blocks", 4)):
    CONSTS[_name] = (_at, _w)
    _at += _w
NCONST = _at


def constants():
    import numpy as np
    c = np.zeros((P, NCONST), np.float32)

    def put(name, a):
        o, w = CONSTS[name]
        c[:a.shape[0], o:o + w] = a.reshape(a.shape[0], w)

    p = np.arange(P)
    put("ident", np.eye(P))
    put("upper", (p[:, None] < p[None, :]).astype(np.float32))
    put("ones", np.ones((P, P)))
    put("iota", np.tile(np.where(p < CAP, p, -5)[None, :], (P, 1)))
    h_of = (p // 8) % 4
    put("hmask", (h_of[:, None] == np.arange(4)[None, :]))
    bt = (p // 32) * 8 + p % 8
    put("selT", (bt[:, None] == np.arange(32)[None, :]))
    ic = np.stack([1.0 / np.minimum(np.arange(16) + 1, w) for w in (2, 4, 8, 16)]).astype(np.float32)
    put("icount", np.tile(ic.reshape(1, 64), (P, 1)))
    r = np.arange(64)
    put("newmask", (np.arange(8)[None, :] <= (r % 8)[:, None]))
    put("tokid", (np.arange(5)[None, :] * 128 + p[:, None]).astype(np.float32))
    sel = np.zeros((64, 2, 128))
    for g in range(2):
        for q in range(128):
            sel[(4 * g + q // 32) * 8 + q % 8, g, q] = 1
    put("sel", sel)
    rep = np.zeros((64, 4, 128))
    for k in range(4):
        for q in range(128):
            rep[(2 * k + q // 64) * 8 + q % 8, k, q] = 1
    put("rep", rep)
    put("blocks", np.tile(CAP * np.arange(1, 5)[None, :], (P, 1)))
    put("mhalf", np.full((P, 1), -0.5))
    pos = np.concatenate([np.arange(SEQ), np.tile(PAST + np.arange(DT), DB)]).astype(np.float32)
    inv = (10000.0 ** (-np.arange(0, HD, 2) / HD)).astype(np.float32)
    ang = (pos[:, None] * inv[None, :]).astype(np.float32)
    cs, sn = np.cos(ang.astype(np.float64)).astype(np.float32), np.sin(ang.astype(np.float64)).astype(np.float32)
    rot = np.zeros((NT * P, 2, HD), np.float32)
    rot[:NTOK, 0] = np.concatenate([cs, cs], 1)
    rot[:NTOK, 1] = np.concatenate([-sn, sn], 1)
    return c, rot


def plan_banks():
    jobs = []
    add = lambda key, who: jobs.append((key, who))
    for t in range(NT):
        add(("xT", t, 0), "act")
        add(("xT", t, 1), "dve")

    def qkv(t):
        add(("q", t), "dve")
        add(("kv", t), "dve")

    def rt(t):
        for i in range(3):
            add(("rt", t, i), "act")

    qkv(0)
    for t in range(1, NT):
        qkv(t)
        rt(t - 1)
    rt(NT - 1)
    add(("wsel",), "dve")
    for t in range(1, 4):
        for h in range(IH):
            add(("dot", t, h), "act")
    def kT(b):
        for i in range(4):
            add(("kT", b, i), "act" if i % 2 else "dve")
    kT(0)
    for b in range(DB):
        if b + 1 < DB:
            kT(b + 1)
        for c in range(5):
            add(("sd", b, c), "act")
            add(("sl", b, c), "dve")
        if b % 4 == 3:
            for c in range(5):
                add(("sc", b // 4, c), "dve")
        if 1 <= b <= PG:
            add(("u", b - 1, 0), "act")
            add(("u", b - 1, 1), "act")
    add(("st",), "act")
    add(("uo", 0), "act")
    add(("uo", 1), "act")
    for c in range(2):
        for t in range(NT):
            add(("gb", c, t), "act")
    for g in range(PG):
        add(("pp", g, 0), "act")
        add(("pp", g, 1), "act")
    for t in range(NT):
        for c in range(2):
            add(("pm", t, c), "act")
    for c in range(2):
        for t in range(NT):
            add(("ga", c, t), "act")
    heads = [(t, h) for t in range(4) for h in range(H)]
    for n in range(3):
        add(("l",) + heads[n], "dve")
    add(("pt",) + heads[0], "dve")
    for n, (t, h) in enumerate(heads):
        if n + 3 < len(heads):
            add(("l",) + heads[n + 3], "dve")
        if n + 1 < len(heads):
            add(("pt",) + heads[n + 1], "dve" if n % 2 else "act")
        if h == 0 and t > 0:
            add(("at", t - 1), "act")
    add(("at", 3), "act")
    for c in range(5):
        add(("bs", 0, c), "dve")
    for p in range(4):
        if p < 3:
            for c in range(5):
                add(("bs", p + 1, c), "dve")
        for i in range(5):
            add(("ps", p, i), "act" if i % 2 else "dve")
        add(("ost", p), "dve")
    for t in range(NT):
        for c in range(2):
            add(("m1", t, c), "dve")
    for t in range(NT):
        add(("mT", t, 0), "act")
        add(("mT", t, 1), "dve")
    for t in range(NT):
        for c in range(2):
            add(("wo", c, t), "dve")
    for t in range(NT):
        add(("hT", t, 0), "act")
        add(("hT", t, 1), "act")
    for t in range(NT):
        add(("r", t), "act")
    for t in range(NT):
        add(("s13", t), "dve")
    for t in range(NT):
        add(("rank", t), "dve")
    add(("count",), "dve")
    for t in range(NT):
        add(("s13T", t), "act")
    for t in range(NT):
        for c in range(2):
            add(("s2", t, c), "dve")
    return jobs


def build(nc, a, o):
    jobs = plan_banks()
    NB = 6
    number, bank_of, prev = {}, {}, {}
    count = {"act": 0, "dve": 0}
    last_in = [None] * NB
    for n, (key, who) in enumerate(jobs):
        count[who] += 1
        number[key] = (who, count[who])
        bank_of[key] = n % NB
        prev[key] = last_in[n % NB]
        last_in[n % NB] = key

    ctx = ExitStack()
    with ctx:
        def sem(name):
            return ctx.enter_context(nc.semaphore(name))

        KB = 1024
        ARENA = 212800
        arena = ctx.enter_context(nc.sbuf_tensor("arena", [P, ARENA // 4], F32))

        def at(byte, width, rows=P):
            assert byte % 4 == 0 and byte + 4 * width <= ARENA, (byte, width)
            return arena[0:rows, byte // 4:byte // 4 + width]

        C0, SMALL, RING, GATE = 0, 7 * KB, 14 * KB, 46 * KB
        assert NCONST * 4 <= SMALL
        LG = GATE + 40 * KB
        SS = LG + 4 * SK * 4
        REL = SS + SK * 4
        SPR = REL + SK * 4
        XT = SPR + sum(KEYS) * 4
        QT = XT + 18 * KB
        PV = QT + 18 * KB

        def const(name, rows=P):
            of, w = CONSTS[name]
            return at(C0 + 4 * of, w, rows)

        cst = at(C0, NCONST)
        ident = const("ident")
        small = [SMALL]

        def little(width, rows=P):
            v = at(small[0], width, rows)
            small[0] += 4 * width
            assert small[0] <= RING
            return v

        v_prompt = little(4 * HD).rearrange("p (t d) -> p t d", t=4)
        kk_prompt = little(SEQ)
        kk_new = little(NS)
        v_new = little(DB * HD, 8).rearrange("p (b d) -> p b d", b=DB)
        v_samp = little(HD, NS)
        wi = little(NT * IH).rearrange("p (t h) -> p t h", t=NT)
        wcol8 = little(8).rearrange("p (g h) -> p g h", g=2)
        wcol = little(2)
        w_comb = little(64).rearrange("p (g q) -> p g q", g=2)
        top8 = little(4 * 8).rearrange("p (t k) -> p t k", t=4)
        mx = little(5)
        nmax = little(16)
        esum = little(16)
        erec = little(16)
        pscale = little(PG)
        pages = little(P, 1).bitcast(I32)
        mask_new = little(4, NS).bitcast(BF16)

        ring = [at(RING + 16 * KB * s, 4096) for s in range(2)]
        xs = at(GATE, NT * D).rearrange("p (t n) -> p t n", t=NT)
        xT = at(XT, KT * NTOK).rearrange("p (k n) -> p k n", k=KT)
        qT = at(QT, H * SEQ).rearrange("p (h n) -> p h n", h=H)
        qTs = at(QT + 4 * H * SEQ, H * NS).rearrange("p (b h t) -> p b h t", b=DB, h=H)
        rowsR = at(PV, 2 * 9 * P).rearrange("p (s h d) -> p s h d", s=2, h=9)
        ropeA = at(PV + 10 * KB, 512)
        ropeB = at(PV + 12 * KB, 512)
        rotary = at(REL, NT * 2 * HD).rearrange("p (t c d) -> p t c d", t=NT, c=2)
        KEY_SLOTS = 4
        POOL_PAGES = 8
        knat = [at(where, NPG * P).rearrange("p (g d) -> p g d", g=NPG)
                for where in (GATE + 20 * KB, GATE + 28 * KB, PV + 14 * KB, PV + 22 * KB)]
        kkT = [at(GATE + 8 * KB * s, PAST) for s in range(2)]
        relP = [at(REL + 2 * KB * s, 512) for s in range(4)]
        relS = at(REL, SK)
        scoreS = at(SS, SK, NS)
        scoreP = [at(SPR + 4 * SP_OFF[t], KEYS[t]) for t in range(4)]
        logit = at(LG, 4 * SK).rearrange("p (c s) -> p c s", c=4)
        uext = at(PV, PG * 528).rearrange("p (g n) -> p g n", g=PG)
        uexs = at(PV + 8448, PG * DB * 23).rearrange("p (g b n) -> p g b n", g=PG, b=DB)
        win = [at(PV + 11392 + 2112 * s, 528) for s in range(2)]
        wins = [at(PV + 15616 + 736 * s, DB * 23).rearrange("p (b n) -> p b n", b=DB) for s in range(2)]
        wgrp = at(PV + 17152, PG * P).rearrange("p (g d) -> p g d", g=PG)
        poolT = at(PV + 19200, PG * NTOK).rearrange("p (g n) -> p g n", g=PG)
        pmt = [at(PV + 28416 + 2048 * s, 512) for s in range(2)]
        ust = at(REL, 1024).rearrange("p (s n) -> p s n", s=2)
        stnat = at(REL + 4096, 512, DB * PST)
        uflat = at(PV + 11392, PG * NS).rearrange("p (g n) -> p g n", g=PG)
        sga = at(GATE, NT * D).rearrange("p (t n) -> p t n", t=NT)
        m = at(GATE + 20 * KB, NT * D).rearrange("p (t n) -> p t n", t=NT)
        values = at(PV, DB * NPG * HD).rearrange("p (g d) -> p g d", d=HD)
        probs = [at(REL + 2 * KB * s, 512) for s in range(3)]
        attnT = at(XT, 4 * NTOK).rearrange("p (k n) -> p k n", k=4)
        att = at(XT + 9216, 512)
        probsT = [at(XT + 11264 + 2 * KB * s, 512) for s in range(2)]
        maskS = [at(REL + 6 * KB, 256, NS).bitcast(BF16), at(REL + 7 * KB, 256, NS).bitcast(BF16),
                 at(XT + 15360, 256, NS).bitcast(BF16), at(XT + 16384, 256, NS).bitcast(BF16),
                 mask_new]
        rep_b = at(XT + 17408, 256, NS).bitcast(BF16).rearrange("p (k q) -> p k q", k=4)
        attS = at(REL, HD)
        probsTS = [at(QT + 9 * KB * s, 17 * P).rearrange("p (k q) -> p k q", k=17) for s in range(2)]
        mtmp = [at(XT + 9216 + 2 * KB * s, 512) for s in range(2)]
        mT = at(GATE, KT * NTOK).rearrange("p (k n) -> p k n", k=KT)
        hT = mT
        xr = at(PV, NT * D).rearrange("p (t n) -> p t n", t=NT)
        lng, lnb = at(PV + 20 * KB, D), at(PV + 24 * KB, D)
        wrout = at(PV + 28 * KB, KT * NE).rearrange("p (k e) -> p k e", k=KT)
        rbias = at(PV + 30 * KB, NE)
        stat6 = at(PV + 30 * KB + 256, 12).rearrange("p (c k) -> p c k", c=2)
        mv = at(PV + 30 * KB + 320, 2 * NT).rearrange("p (t k) -> p t k", t=NT)
        rstd = at(PV + 30 * KB + 384, NT)
        R0 = PV + 8 * KB
        sS = at(R0, NT * NE).rearrange("p (t e) -> p t e", t=NT)
        selM = at(R0 + 1280, NT * NE).rearrange("p (t e) -> p t e", t=NT)
        sbt = at(R0 + 2560, NE)
        g88 = at(R0 + 2816, NE).rearrange("p (g k) -> p g k", g=8)
        gsum = at(R0 + 3072, 8)
        gtop = at(R0 + 3104, 8)
        grest = at(R0 + 3136, 8)
        gmask = at(R0 + 3328, 8)
        gadd = at(R0 + 3360, 8)
        msk = at(R0 + 3392, NE)
        e8 = at(R0 + 3648, 8)
        repl = at(R0 + 3680, NE)
        ggate = at(R0 + 3936, NE)
        gden = at(R0 + 4192, 4)
        incl = at(R0 + 4208, NE)
        tok8 = at(R0 + 4464, 8)
        shsig = [at(R0 + (5 + t) * KB, ED) for t in range(NT)]
        shact = [at(R0 + (15 + t) * KB, ED) for t in range(NT)]
        shaT = at(R0 + 10 * KB, 2 * NTOK).rearrange("p (k n) -> p k n", k=2)
        V4 = at(SMALL, NT * NE * 4).rearrange("p (t e k) -> p t e k", t=NT, e=NE)
        posm = at(SMALL + 5120, NT * NE).rearrange("p (t e) -> p t e", t=NT)
        UNROLL = 8
        meta = at(SMALL + 6400, UNROLL * 4).rearrange("p (s k) -> p s k", s=UNROLL)
        metai = meta.bitcast(U32)
        WSLOT = 24 * KB
        w13 = [at(LG + WSLOT * s, KT * 512).rearrange("p (k n) -> p k n", k=KT) for s in range(4)]
        w2 = [at(LG + WSLOT * s + 16 * KB, 2 * D).rearrange("p (k n) -> p k n", k=2) for s in range(4)]
        xg = [at(PV + (8 + 4 * s) * KB, D) for s in range(2)]
        xgT = [at(PV + (16 + 4 * s) * KB, D).rearrange("p (k n) -> p k n", k=KT) for s in range(2)]
        ye = [at(PV + 24 * KB, D), at(GATE + 12 * KB, D)]
        onehot = [at(GATE + 2560 * s, NT * P).rearrange("p (t n) -> p t n", t=NT) for s in range(2)]
        esig = [at(GATE + (5 + s) * KB, ED) for s in range(2)]
        eact = [at(GATE + (7 + s) * KB, ED) for s in range(2)]
        eactT = [at(GATE + (9 + s) * KB, 2 * P).rearrange("p (k n) -> p k n", k=2) for s in range(2)]
        longest = at(SMALL + 6560, 8, 1)
        blocks_f = at(SMALL + 6592, 8, 1)
        blocks_i = at(SMALL + 6628, 1, 1).bitcast(I32)
        wo1 = w13[3]
        yt = [at(LG + 32 * KB * s, TOPE * D).rearrange("p (j n) -> p j n", j=TOPE) for s in range(2)]
        g2, b2 = at(LG + 64 * KB, D), at(LG + 68 * KB, D)
        wpin = at(LG + 72 * KB, 2 * D).rearrange("p (k n) -> p k n", k=2)
        h2T = [at(PV + (8 + 4 * s) * KB, D).rearrange("p (k n) -> p k n", k=KT) for s in range(2)]
        pnat = at(LG + 85 * KB, NT * PLE).rearrange("p (t n) -> p t n", t=NT)
        peT = at(LG + 80 * KB, 2 * NTOK).rearrange("p (k n) -> p k n", k=2)
        sg = [at(GATE + 2 * KB * s, 512) for s in range(4)]
        pin = [at(where, D) for where in (PV, PV + 4 * KB, PV + 16 * KB, PV + 20 * KB, PV + 28 * KB)]
        wpg = at(RING, KT * D).rearrange("p (k n) -> p k n", k=KT)
        stat6b = at(GATE + 9 * KB, 12).rearrange("p (c k) -> p c k", c=2)
        mvb = at(GATE + 9 * KB + 64, 2 * NT).rearrange("p (t k) -> p t k", t=NT)
        rstdb = at(GATE + 9 * KB + 128, NT)

        ps = [ctx.enter_context(nc.psum_tensor(f"ps{i}", [P, 512], F32)) for i in range(8)]

        h_dram = nc.dram_tensor("h_rows", [NTOK, D], F32, kind="Internal").ap()
        y_dram = nc.dram_tensor("y_rows", [NTOK * TOPE, D], F32, kind="Internal").ap()

        xp = a["x_prompt"].rearrange("a (t p) n -> p (a t) n", p=P)
        xsm = a["x_sample"].rearrange("b t n -> (b t) n")
        w_in = a["w_in"][0].rearrange("(k p) n -> p k n", p=P)
        out_k_p = o["k_prompt"].rearrange("a b (t p) d -> p (a b t) d", p=P)
        out_v_p = o["v_prompt"].rearrange("a b (t p) d -> p (a b t) d", p=P)
        out_i_p = o["kidx_prompt"].rearrange("a b (t p) d -> p (a b t) d", p=P)
        out_k_s = o["k_sample"].rearrange("a b t d -> (a b t) d")
        out_v_s = o["v_sample"].rearrange("a b t d -> (a b t) d")
        out_i_s = o["kidx_sample"].rearrange("a b t d -> (a b t) d")

        def wide(w, rows, c0, c1):
            return a[w][0].rearrange("(k p) n -> p k n", p=P)[:, :, c0:c1]

        RING_ITEMS = [("wq", w_in[:, :, QC:QC + 512], ("q", NT - 1)), ("wkv", w_in[:, :, KVC:UC], ("kv", NT - 1)),
                      ("wu", w_in[:, :, UC:GAC], ("u", PG - 1, 1)),
                      ("wgb0", w_in[:, :, GBC:GBC + 512], ("gb", 0, NT - 1)),
                      ("wgb1", w_in[:, :, GBC + 512:GBC + 1024], ("gb", 1, NT - 1)),
                      ("wpo", wide("w_pool_out", 4, 0, D), ("pm", NT - 1, 1)),
                      ("wga0", w_in[:, :, GAC:GAC + 512], ("ga", 0, NT - 1)),
                      ("wga1", w_in[:, :, GAC + 512:GAC + 1024], ("ga", 1, NT - 1)),
                      ("wao", wide("w_att_out", 4, 0, D), ("m1", NT - 1, 1)),
                      ("wo0", wide("w_out", 8, 0, 512), ("wo", 0, NT - 1)),
                      ("sh13", wide("w_sh13", 8, 0, 512), ("s13", NT - 1)),
                      ("sh2", wide("w_sh2", 2, 0, D), ("s2", NT - 1, 1))]
        ring_no = {name: n for n, (name, _, _) in enumerate(RING_ITEMS)}

        def ring_view(name):
            n = ring_no[name]
            k, w = RING_ITEMS[n][1].shape[1:]
            return ring[n % 2][:, 0:k * w].rearrange("p (k n) -> p k n", k=k)

        bank_filled = {"act": sem("banks_filled_for_scalar"), "dve": sem("banks_filled_for_vector")}
        bank_read = {"act": sem("banks_read_by_scalar"), "dve": sem("banks_read_by_vector")}
        consts_in = sem("consts_in")
        rotary_in = sem("rotary_in")
        x_in = [sem(f"x_in{t}") for t in range(NT)]
        ring_in = [sem("ring_in0"), sem("ring_in1")]
        pages_in = sem("page_table_in")
        keys_by_sp = [sem(f"cached_keys_by_sp_in{s}") for s in range(KEY_SLOTS)]
        keys_by_pool = [sem(f"cached_keys_by_pool_in{s}") for s in range(KEY_SLOTS)]
        v_in = [sem("cached_values_in0"), sem("cached_values_in1")]
        rows_cleared = sem("rows_cleared")
        roped = sem("roped")
        rows_stored = [sem("rows_stored0"), sem("rows_stored1")]
        vnew_in = sem("new_values_in")
        step = sem("vector_step")
        pstep = sem("pool_step")
        comb_ready = sem("index_weights_ready")
        rel_used = sem("relu_rows_used")
        summed = sem("prompt_scores_summed")
        barred = sem("later_keys_barred")
        mask_s = sem("sample_mask_ready")
        aux_in = sem("pool_inputs_in")
        cleared = sem("pool_edges_cleared")
        ust_out = sem("pool_rows_stored")
        pooled = sem("pooled")
        mixed = sem("pool_branch_mixed")
        maxed = sem("row_max_ready")
        expd = sem("exp_done")
        pv_done = sem("pv_done")
        att_ready = sem("att_ready")
        wo1_in = sem("second_half_of_w_out_in")
        xr_in = sem("residual_in")
        ln_in = sem("layer_norm_weights_in")
        m_ready = sem("gated_sum_ready")
        var_ready = sem("variance_ready")
        rstd_ready = sem("rstd_ready")
        h_ready = sem("h_ready")
        h_stored = sem("h_stored")
        routed = sem("routed")
        shsig_ready = sem("shared_sigmoid_ready")
        sh_done = sem("shared_done")
        sha_ready = sem("shared_act_ready")

        ew_in = [sem(f"expert_weights_in{s}") for s in range(4)]
        oh_ready = sem("onehot_ready")
        list_ready = sem("list_ready")
        meta_ready = sem("meta_ready")
        xg_clear = sem("gather_buffers_cleared")
        gathered = [sem("gathered0"), sem("gathered1")]
        turned = sem("gathered_turned")
        xta = sem("turned_read_by_scalar")
        xtb = sem("turned_read_by_vector")
        up = sem("up_done")
        sig_ready = sem("sigmoid_ready")
        silu_done = sem("silu_done")
        act_ready = sem("act_ready")
        act_turned = sem("act_turned")
        actT_ready = sem("actT_ready")
        down = sem("down_done")
        ya = sem("y_half_by_scalar")
        yb = sem("y_half_by_vector")
        scattered = [sem("scattered0"), sem("scattered1")]

        passed_dve = sem("vector_passed_a_wait")
        passed_pool = sem("pool_passed_a_wait")

        ov_w = sem("further_weights_in")
        ov_v = sem("further_vector_steps")
        ov_p = sem("further_tensor_steps")
        ov_a = sem("further_scalar_steps")
        ov_g = sem("further_gathered")
        ov_s = sem("further_scattered")
        shifted = sem("further_block_shifted")
        ov_done = sem("further_rounds_done")

        y_in = [sem("choices_in0"), sem("choices_in1")]
        fin_in = sem("finish_inputs_in")
        norm2_in = sem("second_norm_weights_in")
        pin_saved = sem("ple_in_saved")
        pool_summed = sem("choices_summed_by_pool")
        pe_turned = sem("embeddings_turned")
        pe_read = sem("embeddings_read")
        y_summed = sem("choices_summed")
        var2 = sem("variance2_ready")
        rstd2 = sem("rstd2_ready")
        h2_ready = sem("h2_ready")
        h2_turned = sem("h2_turned")
        h2_read = sem("h2T_ready")
        gate_up = sem("ple_gate_up")
        pin_up = sem("ple_in_up")
        sg_ready = sem("ple_sigmoid_ready")
        mul_done = sem("ple_product_done")
        out_ready = sem("out_ready")
        stored = sem("outputs_stored")

        order = {"pe": [], "act": [], "dve": []}

        def filled(eng, key):
            who, n = number[key]
            eng.wait_ge(bank_filled[who], n)

        def read(eng, key):
            who, n = number[key]
            eng.wait_ge(bank_read[who], n)

        def claim(pe, key):
            order["pe"].append(key)
            if prev[key]:
                read(pe, prev[key])
            return ps[bank_of[key]]

        def take(eng, key):
            order[number[key][0]].append(key)
            filled(eng, key)
            return ps[bank_of[key]]

        def fills(ins, key):
            ins.then_inc(bank_filled[number[key][0]], 1)

        def frees(ins, key):
            ins.then_inc(bank_read[number[key][0]], 1)

        def weights(pe, name):
            n = ring_no[name]
            pe.wait_ge(ring_in[n % 2], 16 * (n // 2 + 1))
            return ring_view(name)

        def all_rows_stored(eng):
            eng.wait_ge(rows_stored[0], 16 * 3 * 3)
            eng.wait_ge(rows_stored[1], 16 * 3 * 2)

        def span(t):
            return slice(P * t, P * t + ROWS[t])

        V_STEPS, P_STEPS = 6, 5

        def further(eng, body, before=None):
            eng.wait_ge(ov_v, 1)
            extra = eng.value_load(blocks_i[0:1, 0:1], min_val=0, max_val=(NTOK - 1) // CAP)
            with eng.If(extra > 0):
                with eng.Fori(0, extra) as blk:
                    if before:
                        before(blk)
                    with eng.Fori(0, NE) as e:
                        body(blk * NE + e, e)
            return extra * NE

        def load_pages(eng, b, parts, done, first=0, last=NPG):
            with eng.Fori(first // 4, last // 4) as g4:
                page = [eng.value_load(pages[0:1, bass.ds(b * NPG + 4 * g4 + j, 1)], min_val=0, max_val=a["n_phys"] - 1) for j in range(4)]
                for j in range(4):
                    for table, dest in parts:
                        eng.dma_start(dest(4 * g4 + j), a[table][0][bass.ds(page[j], 1)].rearrange("a p d -> p (a d)")).then_inc(done, 16)

        def load_keys(eng, b, done, first, last):
            s = b % KEY_SLOTS
            if b >= KEY_SLOTS:
                filled(eng, ("kT", b - KEY_SLOTS, 3))
            load_pages(eng, b, (("cache_kidx", lambda g: knat[s][:, bass.ds(g, 1), 0:IDX][:, 0, :]),
                                ("cache_k", lambda g: knat[s][:, bass.ds(g, 1), IDX:][:, 0, :])), done[s], first, last)

        def load_values(eng, b):
            load_pages(eng, b, (("cache_v", lambda g: values[:, bass.ds(b * NPG + g, 1), :][:, 0, :]),), v_in[b % 2])

        block = ctx.enter_context(nc.Block())


        @block.sync
        def _(sp):
            sp.dma_start(cst, a["consts"]).then_inc(consts_in, 16)
            for t in range(4):
                sp.dma_start(xs[:, t, :], xp[:, t, :]).then_inc(x_in[t], 16)
            sp.dma_start(xs[0:NS, 4, :], xsm).then_inc(x_in[4], 16)

            def load_ring(name):
                n = ring_no[name]
                if n >= 2:
                    filled(sp, RING_ITEMS[n - 2][2])
                sp.dma_start(ring_view(name), RING_ITEMS[n][1]).then_inc(ring_in[n % 2], 16)

            load_ring("wq")
            load_ring("wkv")

            sp.wait_ge(pages_in, 16)
            for b in range(DB):
                load_keys(sp, b, keys_by_sp, POOL_PAGES, NPG)
                if b == 3:
                    load_ring("wu")
                    load_ring("wgb0")
            for name in ("wgb1", "wpo", "wga0", "wga1"):
                load_ring(name)
            for t in range(NT):
                filled(sp, ("pm", t, 1))
            sp.wait_ge(mixed, 2 * NT)
            for b in range(0, DB, 2):
                load_values(sp, b)
            load_ring("wao")
            load_ring("wo0")
            sp.wait_ge(pv_done, 4 + 4)
            for t in range(4):
                sp.dma_start(xr[:, t, :], xp[:, t, :]).then_inc(xr_in, 16)
            sp.dma_start(xr[0:NS, 4, :], xsm).then_inc(xr_in, 16)
            sp.dma_start(lng, a["ln1_g"].partition_broadcast(P)).then_inc(ln_in, 16)
            sp.dma_start(lnb, a["ln1_b"].partition_broadcast(P)).then_inc(ln_in, 16)
            sp.dma_start(wrout, a["w_router"][0].rearrange("(k p) e -> p k e", p=P)).then_inc(ln_in, 16)
            sp.dma_start(rbias, a["router_bias"].partition_broadcast(P)).then_inc(ln_in, 16)

            def load_expert(e, s, static):
                if not static:
                    sp.wait_ge(down, 2 * e - 6)
                sp.dma_start(w13[s], a["w_exp13"][0][bass.ds(e, 1)].rearrange("a (k p) n -> p (a k) n", p=P)).then_inc(ew_in[s], 16)
                sp.dma_start(w2[s], a["w_exp2"][0][bass.ds(e, 1)].rearrange("a (k p) n -> p (a k) n", p=P)).then_inc(ew_in[s], 16)

            read(sp, ("ost", 3))
            sp.dma_start(wo1, wide("w_out", 8, 512, D)).then_inc(wo1_in, 16)
            load_expert(0, 0, True)
            load_expert(1, 1, True)
            load_ring("sh13")
            sp.wait_ge(m_ready, NT)
            load_expert(2, 2, True)
            load_ring("sh2")
            read(sp, ("wo", 1, NT - 1))
            load_expert(3, 3, True)
            with sp.Fori(1, NE // 4) as q4:
                for s in range(4):
                    load_expert(4 * q4 + s, s, False)
            sp.wait_ge(sh_done, 1)
            sp.dma_start(wpg, a["w_ple_gate"][0].rearrange("(k p) n -> p k n", p=P)).then_inc(fin_in, 16)
            sp.wait_ge(down, 2 * NE)
            sp.dma_start(wpin, a["w_ple_in"][0].rearrange("(k p) n -> p k n", p=P)).then_inc(fin_in, 16)
            sp.dma_start(pnat[:, 0:4, :], a["p_prompt"].rearrange("a b (t p) n -> p (a b t) n", p=P)).then_inc(fin_in, 16)
            sp.dma_start(pnat[0:NS, 4, :], a["p_sample"].rearrange("a b t n -> (a b t) n")).then_inc(fin_in, 16)
            sp.dma_start(g2, a["ln2_g"].partition_broadcast(P)).then_inc(norm2_in, 16)
            sp.dma_start(b2, a["ln2_b"].partition_broadcast(P)).then_inc(norm2_in, 16)

            def further_weights(n, e):
                sp.wait_ge(ov_done, n + 1)
                sp.dma_start(w13[0], a["w_exp13"][0][bass.ds(e, 1)].rearrange("a (k p) n -> p (a k) n", p=P)).then_inc(ov_w, 16)
                sp.dma_start(w2[0], a["w_exp2"][0][bass.ds(e, 1)].rearrange("a (k p) n -> p (a k) n", p=P)).then_inc(ov_w, 16)

            rounds = further(sp, further_weights)
            sp.wait_ge(ov_done, rounds + 1)
            for i, t in enumerate(LAST_ORDER):
                if i >= 2:
                    sp.wait_ge(y_summed, i - 1)
                sp.dma_start(yt[i % 2][0:ROWS[t]], y_dram[TOPE * P * t:TOPE * (P * t + ROWS[t]), :].rearrange("(p j) n -> p j n", j=TOPE)).then_inc(y_in[i % 2], 16)
            yp = o["y_prompt"].rearrange("a (t p) n -> p (a t) n", p=P)
            ysm = o["y_sample"].rearrange("b t n -> (b t) n")
            for i, t in enumerate(LAST_ORDER):
                sp.wait_ge(out_ready, 2 * i + 2)
                sp.dma_start(yp[:, t, :] if t < 4 else ysm, m[0:ROWS[t], t, :]).then_inc(stored, 16)
            sp.wait_ge(stored, 16 * NT)
            all_rows_stored(sp)
            sp.wait_ge(ust_out, 48)

        @block.gpsimd
        def _(pool):
            count = [0]

            def link(ins):
                count[0] += 1
                ins.then_inc(pstep, 1)
                pool.wait_ge(pstep, count[0])

            pool.dma_start(rotary, a["rotary"].rearrange("(t p) c d -> p t c d", p=P)).then_inc(rotary_in, 16)
            pool.dma_start(pages, a["page_table"].rearrange("b g -> (b g)").unsqueeze(0)).then_inc(pages_in, 16)
            pool.dma_start(pscale, a["pool_scale"][0].rearrange("(g p) -> p g", p=P), allow_slow_non_contiguous=True).then_inc(aux_in, 16)
            for s in range(2):
                ins = nc.gpsimd.memset(rowsR[:, s, 4:8, 0:HD], 0.0)
            ins.then_inc(rows_cleared, 1)

            def some_keys(b):
                load_keys(pool, b, keys_by_pool, 0, POOL_PAGES)

            pool.wait_ge(pages_in, 16)
            some_keys(0)
            some_keys(1)
            for t in range(NT):
                if t in (2, 4):
                    some_keys(t // 2 + 1)
                pool.wait_ge(roped, t + 1)
                n, s = ROWS[t], t % 2
                pool.dma_start(out_k_p[:, t, :] if t < 4 else out_k_s, rowsR[0:n, s, 8, IDX:]).then_inc(rows_stored[s], 16)
                pool.dma_start(out_i_p[:, t, :] if t < 4 else out_i_s, rowsR[0:n, s, 8, 0:IDX]).then_inc(rows_stored[s], 16)
                pool.dma_start(out_v_p[:, t, :] if t < 4 else out_v_s, v_prompt[:, t, :] if t < 4 else v_samp).then_inc(rows_stored[s], 16)
            all_rows_stored(pool)
            pool.dma_start(v_new, o["v_sample"][0].rearrange("b t d -> t b d")).then_inc(vnew_in, 16)

            link(nc.gpsimd.memset(scoreP[0], 0.0))
            nc.gpsimd.affine_select(out=scoreP[0], in_=scoreP[0], compare_op=ALU.is_ge, fill=MASKED, base=0,
                                    pattern=[[-1, P]], channel_multiplier=1).then_inc(barred, 1)
            for t in range(1, 4):
                pool.wait_ge(summed, t)
                diag = scoreP[t][:, P * t:P * t + P]
                nc.gpsimd.affine_select(out=diag, in_=diag, compare_op=ALU.is_ge, fill=BARRED, base=0,
                                        pattern=[[-1, P]], channel_multiplier=1).then_inc(barred, 1)

            link(nc.gpsimd.memset(uext[:, :, 0:PST], 0.0))
            nc.gpsimd.memset(uext[:, :, PST + SEQ:528], 0.0).then_inc(cleared, 1)
            for b in range(4, DB):
                some_keys(b)

            filled(pool, ("kT", DB - 1, 3))
            pool.dma_start(wgrp, a["w_pool_grp"][0].rearrange("g c d -> c g d")).then_inc(aux_in, 16)
            filled(pool, ("sc", 1, 4))
            pool.dma_start(stnat, a["state_pool"][0].rearrange("b s n -> (b s) n")).then_inc(aux_in, 16)
            pool.dma_start(o["pool_sample"][0, :, 0:PST - DT, :], a["state_pool"][0, :, DT:PST, :]).then_inc(ust_out, 16)
            read(pool, ("uo", 1))
            pool.dma_start(o["pool_prompt"][0, 0], ust[0:PST, 0, :]).then_inc(ust_out, 16)
            pool.dma_start(o["pool_sample"][0, :, PST - DT:PST, :].rearrange("b t n -> b t n"), ust[0:NS, 1, :]).then_inc(ust_out, 16)

            pool.wait_ge(consts_in, 16)
            icount = const("icount").rearrange("p (g n) -> p g n", g=PG)
            for g in range(PG):
                if g >= 1:
                    pool.wait_ge(pooled, g)
                w = 2 ** (g + 1)
                src, srcs = uext[:, g, :], uexs[:, g, :, :]
                for lv in range(g + 1):
                    d = 2 ** lv
                    j0 = 2 ** (lv + 1) - 1
                    nc.gpsimd.tensor_tensor(win[lv % 2][:, j0:527], src[:, j0:527], src[:, j0 - d:527 - d], ALU.add)
                    link(nc.gpsimd.tensor_tensor(wins[lv % 2][:, :, j0:23], srcs[:, :, j0:23], srcs[:, :, j0 - d:23 - d], ALU.add))
                    src, srcs = win[lv % 2], wins[lv % 2]
                u = uext[:, g, :]
                nc.gpsimd.tensor_scalar(src[:, 31:527], src[:, 31:527], 1.0 / w, None, ALU.mult)
                nc.gpsimd.tensor_scalar(srcs[:, :, 15:23], srcs[:, :, 15:23], 1.0 / w, None, ALU.mult)
                link(nc.gpsimd.tensor_tensor(src[:, 15:31], src[:, 15:31], icount[:, g, :], ALU.mult))
                link(nc.gpsimd.tensor_tensor(u[:, 15:527], src[:, 15:527], u[:, 15:527], ALU.subtract))
                us = uexs[:, g, :, 15:23]
                nc.gpsimd.tensor_tensor(us, srcs[:, :, 15:23], us, ALU.subtract).then_inc(pooled, 1)
            for n, (t, c) in enumerate([(t, c) for t in range(NT) for c in range(2)]):
                read(pool, ("pm", t, c))
                r = ROWS[t]
                nc.gpsimd.tensor_tensor(m[0:r, t, 512 * c:512 * c + 512], m[0:r, t, 512 * c:512 * c + 512], pmt[n % 2][0:r, :], ALU.mult).then_inc(mixed, 1)

            pool.wait_ge(mixed, 2 * NT)
            for b in range(1, DB, 2):
                load_values(pool, b)

            def store_h(t):
                pool.wait_ge(h_ready, t + 1)
                pool.dma_start(h_dram[P * t:P * t + ROWS[t], :], m[0:ROWS[t], t, :]).then_inc(h_stored, 16)

            for t in range(NT):
                r = ROWS[t]
                pool.wait_ge(var_ready, t + 1)
                nc.gpsimd.tensor_tensor(rstd[0:r, t:t + 1], mv[0:r, t, 1:2], const("mhalf", r), ALU.pow).then_inc(rstd_ready, 1)
                if t >= 1:
                    store_h(t - 1)
            store_h(NT - 1)

            pool.wait_ge(h_stored, 16 * NT)
            pool.wait_ge(sh_done, 1)
            for s in range(2):
                ins = nc.gpsimd.memset(xg[s], 0.0)
            ins.then_inc(xg_clear, 1)
            pool.wait_ge(xg_clear, 1)

            last_row, last_choice = pool.to_reg(NTOK - 1), pool.to_reg(NTOK * TOPE - 1)

            def gather(e, k):
                pool.wait_ge(meta_ready, e + 1)
                if not (isinstance(e, int) and e < 2):
                    pool.wait_ge(turned, 2 * e - 2)
                pool.sem_inc(passed_pool, 1)
                pool.indirect_dma_start(out=xg[k % 2], out_offset=None, in_=h_dram,
                                        in_offset=bass.IndirectOffsetOnAxis(ap=metai[:, k, 0:1], axis=0),
                                        bounds_check=last_row, oob_is_err=False).then_inc(gathered[k % 2], 16)

            def scatter(e, k):
                pool.wait_ge(ya, e + 1)
                pool.wait_ge(yb, e + 1)
                pool.sem_inc(passed_pool, 1)
                pool.indirect_dma_start(out=y_dram, out_offset=bass.IndirectOffsetOnAxis(ap=metai[:, k, 1:2], axis=0),
                                        in_=ye[k % 2], in_offset=None,
                                        bounds_check=last_choice, oob_is_err=False).then_inc(scattered[k % 2], 16)

            def expert(i, k, first=False, last=False):
                if not (last and k >= UNROLL - 2):
                    gather(i + 2, (k + 2) % UNROLL)
                if not (first and k == 0):
                    scatter(i - 1, (k - 1) % UNROLL)

            gather(0, 0)
            gather(1, 1)
            for k in range(UNROLL):
                expert(k, k, first=True)
            with pool.Fori(1, NE // UNROLL - 1) as q:
                for k in range(UNROLL):
                    expert(UNROLL * q + k, k)
            for k in range(UNROLL):
                expert(NE - UNROLL + k, k, last=True)
            scatter(NE - 1, UNROLL - 1)
            for s in range(2):
                pool.wait_ge(scattered[s], 16 * NE // 2)
            pool.sem_inc(ov_done, 1)

            def further_rows(n, e):
                pool.wait_ge(ov_v, V_STEPS * n + 3)
                pool.sem_inc(passed_pool, 1)
                pool.indirect_dma_start(out=xg[0], out_offset=None, in_=h_dram,
                                        in_offset=bass.IndirectOffsetOnAxis(ap=metai[:, 0, 0:1], axis=0),
                                        bounds_check=last_row, oob_is_err=False).then_inc(ov_g, 16)
                pool.wait_ge(ov_v, V_STEPS * n + 7)
                pool.sem_inc(passed_pool, 1)
                pool.indirect_dma_start(out=y_dram, out_offset=bass.IndirectOffsetOnAxis(ap=metai[:, 0, 1:2], axis=0),
                                        in_=ye[0], in_offset=None,
                                        bounds_check=last_choice, oob_is_err=False).then_inc(ov_s, 16)
                pool.wait_ge(ov_s, 16 * n + 16)
                pool.sem_inc(ov_done, 1)

            further(pool, further_rows)

            def choices(i):
                r = ROWS[LAST_ORDER[i]]
                pool.wait_ge(y_in[i % 2], 16 * (i // 2 + 1))
                link(nc.gpsimd.tensor_tensor(yt[i % 2][0:r, 5, :], yt[i % 2][0:r, 5, :], yt[i % 2][0:r, 6, :], ALU.add))
                nc.gpsimd.tensor_tensor(yt[i % 2][0:r, 5, :], yt[i % 2][0:r, 5, :], yt[i % 2][0:r, 7, :], ALU.add).then_inc(pool_summed, 1)

            def add_gated(i):
                t = LAST_ORDER[i]
                r = ROWS[t]
                for c in range(2):
                    n = 2 * i + c
                    cs = slice(512 * c, 512 * c + 512)
                    pool.wait_ge(mul_done, n + 1)
                    nc.gpsimd.tensor_tensor(m[0:r, t, cs], m[0:r, t, cs], sg[n % 4][0:r, :], ALU.add).then_inc(out_ready, 1)

            choices(0)
            for i, t in enumerate(LAST_ORDER):
                r = ROWS[t]
                pool.wait_ge(var2, i + 1)
                nc.gpsimd.tensor_tensor(rstdb[0:r, t:t + 1], mvb[0:r, t, 1:2], const("mhalf", r), ALU.pow).then_inc(rstd2, 1)
                if i + 1 < NT:
                    choices(i + 1)
                if i >= 1:
                    add_gated(i - 1)
            add_gated(NT - 1)

        @block.scalar
        def _(act):
            def copy(out, in_, scale=1.0):
                return nc.scalar.activation(out, in_, ACT.Copy, scale=scale)

            for t in range(NT):
                b = take(act, ("xT", t, 0))
                frees(copy(xT[:, 0:4, span(t)], b[:, :].rearrange("p (k n) -> p k n", k=4)[:, :, 0:ROWS[t]]), ("xT", t, 0))
            for t in range(NT):
                n = ROWS[t]
                for i in range(2):
                    b = take(act, ("rt", t, i))
                    heads4 = b[:, :].rearrange("p (k n) -> p k n", k=4)[:, :, 0:n]
                    if t < 4:
                        ins = copy(qT[:, 4 * i:4 * i + 4, span(t)], heads4)
                    else:
                        ins = copy(qTs[:, :, 4 * i:4 * i + 4, :].rearrange("p b h t -> p h b t"),
                                   heads4.rearrange("p h (b t) -> p h b t", b=DB))
                    frees(ins, ("rt", t, i))
                b = take(act, ("rt", t, 2))
                frees(copy(kk_prompt[:, span(t)] if t < 4 else kk_new, b[:, 0:n]), ("rt", t, 2))
            c_idx = IDX ** -0.5 * IH ** -0.5
            for n, (t, h) in enumerate([(t, h) for t in range(1, 4) for h in range(IH)]):
                b = take(act, ("dot", t, h))
                if n == 0:
                    act.wait_ge(roped, NT)
                if n >= 4:
                    act.wait_ge(rel_used, n - 3)
                frees(nc.scalar.activation(relP[n % 4][:, 0:KEYS[t]], b[:, 0:KEYS[t]], ACT.Relu, scale=c_idx), ("dot", t, h))

            def keysT(b):
                for i in (1, 3):
                    bk = take(act, ("kT", b, i))
                    frees(copy(kkT[b % 2][:, 512 * i:512 * i + 512], bk[:, :]), ("kT", b, i))

            act.wait_ge(rel_used, 12)
            keysT(0)
            for b in range(DB):
                if b + 1 < DB:
                    keysT(b + 1)
                if b == 4:
                    filled(act, ("sc", 0, 4))
                q = 32 * (b % 4)
                for c in range(5):
                    bk = take(act, ("sd", b, c))
                    w = 512 if c < 4 else DT
                    frees(nc.scalar.activation(relS[q:q + 32, 512 * c:512 * c + w], bk[q:q + 32, 0:w], ACT.Relu, scale=c_idx), ("sd", b, c))
                if 1 <= b <= PG:
                    g = b - 1
                    if g == 0:
                        all_rows_stored(act)
                        act.wait_ge(cleared, 1)
                    bk = take(act, ("u", g, 0))
                    frees(copy(uext[:, g, PST:PST + SEQ], bk[:, :]), ("u", g, 0))
                    bk = take(act, ("u", g, 1))
                    copy(uflat[:, g, :], bk[:, 0:NS])
                    frees(copy(uexs[:, g, :, PST:], bk[:, 0:NS].rearrange("p (b n) -> p b n", b=DB)), ("u", g, 1))

            bk = take(act, ("st",))
            frees(copy(uexs[:, :, :, 0:PST], bk[:, 0:480].rearrange("p (g b n) -> p g b n", g=PG, b=DB)), ("st",))
            bk = take(act, ("uo", 0))
            ins = copy(ust[0:PST, 0, :], bk[0:PST, :])
            frees(ins, ("uo", 0))
            bk = take(act, ("uo", 1))
            frees(copy(ust[0:NS, 1, :], bk[0:NS, :]), ("uo", 1))
            for c in range(2):
                for t in range(NT):
                    r = ROWS[t]
                    bk = take(act, ("gb", c, t))
                    frees(nc.scalar.activation(m[0:r, t, 512 * c:512 * c + 512], bk[0:r, :], ACT.Sigmoid), ("gb", c, t))
            act.wait_ge(aux_in, 48)
            for g in range(PG):
                bk = take(act, ("pp", g, 0))
                frees(copy(poolT[:, g, 0:SEQ], bk[:, :], scale=pscale[:, g:g + 1]), ("pp", g, 0))
                bk = take(act, ("pp", g, 1))
                frees(copy(poolT[:, g, SEQ:], bk[:, 0:NS], scale=pscale[:, g:g + 1]), ("pp", g, 1))
            for n, (t, c) in enumerate([(t, c) for t in range(NT) for c in range(2)]):
                bk = take(act, ("pm", t, c))
                if n >= 2:
                    act.wait_ge(mixed, n - 1)
                frees(copy(pmt[n % 2][0:ROWS[t], :], bk[0:ROWS[t], :]), ("pm", t, c))
            for c in range(2):
                for t in range(NT):
                    r = ROWS[t]
                    bk = take(act, ("ga", c, t))
                    frees(nc.scalar.activation(sga[0:r, t, 512 * c:512 * c + 512], bk[0:r, :], ACT.Sigmoid), ("ga", c, t))

            heads = [(t, h) for t in range(4) for h in range(H)]

            def exp_p(n):
                t, h = heads[n]
                act.wait_ge(maxed, n + 1)
                col = 8 * (t % 2) + h
                nc.scalar.activation(probs[n % 3][:, 0:KEYS[t]], probs[n % 3][:, 0:KEYS[t]], ACT.Exp,
                                     bias=nmax[:, col:col + 1], accum_out=esum[:, col:col + 1]).then_inc(expd, 1)

            def att_copy(t):
                bk = take(act, ("at", t))
                frees(copy(attnT[:, :, span(t)], bk[:, :].rearrange("p (k n) -> p k n", k=4)), ("at", t))

            exp_p(0)
            exp_p(1)
            for n, (t, h) in enumerate(heads):
                if n + 2 < len(heads):
                    exp_p(n + 2)
                if n + 1 < len(heads) and n % 2 == 0:
                    t1, h1 = heads[n + 1]
                    bk = take(act, ("pt", t1, h1))
                    frees(copy(probsT[(n + 1) % 2][:, 0:KEYS[t1]], bk[:, 0:KEYS[t1]]), ("pt", t1, h1))
                if h == 0 and t > 0:
                    att_copy(t - 1)
            att_copy(3)
            for p in range(4):
                act.wait_ge(maxed, 32 + p + 1)
                nc.scalar.activation(logit[:, p, :], logit[:, p, :], ACT.Exp, bias=nmax[:, p:p + 1],
                                     accum_out=esum[:, p:p + 1]).then_inc(expd, 1)
                for i in (1, 3):
                    bk = take(act, ("ps", p, i))
                    frees(copy(probsTS[p % 2][:, 4 * i:4 * i + 4, :], bk[:, :].rearrange("p (k n) -> p k n", k=4)), ("ps", p, i))
            for t in range(NT):
                r = ROWS[t]
                bk = take(act, ("mT", t, 0))
                frees(copy(mT[:, 0:4, span(t)], bk[:, :].rearrange("p (k n) -> p k n", k=4)[:, :, 0:r]), ("mT", t, 0))
            for t in range(NT):
                r = ROWS[t]
                for i in range(2):
                    bk = take(act, ("hT", t, i))
                    frees(copy(hT[:, 4 * i:4 * i + 4, span(t)], bk[:, :].rearrange("p (k n) -> p k n", k=4)[:, :, 0:r]), ("hT", t, i))
            for t in range(NT):
                r = ROWS[t]
                bk = take(act, ("r", t))
                if t == 0:
                    read(act, ("wo", 1, NT - 1))
                frees(nc.scalar.activation(sS[0:r, t, :], bk[0:r, 0:NE], ACT.Sigmoid), ("r", t))
            for t in range(NT):
                r = ROWS[t]
                filled(act, ("s13", t))
                nc.scalar.activation(shsig[t][0:r, :], ps[bank_of[("s13", t)]][0:r, 0:ED], ACT.Sigmoid).then_inc(shsig_ready, 1)
            for t in range(NT):
                r = ROWS[t]
                bk = take(act, ("s13T", t))
                frees(copy(shaT[:, :, span(t)], bk[:, 0:256].rearrange("p (k n) -> p k n", k=2)[:, :, 0:r]), ("s13T", t))

            def xgT_half(e, k):
                act.wait_ge(turned, 2 * e + 1)
                copy(xgT[k % 2][:, 0:4, :], ps[4][:, :].rearrange("p (k n) -> p k n", k=4)).then_inc(xta, 1)

            def y_half(e, k):
                act.wait_ge(down, 2 * e + 1)
                if not (isinstance(e, int) and e < 2):
                    act.wait_ge(scattered[k % 2], 8 * e - 8 * (k % 2))
                copy(ye[k % 2][:, 0:512], ps[2][:, :], scale=meta[:, k, 2:3]).then_inc(ya, 1)

            def expert(i, k, first=False, last=False):
                act.wait_ge(up, i + 1)
                if not (first and k < 2):
                    act.wait_ge(act_ready, i - 1)
                nc.scalar.activation(esig[k % 2], ps[k % 2][:, 0:ED], ACT.Sigmoid).then_inc(sig_ready, 1)
                if not (last and k == UNROLL - 1):
                    xgT_half(i + 1, (k + 1) % UNROLL)
                if not (first and k == 0):
                    y_half(i - 1, (k - 1) % UNROLL)
                act.wait_ge(act_turned, i + 1)
                copy(eactT[k % 2], ps[7][:, 0:256].rearrange("p (k n) -> p k n", k=2)).then_inc(actT_ready, 1)

            act.wait_ge(sh_done, 1)
            xgT_half(0, 0)
            for k in range(UNROLL):
                expert(k, k, first=True)
            with act.Fori(1, NE // UNROLL - 1) as q:
                for k in range(UNROLL):
                    expert(UNROLL * q + k, k)
            for k in range(UNROLL):
                expert(NE - UNROLL + k, k, last=True)
            y_half(NE - 1, UNROLL - 1)

            def further_sigmoid(n, e):
                act.wait_ge(ov_p, P_STEPS * n + 3)
                nc.scalar.activation(esig[0], ps[0][:, 0:ED], ACT.Sigmoid).then_inc(ov_a, 1)

            further(act, further_sigmoid)

            for t in range(NT):
                r = ROWS[t]
                act.wait_ge(pe_turned, t + 1)
                copy(peT[:, :, span(t)], ps[6][:, 0:256].rearrange("p (k n) -> p k n", k=2)[:, :, 0:r]).then_inc(pe_read, 1)
            for t in range(NT):
                r = ROWS[t]
                for c in range(2):
                    act.wait_ge(pin_up, 2 * t + c + 1)
                    copy(pin[t][0:r, 512 * c:512 * c + 512], ps[2 + c][0:r, :]).then_inc(pin_saved, 1)
            for q, t in enumerate(LAST_ORDER):
                r = ROWS[t]
                for i in range(2):
                    act.wait_ge(h2_turned, 2 * q + i + 1)
                    copy(h2T[q % 2][:, 4 * i:4 * i + 4, 0:r], ps[4 + i][:, :].rearrange("p (k n) -> p k n", k=4)[:, :, 0:r]).then_inc(h2_read, 1)
                for c in range(2):
                    n = 2 * q + c
                    act.wait_ge(gate_up, n + 1)
                    if n >= 4:
                        act.wait_ge(out_ready, n - 3)
                    nc.scalar.activation(sg[n % 4][0:r, :], ps[n % 4][0:r, :], ACT.Sigmoid).then_inc(sg_ready, 1)

        @block.tensor
        def _(pe):
            mm = nc.tensor.matmul

            def turn4(key, srcs, rows, cols=P):
                b = claim(pe, key)
                for j, src in enumerate(srcs):
                    ins = nc.tensor.transpose(b[0:cols, P * j:P * j + rows], src, ident[0:rows, 0:rows])
                fills(ins, key)

            pe.wait_ge(consts_in, 16)
            for t in range(NT):
                pe.wait_ge(x_in[t], 16)
                for i in range(2):
                    turn4(("xT", t, i), [xs[0:ROWS[t], t, P * k:P * k + P] for k in range(4 * i, 4 * i + 4)], ROWS[t])

            def project(key, t, w, width):
                b = claim(pe, key)
                for k in range(KT):
                    ins = mm(b[0:ROWS[t], 0:width], xT[:, k, span(t)], w[:, k, 0:width], start=(k == 0), stop=(k == KT - 1))
                fills(ins, key)

            def qkv(t):
                read(pe, ("xT", t, 0))
                read(pe, ("xT", t, 1))
                project(("q", t), t, weights(pe, "wq"), 512)
                project(("kv", t), t, weights(pe, "wkv"), KVW)

            def rt(t):
                pe.wait_ge(roped, t + 1)
                s, n = t % 2, ROWS[t]
                turn4(("rt", t, 0), [rowsR[0:n, s, j, :] for j in range(4)], n)
                turn4(("rt", t, 1), [rowsR[0:n, s, j, :] for j in range(4, 8)], n)
                turn4(("rt", t, 2), [rowsR[0:n, s, 8, :]], n)

            qkv(0)
            for t in range(1, NT):
                qkv(t)
                rt(t - 1)
            rt(NT - 1)
            sel = const("sel", NS).rearrange("p (g q) -> p g q", g=2)
            b = claim(pe, ("wsel",))
            for g in range(2):
                ins = mm(b[:, 4 * g:4 * g + 4], sel[:, g, :], wi[0:NS, 4, :], start=True, stop=True)
            fills(ins, ("wsel",))
            for t in range(1, 4):
                for h in range(IH):
                    if h == 0 and t == 1:
                        read(pe, ("rt", NT - 1, 2))
                    b = claim(pe, ("dot", t, h))
                    fills(mm(b[:, 0:KEYS[t]], qT[0:IDX, h, span(t)], kk_prompt[0:IDX, 0:KEYS[t]], start=True, stop=True), ("dot", t, h))

            def keysT(b):
                s = b % KEY_SLOTS
                pe.wait_ge(keys_by_sp[s], 32 * (NPG - POOL_PAGES) * (b // KEY_SLOTS + 1))
                pe.wait_ge(keys_by_pool[s], 32 * POOL_PAGES * (b // KEY_SLOTS + 1))
                for i in range(4):
                    turn4(("kT", b, i), [knat[s][:, 4 * i + j, :] for j in range(4)], P)

            keysT(0)
            for b in range(DB):
                if b + 1 < DB:
                    keysT(b + 1)
                q, o2 = 32 * (b % 4), 64 * (b % 2)
                for c in range(5):
                    key = ("sd", b, c)
                    bk = claim(pe, key)
                    if c < 4:
                        read(pe, ("kT", b, c))
                        keys, w = kkT[b % 2][:, 512 * c:512 * c + 512], 512
                    else:
                        keys, w = kk_new[:, DT * b:DT * b + DT], DT
                    fills(mm(bk[q:q + 32, 0:w], qTs[0:IDX, b, 0:IH, :].rearrange("p h t -> p (h t)"), keys[0:IDX, :], start=True, stop=True), key)
                    key = ("sl", b, c)
                    bk = claim(pe, key)
                    fills(mm(bk[o2:o2 + 64, 0:w], qTs[IDX:, b, :, :].rearrange("p h t -> p (h t)"), keys[IDX:, :], start=True, stop=True), key)
                if b % 4 == 3:
                    g = b // 4
                    pe.wait_ge(comb_ready, 1)
                    for c in range(5):
                        key = ("sc", g, c)
                        w = 512 if c < 4 else DT
                        bk = claim(pe, key)
                        read(pe, ("sd", b, c))
                        fills(mm(bk[32 * g:32 * g + 32, 0:w], w_comb[:, g, :], relS[:, 512 * c:512 * c + w], start=True, stop=True), key)
                if 1 <= b <= PG:
                    g = b - 1
                    w = weights(pe, "wu")
                    for i, (c0, c1) in enumerate(((0, SEQ), (SEQ, NTOK))):
                        key = ("u", g, i)
                        bk = claim(pe, key)
                        for k in range(KT):
                            ins = mm(bk[:, 0:c1 - c0], w[:, k, P * g:P * g + P], xT[:, k, c0:c1], start=(k == 0), stop=(k == KT - 1))
                        fills(ins, key)

            pe.wait_ge(aux_in, 48)
            key = ("st",)
            b = claim(pe, key)
            for g in range(PG):
                ins = nc.tensor.transpose(b[:, 120 * g:120 * g + 120], stnat[:, P * g:P * g + P], ident[0:120, 0:120])
            fills(ins, key)
            key = ("uo", 0)
            read(pe, ("u", PG - 1, 1))
            b = claim(pe, key)
            for g in range(PG):
                ins = nc.tensor.transpose(b[0:PST, P * g:P * g + P], uext[:, g, SEQ:SEQ + PST], ident)
            fills(ins, key)
            key = ("uo", 1)
            b = claim(pe, key)
            for g in range(PG):
                ins = nc.tensor.transpose(b[0:NS, P * g:P * g + P], uflat[:, g, :], ident)
            fills(ins, key)
            for c in range(2):
                w = weights(pe, f"wgb{c}")
                for t in range(NT):
                    project(("gb", c, t), t, w, 512)
            for g in range(PG):
                pe.wait_ge(pooled, g + 1)
                key = ("pp", g, 0)
                b = claim(pe, key)
                fills(mm(b[:, :], wgrp[:, g, :], uext[:, g, PST:PST + SEQ], start=True, stop=True), key)
                key = ("pp", g, 1)
                b = claim(pe, key)
                fills(mm(b[:, 0:NS], wgrp[:, g, :], uexs[:, g, :, PST:], start=True, stop=True), key)
            w = weights(pe, "wpo")
            read(pe, ("pp", PG - 1, 1))
            for t in range(NT):
                for c in range(2):
                    key = ("pm", t, c)
                    b = claim(pe, key)
                    for g in range(PG):
                        ins = mm(b[0:ROWS[t], :], poolT[:, g, span(t)], w[:, g, 512 * c:512 * c + 512], start=(g == 0), stop=(g == PG - 1))
                    fills(ins, key)
            for c in range(2):
                w = weights(pe, f"wga{c}")
                for t in range(NT):
                    project(("ga", c, t), t, w, 512)

            heads = [(t, h) for t in range(4) for h in range(H)]

            def logits(n):
                t, h = heads[n]
                key = ("l", t, h)
                b = claim(pe, key)
                fills(mm(b[:, 0:KEYS[t]], qT[IDX:, h, span(t)], kk_prompt[IDX:, 0:KEYS[t]], start=True, stop=True), key)

            def turn_probs(n):
                t, h = heads[n]
                pe.wait_ge(expd, n + 1)
                turn4(("pt", t, h), [probs[n % 3][:, P * j:P * j + P] for j in range(t + 1)], P)

            def turn_att(t):
                pe.wait_ge(att_ready, t + 1)
                turn4(("at", t), [att[:, P * k:P * k + P] for k in range(4)], P)

            for n in range(3):
                logits(n)
            turn_probs(0)
            for n, (t, h) in enumerate(heads):
                if n + 3 < len(heads):
                    logits(n + 3)
                if n + 1 < len(heads):
                    turn_probs(n + 1)
                if h == 0 and t > 0:
                    turn_att(t - 1)
                read(pe, ("pt", t, h))
                if h == 0 and t >= 2:
                    pe.wait_ge(att_ready, t - 1)
                for j in range(t + 1):
                    ins = mm(ps[6 + t % 2][:, HD * h:HD * h + HD], probsT[n % 2][:, P * j:P * j + P], v_prompt[:, j, :],
                             start=(j == 0), stop=(j == t))
                if h == H - 1:
                    ins.then_inc(pv_done, 1)
            turn_att(3)

            def bias(p):
                for c in range(5):
                    key = ("bs", p, c)
                    w = 512 if c < 4 else DT
                    b = claim(pe, key)
                    fills(mm(b[:, 0:w], rep_b[:, p, :], maskS[c][:, 0:w], start=True, stop=True), key)

            pe.wait_ge(mask_s, 1)
            bias(0)
            for q in range(2):
                pe.wait_ge(v_in[q], 16 * NPG * DB // 2)
            pe.wait_ge(vnew_in, 16)
            for p in range(4):
                if p < 3:
                    bias(p + 1)
                pe.wait_ge(expd, 32 + p + 1)
                for i in range(4):
                    turn4(("ps", p, i), [logit[:, p, P * (4 * i + j):P * (4 * i + j) + P] for j in range(4)], P)
                turn4(("ps", p, 4), [logit[:, p, PAST:SK]], P, DT)
                for i in range(5):
                    read(pe, ("ps", p, i))
                pv = ps[6 + p % 2]
                if p >= 2:
                    pe.wait_ge(att_ready, 4 + p - 1)
                for b2 in range(2):
                    o2 = 64 * b2
                    for g in range(NPG):
                        mm(pv[o2:o2 + 64, 0:HD], probsTS[p % 2][:, g, o2:o2 + 64], values[:, (2 * p + b2) * NPG + g, :], start=(g == 0), stop=False)
                    ins = mm(pv[o2:o2 + 64, 0:HD], probsTS[p % 2][0:DT, NPG, o2:o2 + 64], v_new[:, 2 * p + b2, :], start=False, stop=True)
                ins.then_inc(pv_done, 1)
                pe.wait_ge(att_ready, 4 + p + 1)
                turn4(("ost", p), [attS], P, HD)

            w = weights(pe, "wao")
            read(pe, ("at", 3))
            read(pe, ("ost", 3))
            for t in range(NT):
                for c in range(2):
                    key = ("m1", t, c)
                    b = claim(pe, key)
                    for k in range(4):
                        ins = mm(b[0:ROWS[t], :], attnT[:, k, span(t)], w[:, k, 512 * c:512 * c + 512], start=(k == 0), stop=(k == 3))
                    fills(ins, key)
            for t in range(NT):
                pe.wait_ge(m_ready, NT)
                for i in range(2):
                    turn4(("mT", t, i), [m[0:ROWS[t], t, P * k:P * k + P] for k in range(4 * i, 4 * i + 4)], ROWS[t])

            def by_tiles(tag, name, src, width):
                w = weights(pe, name)
                for t in range(NT):
                    b = claim(pe, tag + (t,))
                    for k in range(KT):
                        ins = mm(b[0:ROWS[t], 0:width], src[:, k, span(t)], w[:, k, 0:width], start=(k == 0), stop=(k == KT - 1))
                    fills(ins, tag + (t,))

            read(pe, ("mT", NT - 1, 0))
            read(pe, ("mT", NT - 1, 1))
            pe.wait_ge(wo1_in, 16)
            w = [weights(pe, "wo0"), wo1]
            for t in range(NT):
                for c in range(2):
                    b = claim(pe, ("wo", c, t))
                    for k in range(KT):
                        ins = mm(b[0:ROWS[t], :], mT[:, k, span(t)], w[c][:, k, :], start=(k == 0), stop=(k == KT - 1))
                    fills(ins, ("wo", c, t))
            for t in range(NT):
                pe.wait_ge(h_ready, t + 1)
                for i in range(2):
                    turn4(("hT", t, i), [m[0:ROWS[t], t, P * k:P * k + P] for k in range(4 * i, 4 * i + 4)], ROWS[t])
            pe.wait_ge(ln_in, 64)
            for t in range(NT):
                read(pe, ("hT", t, 1))
                key = ("r", t)
                b = claim(pe, key)
                for k in range(KT):
                    ins = mm(b[0:ROWS[t], 0:NE], hT[:, k, span(t)], wrout[:, k, :], start=(k == 0), stop=(k == KT - 1))
                fills(ins, key)
            by_tiles(("s13",), "sh13", hT, 512)
            for t in range(NT):
                key = ("rank", t)
                pe.wait_ge(routed, t + 1)
                b = claim(pe, key)
                r = ROWS[t]
                for u in range(t):
                    mm(b[0:r, 0:NE], const("ones")[:, 0:r], selM[:, u, :], start=(u == 0), stop=False)
                fills(mm(b[0:r, 0:NE], const("upper", r)[:, 0:r], selM[0:r, t, :], start=(t == 0), stop=True), key)
            b = claim(pe, ("count",))
            for t in range(NT):
                ins = mm(b[0:1, 0:NE], const("ones", ROWS[t])[:, 0:1], selM[0:ROWS[t], t, :], start=(t == 0), stop=(t == NT - 1))
            fills(ins, ("count",))
            for t in range(NT):
                pe.wait_ge(sha_ready, t + 1)
                turn4(("s13T", t), [shact[t][0:ROWS[t], P * k:P * k + P] for k in range(2)], ROWS[t])
            w = weights(pe, "sh2")
            for t in range(NT):
                read(pe, ("s13T", t))
                for c in range(2):
                    key = ("s2", t, c)
                    b = claim(pe, key)
                    for k in range(2):
                        ins = mm(b[0:ROWS[t], :], shaT[:, k, span(t)], w[:, k, 512 * c:512 * c + 512], start=(k == 0), stop=(k == 1))
                    fills(ins, key)

            def make_list(e, k):
                pe.wait_ge(oh_ready, e + 1)
                if not (isinstance(e, int) and e < 1):
                    pe.wait_ge(meta_ready, e)
                for t in range(NT):
                    r = ROWS[t]
                    ins = mm(ps[6][:, 0:4], onehot[k % 2][0:r, t, :], V4[0:r, t, bass.ds(e, 1), :][:, 0, :], start=(t == 0), stop=(t == NT - 1))
                ins.then_inc(list_ready, 1)

            def turn_x(e, k):
                pe.wait_ge(gathered[k % 2], 8 * e + 16 - 8 * (k % 2))
                if not (isinstance(e, int) and e < 1):
                    pe.wait_ge(xta, e)
                    pe.wait_ge(xtb, e)
                for i in range(2):
                    for j in range(4):
                        kk = 4 * i + j
                        ins = nc.tensor.transpose(ps[4 + i][:, P * j:P * j + P], xg[k % 2][:, P * kk:P * kk + P], ident)
                    ins.then_inc(turned, 1)

            def up_x(e, k):
                pe.wait_ge(ew_in[k % 4], 8 * (e - k % 4) + 32)
                pe.wait_ge(xta, e + 1)
                pe.wait_ge(xtb, e + 1)
                if not (isinstance(e, int) and e < 2):
                    pe.wait_ge(act_ready, e - 1)
                for kk in range(KT):
                    ins = mm(ps[k % 2][:, :], xgT[k % 2][:, kk, :], w13[k % 4][:, kk, :], start=(kk == 0), stop=(kk == KT - 1))
                ins.then_inc(up, 1)

            def down_x(e, k):
                pe.wait_ge(actT_ready, e + 1)
                if not (isinstance(e, int) and e < 1):
                    pe.wait_ge(ya, e)
                    pe.wait_ge(yb, e)
                for c in range(2):
                    for kk in range(2):
                        ins = mm(ps[2 + c][:, :], eactT[k % 2][:, kk, :], w2[k % 4][:, kk, 512 * c:512 * c + 512], start=(kk == 0), stop=(kk == 1))
                    ins.then_inc(down, 1)

            def turn_act(e, k):
                pe.wait_ge(act_ready, e + 1)
                if not (isinstance(e, int) and e < 1):
                    pe.wait_ge(actT_ready, e)
                for kk in range(2):
                    ins = nc.tensor.transpose(ps[7][:, P * kk:P * kk + P], eact[k % 2][:, P * kk:P * kk + P], ident)
                ins.then_inc(act_turned, 1)

            def expert(i, k, first=False, last=False):
                up_x(i, k)
                if not (last and k >= UNROLL - 2):
                    make_list(i + 2, (k + 2) % UNROLL)
                if not (last and k == UNROLL - 1):
                    turn_x(i + 1, (k + 1) % UNROLL)
                if not (first and k == 0):
                    down_x(i - 1, (k - 1) % UNROLL)
                turn_act(i, k)

            pe.wait_ge(sh_done, 1)
            make_list(0, 0)
            make_list(1, 1)
            turn_x(0, 0)
            for k in range(UNROLL):
                expert(k, k, first=True)
            with pe.Fori(1, NE // UNROLL - 1) as q:
                for k in range(UNROLL):
                    expert(UNROLL * q + k, k)
            for k in range(UNROLL):
                expert(NE - UNROLL + k, k, last=True)
            down_x(NE - 1, UNROLL - 1)

            pe.wait_ge(ya, NE)
            pe.wait_ge(yb, NE)

            def further_products(n, e):
                pe.wait_ge(ov_v, V_STEPS * n + 2)
                for t in range(NT):
                    r = ROWS[t]
                    ins = mm(ps[6][:, 0:4], onehot[0][0:r, t, :], V4[0:r, t, bass.ds(e, 1), :][:, 0, :], start=(t == 0), stop=(t == NT - 1))
                ins.then_inc(ov_p, 1)
                pe.wait_ge(ov_g, 16 * n + 16)
                for kk in range(KT):
                    ins = nc.tensor.transpose(ps[4 + kk // 4][:, P * (kk % 4):P * (kk % 4) + P], xg[0][:, P * kk:P * kk + P], ident)
                ins.then_inc(ov_p, 1)
                pe.wait_ge(ov_w, 32 * n + 32)
                pe.wait_ge(ov_v, V_STEPS * n + 4)
                for kk in range(KT):
                    ins = mm(ps[0][:, :], xgT[0][:, kk, :], w13[0][:, kk, :], start=(kk == 0), stop=(kk == KT - 1))
                ins.then_inc(ov_p, 1)
                pe.wait_ge(ov_v, V_STEPS * n + 5)
                for kk in range(2):
                    ins = nc.tensor.transpose(ps[7][:, P * kk:P * kk + P], eact[0][:, P * kk:P * kk + P], ident)
                ins.then_inc(ov_p, 1)
                pe.wait_ge(ov_v, V_STEPS * n + 6)
                for c in range(2):
                    for kk in range(2):
                        ins = mm(ps[2 + c][:, :], eactT[0][:, kk, :], w2[0][:, kk, 512 * c:512 * c + 512], start=(kk == 0), stop=(kk == 1))
                ins.then_inc(ov_p, 1)

            rounds = further(pe, further_products)
            pe.wait_ge(ov_v, rounds * V_STEPS + 1)

            pe.wait_ge(fin_in, 64)
            for t in range(NT):
                r = ROWS[t]
                if t >= 1:
                    pe.wait_ge(pe_read, t)
                for k in range(2):
                    ins = nc.tensor.transpose(ps[6][:, P * k:P * k + r], pnat[0:r, t, P * k:P * k + P], ident[0:r, 0:r])
                ins.then_inc(pe_turned, 1)
            pe.wait_ge(pe_read, NT)
            for t in range(NT):
                r = ROWS[t]
                for c in range(2):
                    n = 2 * t + c
                    if n >= 2:
                        pe.wait_ge(pin_saved, n - 1)
                    for k in range(2):
                        ins = mm(ps[2 + c][0:r, :], peT[:, k, span(t)], wpin[:, k, 512 * c:512 * c + 512], start=(k == 0), stop=(k == 1))
                    ins.then_inc(pin_up, 1)
            pe.wait_ge(pin_saved, 2 * NT)
            for q, t in enumerate(LAST_ORDER):
                r = ROWS[t]
                pe.wait_ge(h2_ready, q + 1)
                for i in range(2):
                    if q >= 1:
                        pe.wait_ge(h2_read, 2 * q)
                    for j in range(4):
                        k = 4 * i + j
                        ins = nc.tensor.transpose(ps[4 + i][:, P * j:P * j + r], m[0:r, t, P * k:P * k + P], ident[0:r, 0:r])
                    ins.then_inc(h2_turned, 1)
                pe.wait_ge(h2_read, 2 * q + 2)
                for c in range(2):
                    n = 2 * q + c
                    if n >= 4:
                        pe.wait_ge(sg_ready, n - 3)
                    for k in range(KT):
                        ins = mm(ps[n % 4][0:r, :], h2T[q % 2][:, k, 0:r], wpg[:, k, 512 * c:512 * c + 512], start=(k == 0), stop=(k == KT - 1))
                    ins.then_inc(gate_up, 1)

        @block.vector
        def _(dve):
            v = nc.vector
            steps = [0]

            def link(ins):
                steps[0] += 1
                ins.then_inc(step, 1)
                dve.wait_ge(step, steps[0])

            def mine(key):
                read(dve, key)

            for t in range(NT):
                b = take(dve, ("xT", t, 1))
                frees(v.tensor_copy(xT[:, 4:8, span(t)], b[:, :].rearrange("p (k n) -> p k n", k=4)[:, :, 0:ROWS[t]]), ("xT", t, 1))
            dve.wait_ge(consts_in, 16)
            dve.wait_ge(rotary_in, 16)
            dve.wait_ge(rows_cleared, 1)

            def rotate(r, t, src, nh, a_, b_, out):
                s = src.rearrange("p (h d) -> p h d", h=nh)
                ca = a_.rearrange("p (h d) -> p h d", h=nh)
                cb = b_.rearrange("p (h d) -> p h d", h=nh)
                cos = rotary[0:r, t, 0, :].unsqueeze(1).broadcast_to([r, nh, HD])
                sin = rotary[0:r, t, 1, :].unsqueeze(1).broadcast_to([r, nh, HD])
                v.tensor_tensor(ca, s, cos, ALU.mult)
                v.tensor_tensor(cb[:, :, 0:32], s[:, :, 32:64], sin[:, :, 0:32], ALU.mult)
                return v.tensor_tensor(cb[:, :, 32:64], s[:, :, 0:32], sin[:, :, 32:64], ALU.mult), (ca, cb, out)

            def total(parts):
                ca, cb, out = parts
                return v.tensor_tensor(out, ca, cb, ALU.add)

            for t in range(NT):
                r, s = ROWS[t], t % 2
                if t >= 1:
                    dve.wait_ge(roped, t)
                if t >= 2:
                    filled(dve, ("rt", t - 2, 2))
                    dve.wait_ge(rows_stored[s], 16 * 3 * (t // 2))
                key = ("q", t)
                b = take(dve, key)
                ins, parts = rotate(r, t, b[0:r, 0:512], H, ropeA[0:r, :], ropeB[0:r, :], rowsR[0:r, s, 0:8, HD:])
                frees(ins, key)
                mine(key)
                link(total(parts))
                key = ("kv", t)
                b = take(dve, key)
                _, p1 = rotate(r, t, b[0:r, 0:64], 1, ropeA[0:r, 0:64], ropeB[0:r, 0:64], rowsR[0:r, s, 8:9, HD:])
                _, p2 = rotate(r, t, b[0:r, 128:448], 5, ropeA[0:r, 64:384], ropeB[0:r, 64:384], None)
                v.tensor_copy(v_prompt[:, t, :] if t < 4 else v_samp, b[0:r, 64:128])
                frees(v.tensor_copy(wi[0:r, t, :], b[0:r, 448:452]), key)
                mine(key)
                total(p1)
                v.tensor_tensor(rowsR[0:r, s, 0:4, 0:HD], p2[0][:, 0:4, :], p2[1][:, 0:4, :], ALU.add)
                v.tensor_tensor(rowsR[0:r, s, 8:9, 0:IDX], p2[0][:, 4:5, :], p2[1][:, 4:5, :], ALU.add).then_inc(roped, 1)

            key = ("wsel",)
            b = take(dve, key)
            for g in range(2):
                ins = v.tensor_tensor(wcol8[:, g, :], b[:, 4 * g:4 * g + 4], const("hmask"), ALU.mult)
            frees(ins, key)
            mine(key)
            link(v.tensor_reduce(wcol, wcol8, AX, ALU.add))
            for g in range(2):
                ins = v.tensor_scalar(w_comb[:, g, :], const("selT"), wcol[:, g:g + 1], None, ALU.mult)
            ins.then_inc(comb_ready, 1)
            for n, (t, h) in enumerate([(t, h) for t in range(1, 4) for h in range(IH)]):
                read(dve, ("dot", t, h))
                rel = relP[n % 4][:, 0:KEYS[t]]
                if h == 0:
                    v.tensor_scalar(scoreP[t], rel, wi[:, t, 0:1], None, ALU.mult).then_inc(rel_used, 1)
                else:
                    dve.wait_ge(rel_used, n)
                    v.scalar_tensor_tensor(out=scoreP[t], in0=rel, scalar=wi[:, t, h:h + 1], in1=scoreP[t],
                                           op0=ALU.mult, op1=ALU.add).then_inc(rel_used, 1)
                if h == IH - 1:
                    dve.wait_ge(rel_used, n + 1)
                    dve.sem_inc(summed, 1)

            def keysT(b):
                for i in (0, 2):
                    bk = take(dve, ("kT", b, i))
                    frees(v.tensor_copy(kkT[b % 2][:, 512 * i:512 * i + 512], bk[:, :]), ("kT", b, i))

            def strike_prompt(rounds):
                base = steps[0]
                per = 6
                with dve.Fori(0, rounds) as i:
                    for t in range(1, 4):
                        dve.wait_ge(step, base + per * i + t - 1)
                        dve.sem_inc(passed_dve, 1)
                        v.max(top8[:, t, :], scoreP[t]).then_inc(step, 1)
                    for t in range(1, 4):
                        dve.wait_ge(step, base + per * i + 2 + t)
                        dve.sem_inc(passed_dve, 1)
                        v.match_replace(scoreP[t], top8[:, t, :], scoreP[t], STRUCK).then_inc(step, 1)
                steps[0] += per * rounds

            keysT(0)
            for b in range(DB):
                if b + 1 < DB:
                    keysT(b + 1)
                o2 = 64 * (b % 2)
                for c in range(5):
                    w = 512 if c < 4 else DT
                    bk = take(dve, ("sl", b, c))
                    frees(v.tensor_scalar(logit[o2:o2 + 64, b // 2, 512 * c:512 * c + w], bk[o2:o2 + 64, 0:w], HD ** -0.5, None, ALU.mult), ("sl", b, c))
                if b % 4 == 3:
                    g = b // 4
                    for c in range(5):
                        w = 512 if c < 4 else DT
                        bk = take(dve, ("sc", g, c))
                        frees(v.tensor_copy(scoreS[32 * g:32 * g + 32, 512 * c:512 * c + w], bk[32 * g:32 * g + 32, 0:w]), ("sc", g, c))
                if b == 0:
                    dve.wait_ge(barred, 4)
                strike_prompt(TOP_P // 8 // DB)

            dve.wait_ge(step, steps[0])

            for t in range(1, 4):
                link(v.tensor_scalar(scoreP[t], scoreP[t], STRUCK_TEST, MASKED, ALU.is_ge, ALU.mult))
            new = scoreS[:, PAST:SK]
            mine(("sc", 1, 4))
            link(v.tensor_tensor(new, new, const("newmask", NS), ALU.mult))
            link(v.tensor_scalar(top8[0:NS, 0, :], const("newmask", NS), -BARRED, BARRED, ALU.mult, ALU.add))
            link(v.tensor_tensor(new, new, top8[0:NS, 0, :], ALU.add))
            base_s = steps[0]
            with dve.Fori(0, TOP_S // 8) as i:
                dve.wait_ge(step, base_s + 2 * i)
                dve.sem_inc(passed_dve, 1)
                v.max(top8[0:NS, 0, :], scoreS).then_inc(step, 1)
                dve.wait_ge(step, base_s + 2 * i + 1)
                dve.sem_inc(passed_dve, 1)
                v.match_replace(scoreS, top8[0:NS, 0, :], scoreS, STRUCK).then_inc(step, 1)
            steps[0] += 2 * (TOP_S // 8)
            dve.wait_ge(step, steps[0])
            filled(dve, ("ga", 1, NT - 1))
            v.tensor_copy(rep_b, const("rep", NS).rearrange("p (k q) -> p k q", k=4))
            read(dve, ("uo", 1))
            dve.wait_ge(ust_out, 48)
            for c in range(5):
                w = 512 if c < 4 else DT
                ins = v.tensor_scalar(maskS[c][:, 0:w], scoreS[:, 512 * c:512 * c + w], STRUCK_TEST, MASKED, ALU.is_ge, ALU.mult)
            ins.then_inc(mask_s, 1)

            heads = [(t, h) for t in range(4) for h in range(H)]

            def row_max(n):
                t, h = heads[n]
                key = ("l", t, h)
                b = take(dve, key)
                if n >= 3:
                    filled(dve, ("pt",) + heads[n - 3])
                if n >= 1:
                    dve.wait_ge(maxed, n)
                col = 8 * (t % 2) + h
                frees(v.tensor_tensor_reduce(probs[n % 3][:, 0:KEYS[t]], b[:, 0:KEYS[t]], scoreP[t], HD ** -0.5, BARRED,
                                             ALU.add, ALU.max, mx[:, 0:1]), key)
                mine(key)
                v.tensor_scalar(nmax[:, col:col + 1], mx[:, 0:1], -1.0, None, ALU.mult).then_inc(maxed, 1)

            def probs_copy(n):
                t, h = heads[n]
                b = take(dve, ("pt", t, h))
                frees(v.tensor_copy(probsT[n % 2][:, 0:KEYS[t]], b[:, 0:KEYS[t]]), ("pt", t, h))

            for n in range(3):
                row_max(n)
            probs_copy(0)
            for n, (t, h) in enumerate(heads):
                if n + 3 < len(heads):
                    row_max(n + 3)
                if n + 1 < len(heads) and n % 2:
                    probs_copy(n + 1)
                if h == H - 1:
                    c8 = 8 * (t % 2)
                    dve.wait_ge(expd, n + 1)
                    link(v.reciprocal(erec[:, c8:c8 + 8], esum[:, c8:c8 + 8]))
                    dve.wait_ge(pv_done, t + 1)
                    if t >= 1:
                        filled(dve, ("at", t - 1))
                    v.tensor_tensor(att[:, :].rearrange("p (h d) -> p h d", h=H), ps[6 + t % 2][:, :].rearrange("p (h d) -> p h d", h=H),
                                    erec[:, c8:c8 + 8].unsqueeze(2).broadcast_to([P, H, HD]), ALU.mult).then_inc(att_ready, 1)
            def bias_max(p):
                dve.wait_ge(maxed, 32 + p)
                for c in range(5):
                    w = 512 if c < 4 else DT
                    key = ("bs", p, c)
                    b = take(dve, key)
                    lg = logit[:, p, 512 * c:512 * c + w]
                    frees(v.tensor_tensor_reduce(lg, b[:, 0:w], lg, 1.0, BARRED, ALU.add, ALU.max, mx[:, c:c + 1]), key)
                mine(("bs", p, 4))
                link(v.tensor_reduce(mx[:, 0:1], mx[:, 0:5], AX, ALU.max))
                v.tensor_scalar(nmax[:, p:p + 1], mx[:, 0:1], -1.0, None, ALU.mult).then_inc(maxed, 1)

            dve.wait_ge(expd, 32)
            bias_max(0)
            for p in range(4):
                if p < 3:
                    bias_max(p + 1)
                for i in (0, 2):
                    b = take(dve, ("ps", p, i))
                    frees(v.tensor_copy(probsTS[p % 2][:, 4 * i:4 * i + 4, :], b[:, :].rearrange("p (k n) -> p k n", k=4)), ("ps", p, i))
                b = take(dve, ("ps", p, 4))
                frees(v.tensor_copy(probsTS[p % 2][0:DT, NPG, :], b[0:DT, 0:P]), ("ps", p, 4))
                dve.wait_ge(expd, 32 + p + 1)
                link(v.reciprocal(erec[:, p:p + 1], esum[:, p:p + 1]))
                dve.wait_ge(pv_done, 4 + p + 1)
                v.tensor_scalar(attS, ps[6 + p % 2][:, 0:HD], erec[:, p:p + 1], None, ALU.mult).then_inc(att_ready, 1)
                key = ("ost", p)
                b = take(dve, key)
                for odd in range(2):
                    src = b[0:HD, 0:P].rearrange("d (b k o t) -> d o k b t", b=2, k=4, o=2)[:, odd]
                    c0 = SEQ + 2 * DT * p
                    dst = attnT[64 * odd:64 * odd + 64, :, c0:c0 + 2 * DT].rearrange("d k (b t) -> d k b t", b=2)
                    ins = v.tensor_copy(dst, src)
                frees(ins, key)

            dve.wait_ge(mixed, 2 * NT)
            for n, (t, c) in enumerate([(t, c) for t in range(NT) for c in range(2)]):
                r = ROWS[t]
                key = ("m1", t, c)
                b = take(dve, key)
                cs = slice(512 * c, 512 * c + 512)
                frees(v.tensor_tensor(mtmp[n % 2][0:r, :], b[0:r, :], sga[0:r, t, cs], ALU.mult), key)
                mine(key)
                ins = v.tensor_tensor(m[0:r, t, cs], m[0:r, t, cs], mtmp[n % 2][0:r, :], ALU.add)
                if c == 1:
                    ins.then_inc(m_ready, 1)
            for t in range(NT):
                r = ROWS[t]
                b = take(dve, ("mT", t, 1))
                frees(v.tensor_copy(mT[:, 4:8, span(t)], b[:, :].rearrange("p (k n) -> p k n", k=4)[:, :, 0:r]), ("mT", t, 1))
            dve.wait_ge(xr_in, 16 * NT)
            dve.wait_ge(ln_in, 64)

            def norm_stats(t, st, mean_var, var_sem):
                r = ROWS[t]
                for c in range(2):
                    ins = v.bn_stats(st[0:r, c, :], m[0:r, t, 512 * c:512 * c + 512])
                link(ins)
                link(v.bn_aggr(mean_var[0:r, t, :], st[0:r, :, :]))
                v.tensor_scalar(mean_var[0:r, t, 1:2], mean_var[0:r, t, 1:2], EPS, None, ALU.add).then_inc(var_sem, 1)

            def norm_apply(t, mean_var, rs, rstd_sem, gamma, beta, done, i):
                r = ROWS[t]
                row = m[0:r, t, :]
                dve.wait_ge(rstd_sem, i + 1)
                link(v.scalar_tensor_tensor(out=row, in0=row, scalar=mean_var[0:r, t, 0:1], in1=gamma[0:r, :], op0=ALU.subtract, op1=ALU.mult))
                v.scalar_tensor_tensor(out=row, in0=row, scalar=rs[0:r, t:t + 1], in1=beta[0:r, :], op0=ALU.mult, op1=ALU.add).then_inc(done, 1)

            for t in range(NT):
                r = ROWS[t]
                for c in range(2):
                    key = ("wo", c, t)
                    b = take(dve, key)
                    cs = slice(512 * c, 512 * c + 512)
                    frees(v.scalar_tensor_tensor(out=m[0:r, t, cs], in0=xr[0:r, t, cs], scalar=ALPHA, in1=b[0:r, :],
                                                 op0=ALU.mult, op1=ALU.add), key)
                mine(("wo", 1, t))
                norm_stats(t, stat6, mv, var_ready)
                if t >= 1:
                    norm_apply(t - 1, mv, rstd, rstd_ready, lng, lnb, h_ready, t - 1)
            norm_apply(NT - 1, mv, rstd, rstd_ready, lng, lnb, h_ready, NT - 1)

            link(v.tensor_scalar(tok8[:, 0:5], const("tokid"), float(TOPE), -BIG, ALU.mult, ALU.add))
            for t in range(NT):
                r = ROWS[t]
                read(dve, ("r", t))
                sr = sS[0:r, t, :]
                link(v.tensor_tensor(sbt[0:r, :], sr, rbias[0:r, :], ALU.add))
                for g in range(8):
                    ins = v.max(g88[0:r, g, :], sbt[0:r, 8 * g:8 * g + 8])
                link(ins)
                link(v.tensor_tensor(gsum[0:r, :], g88[0:r, :, 0], g88[0:r, :, 1], ALU.add))
                link(v.max(gtop[0:r, :], gsum[0:r, :]))
                link(v.memset(gtop[0:r, 4:8], BARRED))
                link(v.match_replace(grest[0:r, :], gtop[0:r, :], gsum[0:r, :], -2e30))
                link(v.tensor_scalar(gmask[0:r, :], grest[0:r, :], -1.5e30, None, ALU.is_le))
                link(v.tensor_scalar(gadd[0:r, :], gmask[0:r, :], 1e30, -1e30, ALU.mult, ALU.add))
                mk = msk[0:r, :].rearrange("p (g k) -> p g k", g=8)
                link(v.tensor_tensor(mk, sbt[0:r, :].rearrange("p (g k) -> p g k", g=8), gmask[0:r, :].unsqueeze(2).broadcast_to([r, 8, 8]), ALU.mult))
                link(v.tensor_tensor(mk, mk, gadd[0:r, :].unsqueeze(2).broadcast_to([r, 8, 8]), ALU.add))
                link(v.max(e8[0:r, :], msk[0:r, :]))
                link(v.match_replace(repl[0:r, :], e8[0:r, :], msk[0:r, :], -2e30))
                link(v.tensor_scalar(selM[0:r, t, :], repl[0:r, :], -1.5e30, None, ALU.is_le))
                link(v.tensor_tensor(ggate[0:r, :], sr, selM[0:r, t, :], ALU.mult))
                link(v.tensor_reduce(gden[0:r, 0:1], ggate[0:r, :], AX, ALU.add))
                link(v.reciprocal(gden[0:r, 1:2], gden[0:r, 0:1]))
                v.tensor_scalar(V4[0:r, t, :, 2], ggate[0:r, :], gden[0:r, 1:2], SCALE_ROUTED, ALU.mult, ALU.mult)
                link(v.tensor_tensor_scan(incl[0:r, :], const("ones", r)[:, 0:NE], selM[0:r, t, :], 0.0, ALU.mult, ALU.add))
                link(v.tensor_tensor(incl[0:r, :], incl[0:r, :], selM[0:r, t, :], ALU.subtract))
                v.tensor_scalar(V4[0:r, t, :, 1], incl[0:r, :], tok8[0:r, t:t + 1], None, ALU.add)
                v.tensor_scalar(V4[0:r, t, :, 0], const("iota", r)[:, 0:NE], 0.0, const("tokid", r)[:, t:t + 1], ALU.mult, ALU.add)
                link(v.memset(V4[0:r, t, :, 3], 0.0))
                v.tensor_scalar(V4[0:r, t, :, 0], V4[0:r, t, :, 0], -BIG, None, ALU.add).then_inc(routed, 1)
            for t in range(NT):
                r = ROWS[t]
                key = ("s13", t)
                b = take(dve, key)
                dve.wait_ge(shsig_ready, t + 1)
                link(v.tensor_tensor(shact[t][0:r, :], b[0:r, 0:ED], shsig[t][0:r, :], ALU.mult))
                frees(v.tensor_tensor(shact[t][0:r, :], b[0:r, ED:512], shact[t][0:r, :], ALU.mult), key)
                mine(key)
                dve.sem_inc(sha_ready, 1)
            for t in range(NT):
                r = ROWS[t]
                key = ("rank", t)
                b = take(dve, key)
                frees(v.scalar_tensor_tensor(out=posm[0:r, t, :], in0=b[0:r, 0:NE], scalar=1.0, in1=selM[0:r, t, :],
                                             op0=ALU.add, op1=ALU.mult), key)
                mine(key)
                link(v.tensor_scalar(posm[0:r, t, :], posm[0:r, t, :], -1.0, None, ALU.add))
            b = take(dve, ("count",))
            frees(v.tensor_reduce(longest[:, 0:1], b[0:1, 0:NE], AX, ALU.max), ("count",))
            mine(("count",))
            link(v.tensor_scalar(blocks_f[:, 0:4], const("blocks", 1), longest[:, 0:1], None, ALU.is_lt))
            link(v.tensor_reduce(blocks_f[:, 4:5], blocks_f[:, 0:4], AX, ALU.add))
            v.tensor_copy(blocks_i, blocks_f[:, 4:5]).then_inc(ov_v, 1)
            for t in range(NT):
                r = ROWS[t]
                for c in range(2):
                    cs = slice(512 * c, 512 * c + 512)
                    key = ("s2", t, c)
                    b = take(dve, key)
                    if (t, c) == (0, 0):
                        dve.wait_ge(h_stored, 16 * NT)
                    frees(v.scalar_tensor_tensor(out=m[0:r, t, cs], in0=m[0:r, t, cs], scalar=ALPHA, in1=b[0:r, :],
                                                 op0=ALU.mult, op1=ALU.add), key)
            mine(("s2", NT - 1, 1))
            dve.sem_inc(sh_done, 1)

            def one_hot(e, k):
                if not (isinstance(e, int) and e < 2):
                    dve.wait_ge(list_ready, e - 1)
                for t in range(NT):
                    r = ROWS[t]
                    ins = v.tensor_scalar(onehot[k % 2][0:r, t, :], const("iota", r), posm[0:r, t, bass.ds(e, 1)], None, ALU.is_equal)
                ins.then_inc(oh_ready, 1)

            def make_meta(e, k):
                dve.wait_ge(list_ready, e + 1)
                if not (isinstance(e, int) and e < UNROLL):
                    dve.wait_ge(scattered[k % 2], 8 * e - 8 * (k % 2) + 16 - 8 * UNROLL)
                v.tensor_scalar(metai[:, k, 0:2], ps[6][:, 0:2], BIG, None, ALU.add)
                v.tensor_copy(meta[:, k, 2:3], ps[6][:, 2:3]).then_inc(meta_ready, 1)

            def xgT_half(e, k):
                dve.wait_ge(turned, 2 * e + 2)
                v.tensor_copy(xgT[k % 2][:, 4:8, :], ps[5][:, :].rearrange("p (k n) -> p k n", k=4)).then_inc(xtb, 1)

            def y_half(e, k):
                dve.wait_ge(down, 2 * e + 2)
                if not (isinstance(e, int) and e < 2):
                    dve.wait_ge(scattered[k % 2], 8 * e - 8 * (k % 2))
                v.tensor_scalar(ye[k % 2][:, 512:1024], ps[3][:, :], meta[:, k, 2:3], None, ALU.mult).then_inc(yb, 1)

            def expert(i, k, first=False, last=False):
                if not (last and k >= UNROLL - 2):
                    make_meta(i + 2, (k + 2) % UNROLL)
                dve.wait_ge(sig_ready, i + 1)
                if not (first and k < 2):
                    dve.wait_ge(act_turned, i - 1)
                v.tensor_tensor(esig[k % 2], ps[k % 2][:, 0:ED], esig[k % 2], ALU.mult).then_inc(silu_done, 1)
                dve.wait_ge(silu_done, i + 1)
                v.tensor_tensor(eact[k % 2], ps[k % 2][:, ED:512], esig[k % 2], ALU.mult).then_inc(act_ready, 1)
                if not (last and k == UNROLL - 1):
                    xgT_half(i + 1, (k + 1) % UNROLL)
                if not (last and k >= UNROLL - 3):
                    one_hot(i + 3, (k + 3) % UNROLL)
                if not (first and k == 0):
                    y_half(i - 1, (k - 1) % UNROLL)

            one_hot(0, 0)
            one_hot(1, 1)
            one_hot(2, 2)
            make_meta(0, 0)
            make_meta(1, 1)
            xgT_half(0, 0)
            for k in range(UNROLL):
                expert(k, k, first=True)
            with dve.Fori(1, NE // UNROLL - 1) as q:
                for k in range(UNROLL):
                    expert(UNROLL * q + k, k)
            for k in range(UNROLL):
                expert(NE - UNROLL + k, k, last=True)
            y_half(NE - 1, UNROLL - 1)

            def next_block(blk):
                dve.wait_ge(ov_done, blk * NE + 1)
                for t in range(NT):
                    r = ROWS[t]
                    ins = v.tensor_scalar(posm[0:r, t, :], posm[0:r, t, :], -float(CAP), None, ALU.add)
                ins.then_inc(shifted, 1)
                dve.wait_ge(shifted, blk + 1)
                dve.sem_inc(passed_dve, 1)

            def further_steps(n, e):
                dve.wait_ge(ov_done, n + 1)
                for t in range(NT):
                    r = ROWS[t]
                    ins = v.tensor_scalar(onehot[0][0:r, t, :], const("iota", r), posm[0:r, t, bass.ds(e, 1)], None, ALU.is_equal)
                ins.then_inc(ov_v, 1)
                dve.wait_ge(ov_p, P_STEPS * n + 1)
                v.tensor_scalar(metai[:, 0, 0:2], ps[6][:, 0:2], BIG, None, ALU.add)
                v.tensor_copy(meta[:, 0, 2:3], ps[6][:, 2:3]).then_inc(ov_v, 1)
                dve.wait_ge(ov_p, P_STEPS * n + 2)
                v.tensor_copy(xgT[0][:, 0:4, :], ps[4][:, :].rearrange("p (k n) -> p k n", k=4))
                v.tensor_copy(xgT[0][:, 4:8, :], ps[5][:, :].rearrange("p (k n) -> p k n", k=4)).then_inc(ov_v, 1)
                dve.wait_ge(ov_a, n + 1)
                v.tensor_tensor(esig[0], ps[0][:, 0:ED], esig[0], ALU.mult).then_inc(silu_done, 1)
                dve.wait_ge(silu_done, n + NE + 1)
                v.tensor_tensor(eact[0], ps[0][:, ED:512], esig[0], ALU.mult).then_inc(ov_v, 1)
                dve.wait_ge(ov_p, P_STEPS * n + 4)
                v.tensor_copy(eactT[0], ps[7][:, 0:256].rearrange("p (k n) -> p k n", k=2)).then_inc(ov_v, 1)
                dve.wait_ge(ov_p, P_STEPS * n + 5)
                for c in range(2):
                    ins = v.tensor_scalar(ye[0][:, 512 * c:512 * c + 512], ps[2 + c][:, :], meta[:, 0, 2:3], None, ALU.mult)
                ins.then_inc(ov_v, 1)

            further(dve, further_steps, next_block)

            dve.wait_ge(norm2_in, 32)
            def choices(i):
                t = LAST_ORDER[i]
                r = ROWS[t]
                dve.wait_ge(y_in[i % 2], 16 * (i // 2 + 1))
                for j in range(5):
                    link(v.tensor_tensor(m[0:r, t, :], m[0:r, t, :], yt[i % 2][0:r, j, :], ALU.add))
                dve.wait_ge(pool_summed, i + 1)
                v.tensor_tensor(m[0:r, t, :], m[0:r, t, :], yt[i % 2][0:r, 5, :], ALU.add).then_inc(y_summed, 1)
                dve.wait_ge(y_summed, i + 1)
                norm_stats(t, stat6b, mvb, var2)

            def gated(i):
                t = LAST_ORDER[i]
                r = ROWS[t]
                for c in range(2):
                    n = 2 * i + c
                    cs = slice(512 * c, 512 * c + 512)
                    dve.wait_ge(sg_ready, n + 1)
                    v.tensor_tensor(sg[n % 4][0:r, :], pin[t][0:r, cs], sg[n % 4][0:r, :], ALU.mult).then_inc(mul_done, 1)

            choices(0)
            for i in range(NT):
                norm_apply(LAST_ORDER[i], mvb, rstdb, rstd2, g2, b2, h2_ready, i)
                if i + 1 < NT:
                    choices(i + 1)
                if i >= 1:
                    gated(i - 1)
            gated(NT - 1)

        for who in ("act", "dve"):
            want = [key for key, w_ in jobs if w_ == who]
            got = order[who]
            assert got == want, (who, [x for x in zip(got, want) if x[0] != x[1]][:2], len(got), len(want))
        assert order["pe"] == [key for key, _ in jobs]


_INS = ['x_prompt', 'x_sample', 'cache_k', 'cache_v', 'cache_kidx', 'state_pool', 'page_table', 'p_prompt', 'p_sample',
        'w_in', 'w_att_out', 'w_pool_grp', 'pool_scale', 'w_pool_out', 'w_out', 'ln1_g', 'ln1_b', 'w_router',
        'router_bias', 'w_exp13', 'w_exp2', 'w_sh13', 'w_sh2', 'ln2_g', 'ln2_b', 'w_ple_in', 'w_ple_gate']
_OUTS = [('y_prompt', (1, 512, 1024)), ('y_sample', (8, 8, 1024)), ('k_prompt', (1, 1, 512, 64)),
         ('v_prompt', (1, 1, 512, 64)), ('kidx_prompt', (1, 1, 512, 64)), ('pool_prompt', (1, 1, 15, 512)),
         ('k_sample', (1, 8, 8, 64)), ('v_sample', (1, 8, 8, 64)), ('kidx_sample', (1, 8, 8, 64)),
         ('pool_sample', (1, 8, 15, 512))]


def kernel(**inputs):
    import numpy as _np
    import concourse.bacc as _bacc
    from concourse import mybir as _mybir
    from concourse.bass_utils import run_bass_kernel_spmd as _run

    nc = _bacc.Bacc("TRN2", target_bir_lowering=False, num_devices=1)
    arrays, a, o = {}, {}, {}
    data = {name: _np.ascontiguousarray(inputs[name]) for name in _INS}
    data["consts"], data["rotary"] = constants()
    for name, x in data.items():
        arrays[f"in_{name}"] = x
        a[name] = nc.dram_tensor(f"in_{name}", x.shape, _mybir.dt.from_np(x.dtype), kind="ExternalInput").ap()
    a["n_phys"] = data["cache_k"].shape[1]
    for name, shape in _OUTS:
        o[name] = nc.dram_tensor(f"out_{name}", shape, F32, kind="ExternalOutput").ap()
    build(nc, a, o)
    r = _run(nc, [arrays], core_ids=[0])
    return tuple(r.results[0][f"out_{name}"] for name, _ in _OUTS)
```
